# Optimizing a Trainium2 kernel written in Bass

```python
import math
import jax, jax.numpy as jnp
from jax import lax
import numpy as np

D_MODEL = 1024
BATCH = 1
SEQ = 256
DEPTH = 2

GRID_W = 64
CTX_LEN = 256
HEAD_DIM = 64
CHUNK = 64
Q_BLOCK = 128
EPS = 1e-6
GLA_HEADS = 4
GLA_DK = 64
GLA_DV = 64
GLA_GATE_RANK = 16
GLA_TAU = 16.0
GDN_HEADS = 4
GDN_DK = 64
GDN_DV = 64
SHORT_CONV = 5
ATT_Q_HEADS = 8
ATT_KV_HEADS = 2
ATT_GROUP = ATT_Q_HEADS // ATT_KV_HEADS
ROPE_THETA = 10000.0
D_MIX = GLA_HEADS * GLA_DV + GDN_HEADS * GDN_DV + ATT_Q_HEADS * HEAD_DIM
D_FF = 2816
N_EXPERTS = 8
TOP_K = 2
N_DENSE = (DEPTH + 1) // 2
N_MOE = DEPTH // 2
IN_SIZES = (GLA_HEADS * GLA_DK, GLA_HEADS * GLA_DK, GLA_HEADS * GLA_DV, GLA_HEADS * GLA_DV, 2 * GLA_GATE_RANK,
            GDN_HEADS * GDN_DK, GDN_HEADS * GDN_DK, GDN_HEADS * GDN_DV, GDN_HEADS * GDN_DV, 2 * GDN_HEADS, 2 * GDN_HEADS,
            ATT_Q_HEADS * HEAD_DIM, ATT_KV_HEADS * HEAD_DIM, ATT_KV_HEADS * HEAD_DIM)
D_IN = sum(IN_SIZES)

kernel_name = "hybrid_gla_gdn_gqa_moe_diffusion_block"

F32 = jnp.float32

def rmsnorm(x, gain):
    xf = x.astype(F32)
    y = xf * lax.rsqrt(jnp.mean(xf * xf, axis=-1, keepdims=True) + EPS)
    return (y * gain.astype(F32)).astype(x.dtype)

def l2norm(x):
    return x * lax.rsqrt(jnp.sum(x * x, axis=-1, keepdims=True) + EPS)

def modulate(h, shift, scale):
    return h * (1 + scale) + shift

def split_cols(p):
    idx = [int(i) for i in np.cumsum(IN_SIZES)[:-1]]
    return jnp.split(p, idx, axis=-1)

def to_heads(t, n_heads):
    B, L, _ = t.shape
    return t.reshape(B, L, n_heads, -1).transpose(0, 2, 1, 3)

def _chunks(t):
    B, H, L = t.shape[:3]
    t = t.reshape((B, H, L // CHUNK, CHUNK) + t.shape[3:])
    return jnp.moveaxis(t, 2, 0)

def _unchunk(t):
    n, B, H, C = t.shape[:4]
    return jnp.moveaxis(t, 0, 2).reshape((B, H, n * C) + t.shape[4:])

def gla_chunk_scan(q, k, v, log_a, s0):
    tri = jnp.tril(jnp.ones((CHUNK, CHUNK), bool))

    def step(S, inp):
        qc, kc, vc, gc = inp
        b = jnp.cumsum(gc, axis=2)
        diff = b[:, :, :, None, :] - b[:, :, None, :, :]
        decay = jnp.exp(jnp.where(tri[:, :, None], diff, -jnp.inf))
        scores = jnp.einsum('bhtd,bhsd,bhtsd->bhts', qc, kc, decay)
        o = jnp.einsum('bhtd,bhde->bhte', qc * jnp.exp(b), S) + jnp.einsum('bhts,bhse->bhte', scores, vc)
        b_end = b[:, :, -1:, :]
        S = jnp.exp(b_end[:, :, 0, :, None]) * S + jnp.einsum('bhsd,bhse->bhde', kc * jnp.exp(b_end - b), vc)
        return S, o

    S, o = lax.scan(step, s0, tuple(_chunks(t) for t in (q, k, v, log_a)))
    return _unchunk(o), S

def gdn_chunk_scan(q, k, v, log_a, beta, s0):
    tri = jnp.tril(jnp.ones((CHUNK, CHUNK), bool))
    strict = jnp.tril(jnp.ones((CHUNK, CHUNK), bool), -1)
    eye = jnp.eye(CHUNK, dtype=F32)

    def step(S, inp):
        qc, kc, vc, gc, bc = inp
        gam = jnp.cumsum(gc, axis=-1)
        dec = jnp.exp(jnp.where(tri, gam[..., :, None] - gam[..., None, :], -jnp.inf))
        a_mat = jnp.where(strict, bc[..., :, None] * dec * jnp.einsum('bhtd,bhsd->bhts', kc, kc), 0.0)
        rhs = jnp.concatenate([bc[..., None] * vc, (bc * jnp.exp(gam))[..., None] * kc], axis=-1)
        sol = lax.linalg.triangular_solve(a_mat + eye, rhs, left_side=True, lower=True, unit_diagonal=True)
        dv = vc.shape[-1]
        u = sol[..., :dv] - jnp.einsum('bhsd,bhde->bhse', sol[..., dv:], S)
        qk = jnp.einsum('bhtd,bhsd->bhts', qc, kc) * dec
        o = jnp.exp(gam)[..., None] * jnp.einsum('bhtd,bhde->bhte', qc, S) + jnp.einsum('bhts,bhse->bhte', qk, u)
        g_end = gam[..., -1:]
        S = jnp.exp(g_end)[..., None] * S + jnp.einsum('bhsd,bhse->bhde', kc * jnp.exp(g_end - gam)[..., None], u)
        return S, o

    S, o = lax.scan(step, s0, tuple(_chunks(t) for t in (q, k, v, log_a, beta)))
    return _unchunk(o), S

def bidirectional_scan(scan_fn, shared_ctx, shared_lat, dir_ctx, dir_lat, s0):
    o_ctx, o_lat = None, None
    for d in range(2):
        f = (lambda t: jnp.flip(t, axis=2)) if d == 1 else (lambda t: t)
        oc, sc = scan_fn(*[f(t) for t in shared_ctx + dir_ctx[d]], s0)
        ol, _ = scan_fn(*[f(t) for t in shared_lat + dir_lat[d]], sc)
        o_ctx = f(oc) if o_ctx is None else o_ctx + f(oc)
        o_lat = f(ol) if o_lat is None else o_lat + f(ol)
    return o_ctx, o_lat

def centred_dwconv(x, w):
    K, C = w.shape
    pad = K // 2
    return lax.conv_general_dilated(x, w[:, None, :].astype(x.dtype), window_strides=(1,),
                                    padding=[(pad, K - 1 - pad)], dimension_numbers=('NWC', 'WIO', 'NWC'),
                                    feature_group_count=C)

def gla_mixer(p_ctx, p_lat, gate_up, gate_bias, out_gain, need_ctx):
    def prep(parts):
        q, k, v, _, g_low = [t.astype(F32) for t in parts]
        q = to_heads(q, GLA_HEADS) * GLA_DK ** -0.5
        k = to_heads(k, GLA_HEADS)
        v = to_heads(v, GLA_HEADS)
        g_dirs = jnp.split(g_low, 2, axis=-1)
        per_dir = [(to_heads(jax.nn.log_sigmoid(g_dirs[d] @ gate_up[d].astype(F32) + gate_bias[d].astype(F32))
                             / GLA_TAU, GLA_HEADS),) for d in range(2)]
        return (q, k, v), per_dir

    sh_c, dir_c = prep(p_ctx)
    sh_l, dir_l = prep(p_lat)
    s0 = jnp.zeros((p_lat[0].shape[0], GLA_HEADS, GLA_DK, GLA_DV), F32)
    o_c, o_l = bidirectional_scan(gla_chunk_scan, sh_c, sh_l, dir_c, dir_l, s0)

    def finish(o, r):
        B, _, L, _ = o.shape
        o = rmsnorm(jnp.swapaxes(o, 1, 2), out_gain).reshape(B, L, GLA_HEADS * GLA_DV)
        return o * jax.nn.silu(r.astype(F32))

    return (finish(o_c, p_ctx[3]) if need_ctx else None), finish(o_l, p_lat[3])

def gdn_mixer(p_ctx, p_lat, conv_w, a_log, dt_bias, out_gain, need_ctx):
    qk_w = GDN_HEADS * GDN_DK

    def prep(parts):
        q, k, v, _, a, bt = parts
        qkv = jax.nn.silu(centred_dwconv(jnp.concatenate([q, k, v], axis=-1), conv_w).astype(F32))
        q, k, v = jnp.split(qkv, [qk_w, 2 * qk_w], axis=-1)
        q = l2norm(to_heads(q, GDN_HEADS)) * GDN_DK ** -0.5
        k = l2norm(to_heads(k, GDN_HEADS))
        v = to_heads(v, GDN_HEADS)
        a = a.astype(F32)
        bt = bt.astype(F32)
        per_dir = []
        for d in range(2):
            ad = a[..., d * GDN_HEADS:(d + 1) * GDN_HEADS]
            bd = bt[..., d * GDN_HEADS:(d + 1) * GDN_HEADS]
            g = -jnp.exp(a_log[d].astype(F32)) * jax.nn.softplus(ad + dt_bias[d].astype(F32))
            per_dir.append((jnp.swapaxes(g, 1, 2), jnp.swapaxes(jax.nn.sigmoid(bd), 1, 2)))
        return (q, k, v), per_dir

    sh_c, dir_c = prep(p_ctx)
    sh_l, dir_l = prep(p_lat)
    s0 = jnp.zeros((p_lat[0].shape[0], GDN_HEADS, GDN_DK, GDN_DV), F32)
    o_c, o_l = bidirectional_scan(gdn_chunk_scan, sh_c, sh_l, dir_c, dir_l, s0)

    def finish(o, z):
        B, _, L, _ = o.shape
        z = z.astype(F32).reshape(B, L, GDN_HEADS, GDN_DV)
        return (rmsnorm(jnp.swapaxes(o, 1, 2), out_gain) * jax.nn.silu(z)).reshape(B, L, GDN_HEADS * GDN_DV)

    return (finish(o_c, p_ctx[3]) if need_ctx else None), finish(o_l, p_lat[3])

def _rotate(xs, ang):
    x1, x2 = jnp.split(xs, 2, axis=-1)
    cos = jnp.cos(ang).astype(xs.dtype)
    sin = jnp.sin(ang).astype(xs.dtype)
    return jnp.concatenate([x1 * cos - x2 * sin, x2 * cos + x1 * sin], axis=-1)

def axial_rope(x, ang_row, ang_col):
    shape = (1, x.shape[1]) + (1,) * (x.ndim - 3) + (ang_row.shape[-1],)
    xr, xc = jnp.split(x, 2, axis=-1)
    return jnp.concatenate([_rotate(xr, ang_row.reshape(shape)), _rotate(xc, ang_col.reshape(shape))], axis=-1)

def blocked_attention(q, k, v):
    B, Lq = q.shape[:2]
    nb = Lq // Q_BLOCK
    kf = k.astype(F32)
    scale = HEAD_DIM ** -0.5
    qb = jnp.moveaxis(q.reshape((B, nb, Q_BLOCK) + q.shape[2:]), 1, 0)

    def one(qblk):
        s = jnp.einsum('bqhgd,bkhd->bhgqk', qblk.astype(F32), kf) * scale
        p = jax.nn.softmax(s, axis=-1)
        return jnp.einsum('bhgqk,bkhd->bqhgd', p.astype(v.dtype), v)

    o = lax.map(one, qb)
    return jnp.moveaxis(o, 0, 1).reshape(q.shape)

def attention_mixer(p_ctx, p_lat, q_gain, k_gain, ang_row, ang_col, need_ctx):
    def prep(parts, rope):
        q, k, v = parts
        B, L, _ = q.shape
        q = rmsnorm(q.reshape(B, L, ATT_KV_HEADS, ATT_GROUP, HEAD_DIM), q_gain)
        k = rmsnorm(k.reshape(B, L, ATT_KV_HEADS, HEAD_DIM), k_gain)
        v = v.reshape(B, L, ATT_KV_HEADS, HEAD_DIM)
        if rope:
            q = axial_rope(q, ang_row, ang_col)
            k = axial_rope(k, ang_row, ang_col)
        return q, k, v

    qc, kc, vc = prep(p_ctx, False)
    ql, kl, vl = prep(p_lat, True)
    k_all = jnp.concatenate([kl, kc], axis=1)
    v_all = jnp.concatenate([vl, vc], axis=1)
    B, L = ql.shape[:2]
    o_lat = blocked_attention(ql, k_all, v_all).reshape(B, L, ATT_Q_HEADS * HEAD_DIM)
    o_ctx = blocked_attention(qc, kc, vc).reshape(B, qc.shape[1], ATT_Q_HEADS * HEAD_DIM) if need_ctx else None
    return o_ctx, o_lat

def swiglu(h, w_gu, w_down):
    g, u = jnp.split(h @ w_gu, 2, axis=-1)
    return (jax.nn.silu(g) * u) @ w_down

def moe_swiglu(h, w_router, b_router, w_gu, w_down):
    logits = h.astype(F32) @ w_router.astype(F32) + b_router.astype(F32)
    top_v, top_i = lax.top_k(logits, TOP_K)
    top_w = jax.nn.softmax(top_v, axis=-1)
    combine = jnp.sum(jax.nn.one_hot(top_i, N_EXPERTS, dtype=F32) * top_w[..., None], axis=-2)
    y = jnp.zeros(h.shape, F32)
    for e in range(N_EXPERTS):
        y = y + combine[..., e:e + 1] * swiglu(h, w_gu[e], w_down[e]).astype(F32)
    return y.astype(h.dtype)

def setup_inputs(seed: int = 0) -> dict:
    key = jax.random.key(seed)
    ks = iter(jax.random.split(key, 32))

    def nrm(shape, scale):
        return jax.random.normal(next(ks), shape, F32) * scale

    x = nrm((BATCH, SEQ, D_MODEL), 1.0)
    c = nrm((BATCH, D_MODEL), 1.0)
    ctx = nrm((BATCH, CTX_LEN, D_MODEL), 1.0)
    c_ctx = nrm((D_MODEL,), 1.0)
    w_mod = nrm((DEPTH, D_MODEL, 6 * D_MODEL), 0.5 * D_MODEL ** -0.5)
    b_mod = nrm((DEPTH, 6 * D_MODEL), 0.02)
    norm_mix = 1.0 + nrm((DEPTH, D_MODEL), 0.02)
    norm_ffn = 1.0 + nrm((DEPTH, D_MODEL), 0.02)
    w_in = nrm((DEPTH, D_MODEL, D_IN), D_MODEL ** -0.5)
    gla_gate_up = nrm((DEPTH, 2, GLA_GATE_RANK, GLA_HEADS * GLA_DK), GLA_GATE_RANK ** -0.5)
    gla_gate_bias = nrm((DEPTH, 2, GLA_HEADS * GLA_DK), 0.1)
    gla_out_gain = 1.0 + nrm((DEPTH, GLA_DV), 0.02)
    gdn_conv = nrm((DEPTH, SHORT_CONV, 2 * GDN_HEADS * GDN_DK + GDN_HEADS * GDN_DV), SHORT_CONV ** -0.5)
    gdn_a_log = jnp.log(jax.random.uniform(next(ks), (DEPTH, 2, GDN_HEADS), F32, 1.0, 16.0))
    dt = jnp.exp(jax.random.uniform(next(ks), (DEPTH, 2, GDN_HEADS), F32, math.log(1e-3), math.log(0.1)))
    gdn_dt_bias = dt + jnp.log(-jnp.expm1(-dt))
    gdn_out_gain = 1.0 + nrm((DEPTH, GDN_DV), 0.02)
    att_q_gain = 1.0 + nrm((DEPTH, HEAD_DIM), 0.02)
    att_k_gain = 1.0 + nrm((DEPTH, HEAD_DIM), 0.02)
    w_out = nrm((DEPTH, D_MIX, D_MODEL), D_MIX ** -0.5)
    ffn_gate_up = nrm((N_DENSE, D_MODEL, 2 * D_FF), D_MODEL ** -0.5)
    ffn_down = nrm((N_DENSE, D_FF, D_MODEL), D_FF ** -0.5)
    moe_router = nrm((N_MOE, D_MODEL, N_EXPERTS), D_MODEL ** -0.5)
    moe_router_bias = nrm((N_MOE, N_EXPERTS), 0.01)
    moe_gate_up = nrm((N_MOE, N_EXPERTS, D_MODEL, 2 * D_FF), D_MODEL ** -0.5)
    moe_down = nrm((N_MOE, N_EXPERTS, D_FF, D_MODEL), D_FF ** -0.5)
    return {"x": x, "c": c, "ctx": ctx, "c_ctx": c_ctx, "w_mod": w_mod, "b_mod": b_mod,
            "norm_mix": norm_mix, "norm_ffn": norm_ffn, "w_in": w_in, "gla_gate_up": gla_gate_up,
            "gla_gate_bias": gla_gate_bias, "gla_out_gain": gla_out_gain, "gdn_conv": gdn_conv,
            "gdn_a_log": gdn_a_log, "gdn_dt_bias": gdn_dt_bias, "gdn_out_gain": gdn_out_gain,
            "att_q_gain": att_q_gain, "att_k_gain": att_k_gain, "w_out": w_out,
            "ffn_gate_up": ffn_gate_up, "ffn_down": ffn_down, "moe_router": moe_router,
            "moe_router_bias": moe_router_bias, "moe_gate_up": moe_gate_up, "moe_down": moe_down}

def reference(x, c, ctx, c_ctx, w_mod, b_mod, norm_mix, norm_ffn, w_in, gla_gate_up, gla_gate_bias,
              gla_out_gain, gdn_conv, gdn_a_log, gdn_dt_bias, gdn_out_gain, att_q_gain, att_k_gain, w_out,
              ffn_gate_up, ffn_down, moe_router, moe_router_bias, moe_gate_up, moe_down):
    L = x.shape[1]
    rows = L // GRID_W
    row = jnp.repeat(jnp.arange(rows), GRID_W).astype(F32)
    col = jnp.tile(jnp.arange(GRID_W), rows).astype(F32)
    inv_freq = ROPE_THETA ** (-jnp.arange(0, HEAD_DIM // 2, 2, dtype=F32) / (HEAD_DIM // 2))
    ang_row = row[:, None] * inv_freq
    ang_col = col[:, None] * inv_freq

    h_lat, h_ctx = x, ctx
    for layer in range(DEPTH):
        need_ctx = layer < DEPTH - 1
        m_lat = jax.nn.silu(c) @ w_mod[layer] + b_mod[layer]
        m_ctx = jax.nn.silu(c_ctx) @ w_mod[layer] + b_mod[layer]
        sh1, sc1, g1, sh2, sc2, g2 = jnp.split(m_lat[:, None, :], 6, axis=-1)
        sh1c, sc1c, g1c, sh2c, sc2c, g2c = jnp.split(m_ctx, 6, axis=-1)

        a_lat = modulate(rmsnorm(h_lat, norm_mix[layer]), sh1, sc1)
        a_ctx = modulate(rmsnorm(h_ctx, norm_mix[layer]), sh1c, sc1c)
        p_lat = split_cols(a_lat @ w_in[layer])
        p_ctx = split_cols(a_ctx @ w_in[layer])
        gla_c, gla_l = gla_mixer(p_ctx[0:5], p_lat[0:5], gla_gate_up[layer], gla_gate_bias[layer],
                                 gla_out_gain[layer], need_ctx)
        gdn_c, gdn_l = gdn_mixer(p_ctx[5:11], p_lat[5:11], gdn_conv[layer], gdn_a_log[layer], gdn_dt_bias[layer],
                                 gdn_out_gain[layer], need_ctx)
        att_c, att_l = attention_mixer(p_ctx[11:14], p_lat[11:14], att_q_gain[layer], att_k_gain[layer],
                                       ang_row, ang_col, need_ctx)
        y_lat = jnp.concatenate([gla_l, gdn_l, att_l], axis=-1).astype(h_lat.dtype) @ w_out[layer]
        h_lat = h_lat + g1 * y_lat
        if need_ctx:
            y_ctx = jnp.concatenate([gla_c, gdn_c, att_c], axis=-1).astype(h_ctx.dtype) @ w_out[layer]
            h_ctx = h_ctx + g1c * y_ctx

        b_lat = modulate(rmsnorm(h_lat, norm_ffn[layer]), sh2, sc2)
        j = layer // 2
        if layer % 2 == 0:
            h_lat = h_lat + g2 * swiglu(b_lat, ffn_gate_up[j], ffn_down[j])
        else:
            h_lat = h_lat + g2 * moe_swiglu(b_lat, moe_router[j], moe_router_bias[j], moe_gate_up[j], moe_down[j])
        if need_ctx:
            b_ctx = modulate(rmsnorm(h_ctx, norm_ffn[layer]), sh2c, sc2c)
            if layer % 2 == 0:
                h_ctx = h_ctx + g2c * swiglu(b_ctx, ffn_gate_up[j], ffn_down[j])
            else:
                h_ctx = h_ctx + g2c * moe_swiglu(b_ctx, moe_router[j], moe_router_bias[j], moe_gate_up[j],
                                                 moe_down[j])
    return h_lat


_drawn_inputs = setup_inputs


def setup_inputs(seed=0):
    import zlib

    import numpy as np

    out = dict(_drawn_inputs(seed))
    spreads = {}
    factors = {'norm_mix': 5.665,
     'norm_ffn': 3.679,
     'gla_gate_bias': 6.215,
     'gla_out_gain': 8.0,
     'gdn_out_gain': 7.225,
     'att_q_gain': 8.0,
     'att_k_gain': 8.0,
     'moe_router_bias': 14.655}
    for name, (base, spread) in spreads.items():
        noise = np.random.default_rng([zlib.crc32(name.encode()), seed]).standard_normal(out[name].shape)
        drawn = base * np.exp(spread * noise) if base else spread * noise
        out[name] = __import__('jax').numpy.asarray(drawn.astype(out[name].dtype))
    for name, factor in factors.items():
        out[name] = (out[name] * factor).astype(out[name].dtype)
    return out
```

```python
from contextlib import ExitStack

import numpy as np
import concourse.bass as bass
from concourse import mybir

ALU = mybir.AluOpType
ACT = mybir.ActivationFunctionType
F32 = mybir.dt.float32
I32 = mybir.dt.int32
U32 = mybir.dt.uint32
AX = mybir.AxisListType.X

P = 128
LAYERS = 2
D = 1024
KD = D // P
TOK = 512
STREAM = 256
TILES = TOK // P
CHUNK = 64
CHUNKS = TOK // CHUNK
HD = 64
EPS = 1e-6
D_FF = 2816
FC = D_FF // P
EXPERTS = 8
SLOTS = 128
RING = 11
BLK = 1024
LEVELS = 6
Q_HEADS, KV_HEADS = 8, 2
C_GLA_Q, C_GLA_K, C_GLA_V, C_GLA_R, C_GLOW = 0, 256, 512, 768, 1024
C_GDN_Q, C_GDN_K, C_GDN_V, C_GDN_Z, C_AB, C_ATT = 1056, 1312, 1568, 1824, 2080, 2096
IN_BLOCKS = [("att0", C_ATT, True), ("att1", C_ATT + 256, True), ("att2", C_ATT + 512, True),
             ("gdn0", C_GDN_Q, False), ("gdn1", C_GDN_K, False), ("gdn2", C_GDN_V, False),
             ("gq", C_GLA_Q, False), ("gk", C_GLA_K, False), ("gv", C_GLA_V, True),
             ("gr", C_GLA_R, False), ("gz", C_GDN_Z, False)]
MOD_BLOCKS = 6 * D // 512

PARAMS = [("ident", 128), ("ones", 128), ("headones", 128), ("lt", 256), ("minc", 256),
          ("level", 2 * LEVELS * 128), ("ranktri", 128), ("maskc", 128), ("iota", 128), ("iota8", 8),
          ("scanmask", TOK), ("cos", 128), ("sin", 128), ("eps", 1), ("one", 1),
          ("cond", 16), ("bmod", LAYERS * 48), ("norms", LAYERS * 16), ("gate_up", LAYERS * 512),
          ("gate_bias", LAYERS * 4), ("gains", LAYERS * 2), ("conv", LAYERS * 30), ("dtb", LAYERS * 8),
          ("alog", LAYERS * 8), ("qkgain", LAYERS * 128), ("router", 64), ("rbias", 8),
          ("wsmall", LAYERS * KD * 48)]
OFFSET, NPARAM = {}, 0
for _name, _width in PARAMS:
    OFFSET[_name] = NPARAM
    NPARAM += _width


class Counts:

    def __init__(self, sems):
        self.sems, self.n, self.per, self.turn, self.start = sems, {}, {}, None, None
        self.held = {bank: ("params_in", 16) for bank in range(8)}

    def seen(self, name):
        return self.n.get(name, 0)

    def at(self, name, count):
        if self.turn is not None and self.per.get(name):
            assert self.per[name] + count > 0, (name, count)
            return self.per[name] * self.turn + count
        assert count > 0, (name, count)
        return count

    def next(self, name, k=1):
        self.n[name] = self.seen(name) + k
        return self.at(name, self.n[name])

    def up(self, name, k=1):
        self.n[name] = self.seen(name) + k
        return k

    def now(self, name):
        return self.at(name, self.seen(name))

    def filled(self, bank, emptied_by, k=1):
        self.n[emptied_by] = self.seen(emptied_by) + k
        for b in (bank if isinstance(bank, (list, tuple)) else [bank]):
            self.held[b] = (emptied_by, self.n[emptied_by])
        return self.n[emptied_by]

    def emptied(self, bank):
        name, count = self.held[bank]
        return self.sems[name], self.at(name, count)

    def begin(self):
        self.start = dict(self.n)
        self.held_start = dict(self.held)

    def repeat(self, turn):
        self.per = {k: v - self.start.get(k, 0) for k, v in self.n.items() if v != self.start.get(k, 0)}
        for b, (name, count) in self.held.items():
            if self.held_start.get(b) != (name, count):
                self.held[b] = (name, count - self.per.get(name, 0))
        self.n, self.turn = dict(self.start), turn

    def end(self, turns):
        self.n = dict(self.start)
        for k, v in self.per.items():
            self.n[k] = self.start.get(k, 0) + v * turns
        for b, (name, count) in list(self.held.items()):
            self.held[b] = (name, count + self.per.get(name, 0) * (turns - 1)) if self.per.get(name) else (name, count)
        self.per, self.turn = {}, None


SEMS = ["params_in", "x_in", "ring_free", "out_stored"] + [f"ring_full{i}" for i in range(RING)] + [
    "pe_step", "act_step", "dve_step", "pool_step",
    "cond_exp", "cond", "mod_psum", "mod_row", "modT_psum", "mod",
    "sq", "sumsq_psum", "rstd", "a", "h_mix", "h_ffn",
    "projd_psum", "proja_psum", "projd", "proja",
    "att_sq", "att_ss", "att_rstd", "att_normed", "qk", "kz_zero", "cin_zero",
    "qT_psum", "kT_psum", "qT", "kz", "scores_psum", "smax", "att_exp", "att_p", "pT_psum", "pT",
    "pv_psum", "att_out",
    "conv", "conv_exp", "conv_exp1", "conv_rec", "convd", "qk_sq", "qk_ss_psum", "qk_rn", "kq", "kz2",
    "kz2_zero", "kvT_psum", "kvtok",
    "gx", "g_act", "g", "gscan_psum", "eg", "erb",
    "gr", "dec_psum", "decE", "decB", "dtb", "qg", "kd", "ke", "kk_psum", "kk_out",
    "y_psum", "ym", "dtu_psum", "tu", "x_psum", "x_out", "ru_psum", "gdn_u", "ro_psum", "gdn_o",
    "rw_psum", "gdn_s",
    "gate_psum", "gate_x", "gate_ln", "gate_mn", "gate_D", "gate_E", "gate_q", "gate_k", "gate_f", "gate_fe", "gate_c",
    "ktr_psum", "ktok", "gs_psum", "gla_pt", "go_psum", "gla_o", "gw_psum", "gla_s",
    "fin_sq", "fin_psum", "fin_rs", "fin_e", "fin_e1", "fin_rec", "fin_sg", "fin_o", "mix",
    "wout_psum", "gu_psum", "gu_exp", "gu_act", "down_psum",
    "logit_psum", "bT_psum", "btok", "top", "top_e", "mask", "rank_psum", "gmat", "gw", "gT_psum", "smat",
    "xe_psum", "xe", "mgu_psum", "mgu_exp", "mgu_act", "aT_psum", "aT_sb", "y2_psum", "y2", "sc_psum",
    "flag", "final"]


def gdn_order():
    order = []
    for i in range(TILES + 1):
        if i < TILES:
            for kind in ("decay", "kk", "first"):
                order += [(kind, d, i, 1) for d in range(2)]
        for level in range(2, LEVELS + 1):
            if i < TILES:
                order += [("Y", d, i, level) for d in range(2)]
            if i > 0 and level < 6:
                kind, k = ("ru", "ro")[level % 2], (level - 2) // 2
                order += [(kind, d, i - 1, k) for d in range(2)]
            if i < TILES:
                order += [("dTU", d, i, level) for d in range(2)]
        if i < TILES:
            order += [("X", d, i, 0) for d in range(2)]
    return order


TILE_ORDER = [[0, 1, 2, 3], [1, 0, 3, 2]]
CHUNK_ORDER = [[0, 1, 2, 3, 4, 5, 6, 7], [3, 2, 1, 0, 7, 6, 5, 4]]


def rep(ap, axis, n):
    ap = ap.unsqueeze(axis)
    shape = list(ap.shape)
    shape[axis] = n
    return ap.broadcast_to(shape)


def build(nc, xT, params, w_mod, w_in, w_out, ffn_gu, ffn_down, moe_gu, moe_down, outT):
    with ExitStack() as ctx:
        def sb(name, shape, dt=F32):
            return ctx.enter_context(nc.sbuf_tensor(name, shape, dt))

        par = sb("par", [P, NPARAM])
        hT = sb("hT", [P, KD, TOK])
        aT = sb("aT", [P, KD, TOK])
        ring = sb("ring", [P, RING, BLK])
        arena = sb("arena", [P, 26112])
        mcol = sb("mcol", [P, 48, 2])
        coef = sb("coef", [P, 2, 8, 2])
        cond = sb("cond_sb", [P, 8, 2])
        ab = sb("ab", [P, TILES, 16])
        gsm = sb("gsm", [P, 6, TILES, 8])
        eg = sb("eg", [P, 4, TILES, 4])
        erb = sb("erb", [P, 2, TILES, 4])
        eend = sb("eend", [P, 2, 2, 4, 2])
        state = sb("state", [P, 2, 2, P])
        ubuf = sb("ubuf", [P, 2, 256])
        ssq = sb("ssq", [P, TILES, 10])
        nmx = sb("nmx", [P, 34])
        rsum = sb("rsum", [P, 32])
        flag = sb("flag", [1, 1], I32)
        gfac = ubuf[:, 0, 0:128].rearrange("p (a b c d) -> p a b c d", a=4, b=2, c=2)
        rtop = state[:, 0, 0, 0:96].rearrange("p (a b c) -> p a b c", a=2, b=6)
        cnt = state[:, 0, 0, 96:104]
        idx = state[:, 0, 1, 0:16].bitcast(U32).rearrange("p (a b) -> p a b", a=2)
        ps = [ctx.enter_context(nc.psum_tensor(f"ps{i}", [P, 512], F32)) for i in range(8)]
        S = {name: ctx.enter_context(nc.semaphore(name)) for name in SEMS}

        def pr(name, width=None, at=0, rows=P):
            o = OFFSET[name] + at
            return par[0:rows, o:o + (width if width is not None else dict(PARAMS)[name])]

        ident, ones, headones = pr("ident"), pr("ones"), pr("headones")
        eps, one = pr("eps"), pr("one")
        lt = [pr("lt", 128, 128 * d) for d in range(2)]
        minc = [pr("minc", 128, 128 * d) for d in range(2)]
        maskc = [pr("maskc", 64, 64 * d) for d in range(2)]

        def level_mask(d, l):
            return pr("level", 128, 128 * (LEVELS * d + l - 1))

        def ar(offset, *shape):
            size = int(np.prod(shape))
            v = arena[:, offset:offset + size]
            if len(shape) == 1:
                return v
            names = "abcde"[:len(shape)]
            return v.rearrange(f"p ({' '.join(names)}) -> p {' '.join(names)}",
                               **{n: s for n, s in zip(names[1:], shape[1:])})

        gq, gk, gr_, gz = (ar(1024 * i, 2, TOK) for i in range(4))
        glow = arena[0:32, 4096:4608]
        gv = ar(4608, TILES, 256)
        KQ = 5632
        UN = KQ + 4096 + 2048
        OT = UN + 12288
        kq = ar(KQ, 2, 2, TOK)
        kz = ar(KQ + 2048, 2, 2, TOK)
        cin = ar(KQ, 6, 2, 260)
        kvtok = ar(KQ + 4096, TILES, 512)
        cv = ar(UN + 11264, 6, 2, 256)
        ce = ar(UN, 6, 2, 256)
        csq = ar(UN + 3072, 4, TOK)
        crn = ar(UN + 5120, 4, TOK)
        og = ar(OT, 2, 2, TOK)
        att = ar(UN, TILES, 12, HD)
        qT = ar(UN + 3072, 4, TOK)
        akz = ar(UN + 5120, 2, TOK)
        Pb = ar(UN + 6144, 3, TOK)
        PTb = ar(UN + 7680, 2, 4, P)
        asq = ar(UN + 6144, TILES, 10, HD)
        ra = ar(UN + 8704, 10, HD)
        rb = ar(UN + 9344, 10, HD)

        def scratch(d, k):
            return ar(UN + 3072 * d + 512 * k, 4, P)

        Gr, E, AT, T, U, Y = ([scratch(d, k) for d in range(2)] for k in range(6))

        def slot(d, i):
            o = UN + 6144 + 1536 * (2 * d + i % 2)
            return ar(o, 4, P), ar(o + 512, 256), ar(o + 768, 2, P), ar(o + 1024, 4, HD), ar(o + 1280, 2, P)

        GA = KQ
        qp = ar(GA, 2, 2, TOK)
        kp = ar(GA + 2048, 2, 2, TOK)
        qz = ar(GA + 4096, 2, 2, 2, TOK)
        kt = ar(GA + 8192, 2, TILES, 256)
        pg = ar(GA + 10240, 2, TILES, 4, CHUNK)
        gw_ = ar(GA + 12288, 2, 4, TOK)
        ol = ar(GA + 16384, 2, 2, TOK)
        fsq, fsg, frs = ar(GA, 4, TOK), ar(GA + 2048, 4, TOK), ar(GA + 4096, 4, TOK)
        nsq, nhn = ar(0, KD, TOK), ar(4096, KD, TOK)
        mrow = arena[0:2, 12288:12288 + 1024].rearrange("p (a b) -> p a b", a=2)
        act = ar(0, FC, TOK)
        fe, ft = ar(11264, 4, TOK), ar(13312, 4, TOK)
        btok = ar(8192, 2, D)
        gm = ar(10240, 2, EXPERTS, SLOTS)
        gwt = ar(12288, 2, EXPERTS, SLOTS)
        sm = ar(14336, EXPERTS, STREAM)
        xe = ar(16384, KD, SLOTS)
        mact = ar(17408, D_FF)
        mactT = ar(20224, FC, SLOTS)
        y2 = ar(23040, D)
        me, mt = ar(24064, 2, 256), ar(24576, 2, 256)
        osb = ar(0, KD, STREAM)

        def h_range(layer):
            return (0, TOK) if layer < LAYERS - 1 else (STREAM, TOK)

        def att_units(layer):
            out, g = [], 0
            for lat in ((0, 1) if layer < LAYERS - 1 else (1,)):
                for pair in range(4):
                    for par_ in range(2):
                        for qt in range(2):
                            out.append((2 * pair + par_, 2 * lat + qt, 4 if lat else 2, g, pair, lat, qt))
                    g += 1
            return out

        def rstd_buf(n):
            return fe_rstd[:, 0:n]

        fe_rstd = ar(8192, TOK)

        def proj_dst(name, half):
            if name.startswith("att"):
                c = 4 * int(name[3])
                place = slice(8, 12) if c == 8 else slice(c // 4, 8, 2)
                return att[:, 2 * half:2 * half + 2, place, :]
            if name == "gv":
                return gv[:, 2 * half:2 * half + 2, :]
            if name.startswith("gdn"):
                return cin[:, 2 * int(name[3]) + half, :, 2:258]
            return {"gq": gq, "gk": gk, "gr": gr_, "gz": gz}[name][:, half, :]

        def proj_src(name, bank):
            if name.startswith("att"):
                return ps[bank][:, :].rearrange("p (a b c) -> p a b c", a=2, b=4)
            if name == "gv" or name.startswith("gdn"):
                return ps[bank][:, :].rearrange("p (a b) -> p a b", a=2)
            return ps[bank][:, :]

        block = ctx.enter_context(nc.Block())

        @block.sync
        def _(sp):
            G = Counts(S)
            sp.dma_start(par[:, :], params).then_inc(S["params_in"], 16)
            sp.dma_start(hT[:, :, :], xT.rearrange("(k p) t -> p k t", p=P)).then_inc(S["x_in"], 16)
            count = [0]

            def load(src, k):
                n = count[0]
                count[0] += 1
                if G.turn is not None or n >= RING:
                    G.n["ring_free"] = n - RING + 1
                    sp.wait_ge(S["ring_free"], G.at("ring_free", n - RING + 1))
                dst = ring[:, n % RING, :]
                if k > 1:
                    dst = dst.rearrange("p (k c) -> p k c", k=k)
                sp.dma_start(dst, src).then_inc(S[f"ring_full{n % RING}"], 16)

            def load_cols(w, c0):
                for kb in range(2):
                    load(w[512 * kb:512 * kb + 512, c0:c0 + 256].rearrange("(k p) c -> p k c", p=P), 4)

            def load_ffn(gu, down):
                for j in range(11):
                    for kb in range(2):
                        for s in range(2):
                            c0 = D_FF * s + 256 * j
                            load(gu[512 * kb:512 * kb + 512, c0:c0 + 256].rearrange("(k p) c -> p k c", p=P), 4)
                for f in range(FC):
                    load(down[P * f:P * f + P, :], 1)

            for layer in range(LAYERS):
                for i in range(2 * MOD_BLOCKS):
                    load_cols(w_mod[layer], 256 * i)
                for _, c0, _ in IN_BLOCKS:
                    load_cols(w_in[layer], c0)
                for i in range(4):
                    load_cols(w_out[layer], 256 * i)
                if layer == 0:
                    load_ffn(ffn_gu[0], ffn_down[0])

            def experts():
                first = count[0]
                G.n["ring_free"] = first - RING
                G.begin()
                load_ffn(moe_gu[0, 0], moe_down[0, 0])
                G.n["ring_free"] = count[0] - RING
                with sp.Fori(1, EXPERTS) as e:
                    G.repeat(e)
                    count[0] = first
                    load_ffn(moe_gu[0, e], moe_down[0, e])
                G.end(EXPERTS)
                count[0] = first + 66 * EXPERTS

            experts()
            sp.wait_ge(S["flag"], 1)
            over = sp.value_load(flag[0:1, 0:1], min_val=0, max_val=1)
            with sp.If(over > 0):
                experts()
            sp.wait_ge(S["final"], 1)
            sp.dma_start(outT.rearrange("(k p) t -> p k t", p=P), osb).then_inc(S["out_stored"], 16)
            sp.wait_ge(S["out_stored"], 16)

        @block.tensor
        def _(pe):
            G = Counts(S)
            count = [0]

            def block_in():
                s = count[0] % RING
                count[0] += 1
                pe.wait_ge(S[f"ring_full{s}"], G.next(f"ring_full{s}", 16))
                return s

            owed = [0]

            def release(mm):
                mm.then_inc(S["ring_free"], 1)

            def release_next():
                owed[0] += 1

            def pay(mm):
                if owed[0]:
                    owed[0] -= 1
                    release(mm)

            def modulation(layer):
                for i in range(MOD_BLOCKS + 1):
                    if i < MOD_BLOCKS:
                        pe.wait_ge(*G.emptied(7))
                        for half in range(2):
                            for kb in range(2):
                                s = block_in()
                                w = ring[:, s, :].rearrange("p (k c) -> p k c", k=4)
                                for kk in range(4):
                                    mm = pe.matmul(ps[7][0:2, 256 * half:256 * half + 256],
                                                   cond[:, 4 * kb + kk, :], w[:, kk, :],
                                                   start=(kb + kk == 0), stop=(kb == 1 and kk == 3))
                                    if kk == 0:
                                        pay(mm)
                                if half == 0 or kb == 0:
                                    release(mm)
                                else:
                                    release_next()
                        mm.then_inc(S["mod_psum"], 1)
                        G.filled(7, "mod_row")
                    if i == 0:
                        pe.wait_ge(*G.emptied(0))
                    else:
                        pe.wait_ge(S["mod_row"], G.at("mod_row", G.seen("mod_row") - (1 if i < MOD_BLOCKS else 0)))
                        for q in range(4):
                            c = 4 * (i - 1) + q
                            mm = pe.transpose(ps[0][:, 2 * c:2 * c + 2],
                                              mrow[0:2, (i - 1) % 2, P * q:P * q + P], ident[0:2, 0:2])
                mm.then_inc(S["modT_psum"], 1)
                G.filled(0, "mod")

            def sum_over_features(t0, t1):
                pe.wait_ge(*G.emptied(5))
                for k in range(KD):
                    pe.wait_ge(S["sq"], G.next("sq"))
                    mm = pe.matmul(ps[5][:, 0:t1 - t0], ones, nsq[:, k, t0:t1], start=(k == 0), stop=(k == KD - 1))
                mm.then_inc(S["sumsq_psum"], 1)
                G.filled(5, "rstd")

            def projections(layer):
                base = G.seen("a")
                for n, (_, _, by_token) in enumerate(IN_BLOCKS):
                    s = [block_in(), block_in()]
                    w = [ring[:, x, :].rearrange("p (k c) -> p k c", k=4) for x in s]
                    for half in range(2):
                        bank = (0, 5)[half] + n % 2
                        pe.wait_ge(*G.emptied(bank))
                        for t in range(2 if by_token else 1):
                            for k in range(KD):
                                if n == 0 and half == 0 and t == 0:
                                    pe.wait_ge(S["a"], G.at("a", base + k + 1))
                                if by_token:
                                    tile = 2 * half + t
                                    mm = pe.matmul(ps[bank][:, 256 * t:256 * t + 256],
                                                   aT[:, k, P * tile:P * tile + P], w[k // 4][:, k % 4, :],
                                                   start=(k == 0), stop=(k == KD - 1))
                                else:
                                    mm = pe.matmul(ps[bank][:, :], w[k // 4][:, k % 4, P * half:P * half + P],
                                                   aT[:, k, :], start=(k == 0), stop=(k == KD - 1))
                                if k == 0:
                                    pay(mm)
                                if half == 1 and t == (1 if by_token else 0) and k == 3:
                                    release(mm)
                        if half == 0:
                            mm.then_inc(S["projd_psum"], 1)
                            G.filled(bank, "projd")
                        else:
                            mm.then_inc(S["proja_psum"], 1)
                            G.filled(bank, "proja")
                            release_next()
                    if n == 5:
                        w_small = pr("wsmall", KD * 48, layer * KD * 48).rearrange("p (k c) -> p k c", k=KD)
                        pe.wait_ge(*G.emptied(4))
                        for tile in range(TILES):
                            for k in range(KD):
                                mm = pe.matmul(ps[4][:, 16 * tile:16 * tile + 16],
                                               aT[:, k, P * tile:P * tile + P], w_small[:, k, 32:48],
                                               start=(k == 0), stop=(k == KD - 1))
                        mm.then_inc(S["projd_psum"], 1)
                        G.filled(4, "projd")
                        pe.wait_ge(*G.emptied(7))
                        for k in range(KD):
                            mm = pe.matmul(ps[7][0:32, :], w_small[:, k, 0:32], aT[:, k, :],
                                           start=(k == 0), stop=(k == KD - 1))
                        mm.then_inc(S["proja_psum"], 1)
                        G.filled(7, "proja")
                G.n["a"] = base + KD

            def attention(layer):
                for i in range(TILES):
                    pe.wait_ge(S["qk"], G.next("qk"))
                    if layer == 0 or i >= 2:
                        pe.wait_ge(*G.emptied(2 + i % 2))
                        for hh in range(4):
                            q = att[:, i, 2 * hh:2 * hh + 2, :]
                            mm = pe.transpose(ps[2 + i % 2][:, P * hh:P * hh + P], q, ident)
                        mm.then_inc(S["qT_psum"], 1)
                        G.filled(2 + i % 2, "qT")
                    pe.wait_ge(*G.emptied(4))
                    mm = pe.transpose(ps[4][:, 0:P], att[:, i, 8:10, :], ident)
                    mm.then_inc(S["kT_psum"], 1)
                    G.filled(4, "kz")
                pe.wait_ge(S["qT"], G.now("qT"))
                pe.wait_ge(S["kz"], G.now("kz"))
                units = att_units(layer)
                exp0, p0, pt0 = G.seen("att_exp"), G.seen("att_p"), G.seen("pT")
                for i in range(len(units) + 2):
                    if i < len(units):
                        h, qt, nk, *_ = units[i]
                        pe.wait_ge(*G.emptied(i % 2))
                        mm = pe.matmul(ps[i % 2][:, 0:P * nk], qT[:, h % 4, P * qt:P * qt + P],
                                       akz[:, h // 4, 0:P * nk], start=True, stop=True)
                        mm.then_inc(S["scores_psum"], 1)
                        G.filled(i % 2, "att_exp")
                    if 1 <= i <= len(units):
                        h, qt, nk, *_ = units[i - 1]
                        pe.wait_ge(S["att_p"], G.next("att_p"))
                        pe.wait_ge(*G.emptied(2 + (i - 1) % 2))
                        for kt_ in range(nk):
                            mm = pe.transpose(ps[2 + (i - 1) % 2][:, P * kt_:P * kt_ + P],
                                              Pb[:, (i - 1) % 3, P * kt_:P * kt_ + P], ident)
                        mm.then_inc(S["pT_psum"], 1)
                        G.filled(2 + (i - 1) % 2, "pT")
                    if i >= 2:
                        h, qt, nk, g, pair, lat, qq = units[i - 2]
                        pe.wait_ge(S["pT"], G.at("pT", pt0 + i - 1))
                        bank = 4 + g % 2
                        if (i - 2) % 4 == 0:
                            pe.wait_ge(*G.emptied(bank))
                        half = HD * (h % 2)
                        for kt_ in range(nk):
                            mm = pe.matmul(ps[bank][half:half + HD, P * qq:P * qq + P],
                                           att[:, kt_, 10 + h // 4, :], PTb[:, (i - 2) % 2, kt_, :],
                                           start=(kt_ == 0), stop=(kt_ == nk - 1))
                        if (i - 2) % 4 == 3:
                            mm.then_inc(S["pv_psum"], 1)
                            G.filled(bank, "att_out")

            def gdn_prepare(layer):
                for n, c in enumerate((2, 3, 0, 1)):
                    pe.wait_ge(S["qk_sq"], G.next("qk_sq"))
                    pe.wait_ge(*G.emptied(n % 2))
                    mm = pe.matmul(ps[n % 2][:, :], headones, csq[:, c, :], start=True, stop=True)
                    mm.then_inc(S["qk_ss_psum"], 1)
                    G.filled(n % 2, "qk_rn")
                pe.wait_ge(S["g"], G.next("g"))
                pe.wait_ge(*G.emptied(4))
                for d in range(2):
                    for kind, m in ((0, minc[d]), (2, lt[d])):
                        mm = pe.matmul(ps[4][:, 16 * (kind + d):16 * (kind + d) + 16], m,
                                       gsm[:, 4, :, 4 * d:4 * d + 4], start=True, stop=True)
                mm.then_inc(S["gscan_psum"], 1)
                G.filled(4, "eg")
                pe.wait_ge(S["kq"], G.next("kq", 4))
                pe.wait_ge(S["convd"], G.next("convd", 6))
                for tile in range(TILES):
                    pe.wait_ge(*G.emptied(2 + tile % 2))
                    t = slice(P * tile, P * tile + P)
                    for n in range(4):
                        src = kq[:, 0, n, t] if n < 2 else cv[:, 2 + n, tile // 2, P * (tile % 2):P * (tile % 2) + P]
                        mm = pe.transpose(ps[2 + tile % 2][:, P * n:P * n + P], src, ident)
                    mm.then_inc(S["kvT_psum"], 1)
                    G.filled(2 + tile % 2, "kvtok")
                pe.wait_ge(S["kvtok"], G.now("kvtok"))
                pe.wait_ge(S["kz2"], G.next("kz2"))

            def gdn(layer):
                misc = [0]

                def bank67():
                    misc[0] += 1
                    return 6 + misc[0] % 2

                tu, kko, xo = {}, {}, {}
                for kind, d, i, k in gdn_order():
                    if kind in ("ru", "ro"):
                        c = k if d == 0 else 1 - k
                        r = slice(CHUNK * c, CHUNK * c + CHUNK)
                    tile = TILE_ORDER[d][i]
                    pt, xv, xk, kd_, qg_ = slot(d, i)
                    if kind == "decay":
                        pe.wait_ge(S["gr"], G.next("gr"))
                        pe.wait_ge(*G.emptied(4 + d))
                        mm = pe.matmul(ps[4 + d][:, :], lt[d], Gr[d].rearrange("p a b -> p (a b)"), start=True, stop=True)
                        mm.then_inc(S["dec_psum"], 1)
                        G.filled(4 + d, "decE")
                        pe.wait_ge(*G.emptied(2 + d))
                        mm = pe.matmul(ps[2 + d][:, :], ones, Gr[d].rearrange("p a b -> p (a b)"), start=True, stop=True)
                        mm.then_inc(S["dec_psum"], 1)
                        G.filled(2 + d, "decB")
                    elif kind == "kk":
                        t = slice(P * tile, P * tile + P)
                        for pair in range(2):
                            bank = (d, 4 + d)[pair]
                            pe.wait_ge(*G.emptied(bank))
                            for p_ in range(2):
                                mm = pe.matmul(ps[bank][:, 256 * p_:256 * p_ + 256], kz[:, pair, p_, t],
                                               kq[:, :, pair, t], start=True, stop=True)
                            mm.then_inc(S["kk_psum"], 1)
                            kko[d] = G.filled(bank, "kk_out")
                    elif kind == "first":
                        pe.wait_ge(S["kk_out"], G.at("kk_out", kko[d]))
                        pe.wait_ge(*G.emptied(d))
                        for h in range(4):
                            mm = pe.matmul(ps[d][:, P * h:P * h + P], AT[d][:, h, :], ident, start=True, stop=True)
                        mm.then_inc(S["y_psum"], 1)
                        tu[d] = G.filled(d, "tu")
                    elif kind == "Y":
                        pe.wait_ge(S["tu"], G.at("tu", tu[d]))
                        pe.wait_ge(*G.emptied(d))
                        for h in range(4):
                            mm = pe.matmul(ps[d][:, P * h:P * h + P], AT[d][:, h, :], T[d][:, h, :],
                                           start=True, stop=True)
                        mm.then_inc(S["y_psum"], 1)
                        xo[d, "ym"] = G.filled(d, "ym")
                    elif kind == "dTU":
                        pe.wait_ge(S["ym"], G.at("ym", xo[d, "ym"]))
                        if k < LEVELS:
                            pe.wait_ge(*G.emptied(2 + d))
                            for h in range(4):
                                pe.matmul(ps[2 + d][:, P * h:P * h + P], U[d][:, h, :], Y[d][:, h, :],
                                          start=True, stop=True)
                        pe.wait_ge(*G.emptied(4 + d))
                        for h in range(4):
                            mm = pe.matmul(ps[4 + d][:, P * h:P * h + P], Y[d][:, h, :], U[d][:, h, :],
                                           start=True, stop=True)
                        mm.then_inc(S["dtu_psum"], 1)
                        tu[d] = G.filled([2 + d, 4 + d] if k < LEVELS else 4 + d, "tu")
                    elif kind == "X":
                        pe.wait_ge(S["tu"], G.at("tu", tu[d]))
                        pe.wait_ge(S["ke"], G.next("ke"))
                        pe.wait_ge(*G.emptied(d))
                        for h in range(4):
                            mm = pe.matmul(ps[d][:, HD * h:HD * h + HD], U[d][:, h, :],
                                           kvtok[:, tile, 256 + HD * h:256 + HD * h + HD], start=True, stop=True)
                        mm.then_inc(S["x_psum"], 1)
                        G.filled(d, "x_out")
                        pe.wait_ge(*G.emptied(2 + d))
                        for h in range(4):
                            half = HD * (h % 2)
                            mm = pe.matmul(ps[2 + d][half:half + HD, P * (h // 2):P * (h // 2) + P],
                                           E[d].rearrange("p a b -> p (a b)")[:, HD * h:HD * h + HD],
                                           U[d][:, h, :], start=True, stop=True)
                        mm.then_inc(S["x_psum"], 1)
                        xo[d, i] = G.filled(2 + d, "x_out")
                    elif kind == "ru":
                        pe.wait_ge(S["x_out"], G.at("x_out", xo[d, i]))
                        if (i, k) != (0, 0):
                            pe.wait_ge(S["gdn_s"], G.at("gdn_s", G.seen("gdn_s") - 1 + d))
                        bank = bank67()
                        pe.wait_ge(*G.emptied(bank))
                        for pair in range(2):
                            mm = pe.matmul(ps[bank][r, P * pair:P * pair + P], xk[:, pair, r], state[:, d, pair, :],
                                           start=True, stop=True)
                        mm.then_inc(S["ru_psum"], 1)
                        xo[d, "u"] = G.filled(bank, "gdn_u")
                    elif kind == "ro":
                        pe.wait_ge(S["gdn_u"], G.at("gdn_u", xo[d, "u"]))
                        if k == 0:
                            pe.wait_ge(S["qg"], G.next("qg"))
                            pe.wait_ge(S["kd"], G.next("kd"))
                        bank = bank67()
                        pe.wait_ge(*G.emptied(bank))
                        for pair in range(2):
                            pe.matmul(ps[bank][:, HD * pair:HD * pair + HD], state[:, d, pair, :], qg_[:, pair, r],
                                      start=True, stop=False, skip_group_check=True)
                            for p_ in range(2):
                                h = 2 * pair + p_
                                half = HD * p_
                                mm = pe.matmul(ps[bank][half:half + HD, HD * pair:HD * pair + HD],
                                               ubuf[r, d, HD * h:HD * h + HD], pt[r, h, r],
                                               start=False, stop=True, skip_group_check=True)
                        mm.then_inc(S["ro_psum"], 1)
                        G.filled(bank, "gdn_o")
                        bank = bank67()
                        pe.wait_ge(*G.emptied(bank))
                        for pair in range(2):
                            mm = pe.matmul(ps[bank][:, P * pair:P * pair + P],
                                           kd_[r, 2 * pair:2 * pair + 2, :].rearrange("p a b -> p (a b)"),
                                           ubuf[r, d, P * pair:P * pair + P], start=True, stop=True)
                        mm.then_inc(S["rw_psum"], 1)
                        G.filled(bank, "gdn_s")

            def gla(layer):
                gu_ = pr("gate_up", 512, 512 * layer, 32)
                for d in range(2):
                    for ch in range(2):
                        pe.wait_ge(*G.emptied(2 * d + ch))
                        mm = pe.matmul(ps[2 * d + ch][:, :], gu_[:, 256 * d + P * ch:256 * d + P * ch + P], glow,
                                       start=True, stop=True)
                        mm.then_inc(S["gate_psum"], 1)
                        G.filled(2 * d + ch, "gate_x")
                for d in range(2):
                    pe.wait_ge(S["gate_k"], G.next("gate_k", 2))
                    pe.wait_ge(S["gate_q"], G.next("gate_q", 2))
                    for hf in range(2):
                        pe.wait_ge(*G.emptied(4 + hf))
                        for tt in range(2):
                            tile = 2 * hf + tt
                            for pair in range(2):
                                mm = pe.transpose(ps[4 + hf][:, 256 * tt + P * pair:256 * tt + P * pair + P],
                                                  kp[:, d, pair, P * tile:P * tile + P], ident)
                        mm.then_inc(S["ktr_psum"], 1)
                        G.filled(4 + hf, "ktok")
                        pe.wait_ge(*G.emptied(6 + hf))
                        for tt in range(2):
                            for c in range(2):
                                t = slice(P * (2 * hf + tt) + CHUNK * c, P * (2 * hf + tt) + CHUNK * c + CHUNK)
                                for pair in range(2):
                                    o = 256 * tt + P * pair
                                    mm = pe.matmul(ps[6 + hf][CHUNK * c:CHUNK * c + CHUNK, o:o + P],
                                                   kp[:, d, pair, t], qz[:, d, pair, :, t], start=True, stop=True)
                        mm.then_inc(S["gs_psum"], 1)
                        G.filled(6 + hf, "gla_pt")
                pe.wait_ge(S["ktok"], G.now("ktok"))
                pe.wait_ge(S["gla_pt"], G.now("gla_pt"))
                pe.wait_ge(S["gate_c"], G.next("gate_c"))
                n = 0
                for k in range(CHUNKS):
                    for d in range(2):
                        g = CHUNK_ORDER[d][k]
                        tile, c = g // 2, g % 2
                        r = slice(CHUNK * c, CHUNK * c + CHUNK)
                        t = slice(CHUNK * g, CHUNK * g + CHUNK)
                        bank = n % 4
                        pe.wait_ge(*G.emptied(bank))
                        for pair in range(2):
                            mm = pe.matmul(ps[bank][:, P * pair:P * pair + P], kt[r, d, tile, P * pair:P * pair + P],
                                           gv[r, tile, P * pair:P * pair + P], start=True, stop=True)
                        mm.then_inc(S["gw_psum"], 1)
                        G.filled(bank, "gla_s")
                        if k:
                            pe.wait_ge(S["gla_s"], G.at("gla_s", G.seen("gla_s") - 2))
                        bank = 4 + n % 4
                        pe.wait_ge(*G.emptied(bank))
                        for pair in range(2):
                            pe.matmul(ps[bank][:, HD * pair:HD * pair + HD], state[:, d, pair, :], qp[:, d, pair, t],
                                      start=True, stop=False, skip_group_check=True)
                            for p_ in range(2):
                                h, half = 2 * pair + p_, HD * p_
                                mm = pe.matmul(ps[bank][half:half + HD, HD * pair:HD * pair + HD],
                                               gv[r, tile, HD * h:HD * h + HD], pg[r, d, tile, h, :],
                                               start=False, stop=True, skip_group_check=True)
                        mm.then_inc(S["go_psum"], 1)
                        G.filled(bank, "gla_o")
                        n += 1

            def closing(layer):
                t0, t1 = h_range(layer)
                for m in range(4):
                    pe.wait_ge(S["fin_sq"], G.next("fin_sq"))
                    pe.wait_ge(*G.emptied(m))
                    mm = pe.matmul(ps[m][:, 0:t1 - t0], headones, fsq[:, m, t0:t1], start=True, stop=True)
                    mm.then_inc(S["fin_psum"], 1)
                    G.filled(m, "fin_rs")

            def out_projection(layer):
                t0, t1 = h_range(layer)
                pe.wait_ge(S["mix"], G.next("mix", 4))
                pe.wait_ge(S["att_out"], G.now("att_out"))
                for i in range(4):
                    s = [block_in(), block_in()]
                    w = [ring[:, x, :].rearrange("p (k c) -> p k c", k=4) for x in s]
                    for half in range(2):
                        bank = (2 * i + half) % 4
                        pe.wait_ge(*G.emptied(bank))
                        for k in range(KD):
                            mm = pe.matmul(ps[bank][:, 0:t1 - t0], w[k // 4][:, k % 4, P * half:P * half + P],
                                           aT[:, k, t0:t1], start=(k == 0), stop=(k == KD - 1))
                            if k == 0:
                                pay(mm)
                            if half == 1 and k == 3:
                                release(mm)
                        mm.then_inc(S["wout_psum"], 1)
                        G.filled(bank, "h_mix")
                        if half == 1:
                            release_next()

            def dense_ffn():
                base, act0 = G.seen("a"), G.seen("gu_act")
                for j in range(11):
                    banks = [4 * (j % 2) + x for x in range(4)]
                    for b in banks:
                        pe.wait_ge(*G.emptied(b))
                    for kb in range(2):
                        for u in range(2):
                            s = block_in()
                            w = ring[:, s, :].rearrange("p (k c) -> p k c", k=4)
                            for x in range(2):
                                for k4 in range(4):
                                    k = 4 * kb + k4
                                    if j == 0 and x == 0:
                                        pe.wait_ge(S["a"], G.at("a", base + k + 1))
                                    mm = pe.matmul(ps[banks[2 * u + x]][:, :], w[:, k4, P * x:P * x + P],
                                                   aT[:, k, :], start=(k == 0), stop=(k == KD - 1))
                                    if x == 0 and k4 == 0:
                                        pay(mm)
                            if kb == 0:
                                release(mm)
                            elif u == 0:
                                mm.then_inc(S["gu_psum"], 1)
                                release_next()
                    mm.then_inc(S["gu_psum"], 1)
                    G.filled(banks, "gu_act", 2)
                    release_next()
                G.n["a"] = base + KD
                for b in range(8):
                    pe.wait_ge(*G.emptied(b))
                for f in range(FC):
                    s = block_in()
                    pe.wait_ge(S["gu_act"], G.at("gu_act", act0 + f + 1))
                    for m in range(KD):
                        mm = pe.matmul(ps[m][:, :], ring[:, s, P * m:P * m + P], act[:, f, :],
                                       start=(f == 0), stop=(f == FC - 1))
                        if f == FC - 1:
                            mm.then_inc(S["down_psum"], 1)
                            G.filled(m, "h_ffn")
                        elif m == 0:
                            pay(mm)
                    if f < FC - 1:
                        release(mm)
                release_next()

            def routing():
                base = G.seen("a")
                pe.wait_ge(*G.emptied(0))
                for tile in range(2):
                    t = slice(STREAM + P * tile, STREAM + P * tile + P)
                    for k in range(KD):
                        pe.wait_ge(S["a"], G.at("a", base + k + 1))
                        mm = pe.matmul(ps[0][:, 8 * tile:8 * tile + 8], aT[:, k, t], pr("router", 8, 8 * k),
                                       start=(k == 0), stop=(k == KD - 1))
                mm.then_inc(S["logit_psum"], 1)
                G.filled(0, "top")
                G.n["a"] = base + KD
                for n in range(4):
                    tile, hf = n // 2, n % 2
                    t = slice(STREAM + P * tile, STREAM + P * tile + P)
                    pe.wait_ge(*G.emptied(1 + n))
                    for q in range(4):
                        mm = pe.transpose(ps[1 + n][:, P * q:P * q + P], aT[:, 4 * hf + q, t], ident)
                    mm.then_inc(S["bT_psum"], 1)
                    G.filled(1 + n, "btok")
                pe.wait_ge(S["mask"], G.next("mask"))
                pe.wait_ge(*G.emptied(0))
                pe.matmul(ps[0][:, 0:8], pr("ranktri"), rtop[:, 0, 3, :], start=True, stop=True)
                pe.matmul(ps[0][:, 8:16], ones, rtop[:, 0, 3, :], start=True, stop=False)
                pe.matmul(ps[0][:, 8:16], pr("ranktri"), rtop[:, 1, 3, :], start=False, stop=True)
                pe.matmul(ps[0][:, 16:24], ones, rtop[:, 0, 3, :], start=True, stop=False)
                mm = pe.matmul(ps[0][:, 16:24], ones, rtop[:, 1, 3, :], start=False, stop=True)
                mm.then_inc(S["rank_psum"], 1)
                G.filled(0, "flag")
                pe.wait_ge(S["btok"], G.now("btok"))

            def slot_tables():
                pe.wait_ge(S["gw"], G.next("gw"))
                for n in range(4):
                    pe.wait_ge(*G.emptied(1 + n))
                    for q in range(4):
                        e, tile = 2 * n + q // 2, q % 2
                        mm = pe.transpose(ps[1 + n][:, P * q:P * q + P], gwt[:, tile, e, :], ident)
                    mm.then_inc(S["gT_psum"], 1)
                    G.filled(1 + n, "smat")
                pe.wait_ge(S["smat"], G.now("smat"))

            def expert(e):
                for hf in range(2):
                    pe.wait_ge(*G.emptied(6 + hf))
                    for q in range(4):
                        k = 4 * hf + q
                        for tile in range(2):
                            mm = pe.matmul(ps[6 + hf][:, P * q:P * q + P], btok[:, tile, P * k:P * k + P],
                                           gm[:, tile, e, :], start=(tile == 0), stop=(tile == 1))
                            if q == 0 and tile == 0:
                                pay(mm)
                    mm.then_inc(S["xe_psum"], 1)
                    got = G.filled(6 + hf, "xe")
                evac = {}
                tr = {}

                def transposes(j):
                    pe.wait_ge(S["mgu_act"], G.at("mgu_act", evac[j]))
                    bank = 3 + j % 2
                    pe.wait_ge(*G.emptied(bank))
                    for q in range(2):
                        mm = pe.transpose(ps[bank][:, P * q:P * q + P], mact[:, 256 * j + P * q:256 * j + P * q + P],
                                          ident)
                    mm.then_inc(S["aT_psum"], 1)
                    tr[j] = G.filled(bank, "aT_sb")

                for j in range(11):
                    bank = j % 3
                    pe.wait_ge(*G.emptied(bank))
                    for kb in range(2):
                        s = [block_in(), block_in()]
                        if j == 0:
                            pe.wait_ge(S["xe"], G.at("xe", got - (1 - kb)))
                        for k4 in range(4):
                            k = 4 * kb + k4
                            if s[1] == s[0] + 1:
                                w = ring[:, s[0]:s[0] + 2, 256 * k4:256 * k4 + 256]
                                mm = pe.matmul(ps[bank][:, :], xe[:, k, :], w, start=(k == 0), stop=(k == KD - 1),
                                               skip_group_check=True)
                                if k4 == 0:
                                    pay(mm)
                                if k4 == 1:
                                    pay(mm)
                            else:
                                for u in range(2):
                                    w = ring[:, s[u], 256 * k4:256 * k4 + 256]
                                    mm = pe.matmul(ps[bank][:, 256 * u:256 * u + 256], xe[:, k, :], w,
                                                   start=(k == 0 and u == 0), stop=(k == KD - 1),
                                                   skip_group_check=True)
                                    if k4 == 0:
                                        pay(mm)
                        if kb == 0:
                            release(mm)
                            release_next()
                    mm.then_inc(S["mgu_psum"], 1)
                    evac[j] = G.filled(bank, "mgu_act")
                    release_next()
                    release_next()
                    if j >= 2:
                        transposes(j - 2)
                transposes(9)
                transposes(10)
                pe.wait_ge(*G.emptied(5))
                pe.wait_ge(*G.emptied(0))
                for f in range(FC):
                    s = block_in()
                    if f % 2 == 0:
                        pe.wait_ge(S["aT_sb"], G.at("aT_sb", tr[f // 2]))
                    for n, bank in enumerate((5, 0)):
                        mm = pe.matmul(ps[bank][:, :], mactT[:, f, :], ring[:, s, 512 * n:512 * n + 512],
                                       start=(f == 0), stop=(f == FC - 1))
                        if f == FC - 1:
                            mm.then_inc(S["y2_psum"], 1)
                            got = G.filled(bank, "y2")
                        elif n == 0:
                            pay(mm)
                    if f < FC - 1:
                        release(mm)
                release_next()
                for g in range(4):
                    bank = 1 + g % 2 if g < 2 else 6 + g % 2
                    pe.wait_ge(S["y2"], G.at("y2", got - (1 if g < 2 else 0)))
                    pe.wait_ge(*G.emptied(bank))
                    for q in range(2):
                        m = 2 * g + q
                        mm = pe.matmul(ps[bank][:, STREAM * q:STREAM * q + STREAM], y2[:, P * m:P * m + P],
                                       sm[:, e, :], start=True, stop=True)
                        if q == 0:
                            pay(mm)
                    mm.then_inc(S["sc_psum"], 1)
                    G.filled(bank, "h_ffn")

            def experts():
                slot_tables()
                G.begin()
                expert(0)
                after = count[0]
                with pe.Fori(1, EXPERTS) as e:
                    G.repeat(e)
                    count[0] = after - 66
                    expert(e)
                G.end(EXPERTS)
                count[0] = after + 66 * (EXPERTS - 1)

            pe.wait_ge(S["params_in"], 16)
            pe.wait_ge(S["cond"], G.next("cond"))
            for layer in range(LAYERS):
                modulation(layer)
                sum_over_features(0, TOK)
                projections(layer)
                attention(layer)
                gdn_prepare(layer)
                gdn(layer)
                gla(layer)
                closing(layer)
                out_projection(layer)
                sum_over_features(*h_range(layer))
                if layer == 0:
                    dense_ffn()
            routing()
            experts()
            pe.wait_ge(S["flag"], 1)
            over = pe.value_load(flag[0:1, 0:1], min_val=0, max_val=1)
            with pe.If(over > 0):
                experts()

        @block.scalar
        def _(sc):
            G = Counts(S)
            act_ = sc.activation

            def modulation(layer):
                for i in range(MOD_BLOCKS):
                    sc.wait_ge(S["mod_psum"], G.next("mod_psum"))
                    sc.copy(mrow[:, i % 2, :], ps[7][0:2, :]).then_inc(S["mod_row"], G.up("mod_row"))

            def norm(t0, t1, source):
                for k in range(KD):
                    if source:
                        sc.wait_ge(S[source], G.next(source))
                    act_(nsq[:, k, t0:t1], hT[:, k, t0:t1], ACT.Square).then_inc(S["sq"], G.up("sq"))
                sc.wait_ge(S["sumsq_psum"], G.next("sumsq_psum"))
                act_(ps[5][:, 0:t1 - t0], ps[5][:, 0:t1 - t0], ACT.Ln, bias=eps, scale=1.0 / D).then_inc(S["act_step"], G.up("act_step"))
                sc.wait_ge(S["act_step"], G.now("act_step"))
                act_(rstd_buf(t1 - t0), ps[5][:, 0:t1 - t0], ACT.Exp, scale=-0.5).then_inc(S["rstd"], G.up("rstd"))

            def projections(layer):
                for n, (name, _, by_token) in enumerate(IN_BLOCKS):
                    sc.wait_ge(S["proja_psum"], G.next("proja_psum"))
                    if name in ("gdn0",):
                        sc.wait_ge(S["cin_zero"], G.next("cin_zero"))
                    sc.copy(proj_dst(name, 1), proj_src(name, 5 + n % 2)).then_inc(S["proja"], G.up("proja"))
                    if n == 5:
                        sc.wait_ge(S["proja_psum"], G.next("proja_psum"))
                        sc.copy(glow, ps[7][0:32, :]).then_inc(S["proja"], G.up("proja"))

            def attention(layer):
                base = G.seen("att_normed")
                pd = 12 * layer
                sc.wait_ge(S["projd"], G.at("projd", pd + 3))
                sc.wait_ge(S["proja"], G.now("proja"))
                for i in range(TILES):
                    act_(asq[:, i, :, :], att[:, i, 0:10, :], ACT.Square).then_inc(S["att_sq"], G.up("att_sq"))
                sc.wait_ge(S["att_ss"], G.next("att_ss"))
                act_(ssq[:, :, :], ssq[:, :, :], ACT.Ln, bias=eps, scale=1.0 / HD).then_inc(S["act_step"], G.up("act_step"))
                sc.wait_ge(S["act_step"], G.now("act_step"))
                act_(ssq[:, :, :], ssq[:, :, :], ACT.Exp, scale=-0.5).then_inc(S["att_rstd"], G.up("att_rstd"))
                sc.wait_ge(S["kz_zero"], G.next("kz_zero"))
                for i in range(TILES):
                    sc.wait_ge(S["kT_psum"], G.next("kT_psum"))
                    t = slice(P * i, P * i + P)
                    sc.copy(akz[0:HD, 0, t], ps[4][0:HD, 0:P])
                    sc.copy(akz[HD:P, 1, t], ps[4][HD:P, 0:P]).then_inc(S["kz"], G.up("kz"))
                units = att_units(layer)
                for i in range(len(units) + 1):
                    if i < len(units):
                        nk = units[i][2]
                        sc.wait_ge(S["smax"], G.next("smax"))
                        act_(Pb[:, i % 3, 0:P * nk], ps[i % 2][:, 0:P * nk], ACT.Exp, bias=nmx[:, i:i + 1],
                                   scale=HD ** -0.5, accum_out=rsum[:, i:i + 1]).then_inc(S["att_exp"], G.up("att_exp"))
                    if i >= 1:
                        nk = units[i - 1][2]
                        sc.wait_ge(S["pT_psum"], G.next("pT_psum"))
                        sc.copy(PTb[:, (i - 1) % 2, 0:nk, :],
                                      ps[2 + (i - 1) % 2][:, 0:P * nk].rearrange("p (a b) -> p a b", a=nk)).then_inc(S["pT"], G.up("pT"))

            def gdn_prepare(layer):
                sc.wait_ge(S["gx"], G.next("gx"))
                x_, l_ = gsm[:, 0, :, :], gsm[:, 1, :, :]
                act_(l_, x_, ACT.Abs).then_inc(S["act_step"], G.up("act_step"))
                sc.wait_ge(S["act_step"], G.now("act_step"))
                act_(l_, l_, ACT.Exp, scale=-1.0).then_inc(S["act_step"], G.up("act_step"))
                sc.wait_ge(S["act_step"], G.now("act_step"))
                act_(l_, l_, ACT.Ln, bias=one)
                act_(gsm[:, 2, 0, :], pr("alog", 8, 8 * layer), ACT.Exp)
                act_(gsm[:, 3, :, :], ab[:, :, 8:16], ACT.Exp, scale=-1.0).then_inc(S["g_act"], G.up("g_act"))
                for c in range(6):
                    sc.wait_ge(S["conv"], G.next("conv"))
                    act_(ce[:, c, :, :], cv[:, c, :, :], ACT.Exp, scale=-1.0).then_inc(S["conv_exp"], G.up("conv_exp"))
                for n, c in enumerate((2, 3, 0, 1)):
                    sc.wait_ge(S["qk_ss_psum"], G.next("qk_ss_psum"))
                    act_(crn[:, c, :], ps[n % 2][:, :], ACT.Ln, bias=eps).then_inc(S["act_step"], G.up("act_step"))
                    sc.wait_ge(S["act_step"], G.now("act_step"))
                    act_(crn[:, c, :], crn[:, c, :], ACT.Exp, scale=-0.5).then_inc(S["qk_rn"], G.up("qk_rn"))
                sc.wait_ge(S["gscan_psum"], G.next("gscan_psum"))
                act_(eg[:, :, :, :].rearrange("p a b c -> p (a b c)"), ps[4][:, 0:64], ACT.Exp).then_inc(S["eg"], G.up("eg"))
                for tile in range(TILES):
                    sc.wait_ge(S["kvT_psum"], G.next("kvT_psum"))
                    sc.copy(kvtok[:, tile, :], ps[2 + tile % 2][:, :]).then_inc(S["kvtok"], G.up("kvtok"))

            def gdn(layer):
                misc = [0]
                for kind, d, i, k in gdn_order():
                    pt, xv, xk, kd_, qg_ = slot(d, i)
                    if kind == "decay":
                        sc.wait_ge(S["dec_psum"], G.next("dec_psum"))
                        act_(E[d].rearrange("p a b -> p (a b)"), ps[4 + d][:, :], ACT.Exp).then_inc(S["decE"], G.up("decE"))
                        sc.wait_ge(S["dec_psum"], G.next("dec_psum"))
                        act_(Y[d].rearrange("p a b -> p (a b)"), ps[2 + d][:, :], ACT.Exp).then_inc(S["decB"], G.up("decB"))
                    elif kind == "X":
                        sc.wait_ge(S["x_psum"], G.next("x_psum"))
                        sc.copy(xv, ps[d][:, 0:256]).then_inc(S["x_out"], G.up("x_out"))
                        sc.wait_ge(S["x_psum"], G.next("x_psum"))
                        sc.copy(xk.rearrange("p a b -> p (a b)"), ps[2 + d][:, 0:256]).then_inc(S["x_out"], G.up("x_out"))
                    elif kind == "ru":
                        misc[0] += 1
                    elif kind == "ro":
                        misc[0] += 1
                        bank = 6 + misc[0] % 2
                        misc[0] += 1
                        c = k if d == 0 else 1 - k
                        t0 = P * TILE_ORDER[d][i] + CHUNK * c
                        sc.wait_ge(S["ro_psum"], G.next("ro_psum"))
                        sc.copy(og[:, d, :, t0:t0 + CHUNK],
                                      ps[bank][:, 0:P].rearrange("p (a b) -> p a b", a=2)).then_inc(S["gdn_o"], G.up("gdn_o"))

            def gla(layer):
                for n in range(4):
                    d, ch = n // 2, n % 2
                    w = gw_[:, n % 2]
                    l_ = gw_[:, n % 2, 1, :]
                    sc.wait_ge(S["gate_x"], G.next("gate_x"))
                    act_(l_, w[:, 0, :], ACT.Abs).then_inc(S["act_step"], G.up("act_step"))
                    sc.wait_ge(S["act_step"], G.now("act_step"))
                    act_(l_, l_, ACT.Exp, scale=-1.0).then_inc(S["act_step"], G.up("act_step"))
                    sc.wait_ge(S["act_step"], G.now("act_step"))
                    act_(l_, l_, ACT.Ln, bias=one).then_inc(S["gate_ln"], G.up("gate_ln"))
                    sc.wait_ge(S["gate_D"], G.next("gate_D"))
                    act_(w[:, 2, :], w[:, 3, :], ACT.Exp, scale=1.0)
                    act_(w[:, 1, :], w[:, 3, :], ACT.Exp, scale=-1.0).then_inc(S["gate_E"], G.up("gate_E"))
                sc.wait_ge(S["gate_f"], G.next("gate_f"))
                act_(gfac[:, 2:4, :, :, :].rearrange("p a b c d -> p (a b c d)"),
                           gfac[:, 0:2, :, :, :].rearrange("p a b c d -> p (a b c d)"), ACT.Exp).then_inc(S["gate_fe"], G.up("gate_fe"))
                for d in range(2):
                    for hf in range(2):
                        sc.wait_ge(S["ktr_psum"], G.next("ktr_psum"))
                        sc.copy(kt[:, d, 2 * hf:2 * hf + 2, :],
                                      ps[4 + hf][:, :].rearrange("p (a b) -> p a b", a=2)).then_inc(S["ktok"], G.up("ktok"))
                n = 0
                for k in range(CHUNKS):
                    for d in range(2):
                        t0 = CHUNK * CHUNK_ORDER[d][k]
                        sc.wait_ge(S["go_psum"], G.next("go_psum"))
                        sc.copy(ol[:, d, :, t0:t0 + CHUNK],
                                      ps[4 + n % 4][:, 0:P].rearrange("p (a b) -> p a b", a=2)).then_inc(S["gla_o"], G.up("gla_o"))
                        n += 1

            def closing(layer):
                t0, t1 = h_range(layer)
                for m in range(4):
                    src = gr_ if m < 2 else gz
                    act_(fsg[:, m, t0:t1], src[:, m % 2, t0:t1], ACT.Exp, scale=-1.0).then_inc(S["fin_e"], G.up("fin_e"))
                for m in range(4):
                    sc.wait_ge(S["fin_psum"], G.next("fin_psum"))
                    act_(frs[:, m, t0:t1], ps[m][:, 0:t1 - t0], ACT.Ln, bias=eps, scale=1.0 / HD).then_inc(S["act_step"], G.up("act_step"))
                    sc.wait_ge(S["act_step"], G.now("act_step"))
                    act_(frs[:, m, t0:t1], frs[:, m, t0:t1], ACT.Exp, scale=-0.5).then_inc(S["fin_rs"], G.up("fin_rs"))

            def dense_ffn():
                act0 = G.seen("gu_act")
                for j in range(11):
                    sc.wait_ge(S["gu_psum"], G.next("gu_psum"))
                    if j > 1:
                        sc.wait_ge(S["gu_act"], G.at("gu_act", act0 + 2 * (j - 1)))
                    for x in range(2):
                        m = act_(fe[:, 2 * (j % 2) + x, :], ps[4 * (j % 2) + x][:, :], ACT.Exp, scale=-1.0)
                    m.then_inc(S["gu_exp"], G.up("gu_exp"))
                    sc.wait_ge(S["gu_psum"], G.next("gu_psum"))
                G.n["gu_act"] = act0 + 22

            def routing():
                for n in range(4):
                    tile, hf = n // 2, n % 2
                    sc.wait_ge(S["bT_psum"], G.next("bT_psum"))
                    sc.copy(btok[:, tile, 512 * hf:512 * hf + 512], ps[1 + n][:, :]).then_inc(S["btok"], G.up("btok"))
                sc.wait_ge(S["top"], G.next("top"))
                act_(rtop[:, :, 4, 0:1], rtop[:, :, 4, 1:2], ACT.Exp).then_inc(S["top_e"], G.up("top_e"))

            def slot_tables():
                for n in range(4):
                    sc.wait_ge(S["gT_psum"], G.next("gT_psum"))
                    sc.copy(sm[:, 2 * n:2 * n + 2, :], ps[1 + n][:, :].rearrange("p (a b) -> p a b", a=2)).then_inc(S["smat"], G.up("smat"))

            def expert(e):
                for hf in range(2):
                    sc.wait_ge(S["xe_psum"], G.next("xe_psum"))
                    sc.copy(xe[:, 4 * hf:4 * hf + 4, :], ps[6 + hf][:, :].rearrange("p (a b) -> p a b", a=4)).then_inc(S["xe"], G.up("xe"))

                def copy_T(j):
                    sc.wait_ge(S["aT_psum"], G.next("aT_psum"))
                    sc.copy(mactT[:, 2 * j:2 * j + 2, :],
                                  ps[3 + j % 2][:, 0:256].rearrange("p (a b) -> p a b", a=2)).then_inc(S["aT_sb"], G.up("aT_sb"))

                for j in range(11):
                    sc.wait_ge(S["mgu_psum"], G.next("mgu_psum"))
                    if G.turn is not None or G.seen("mgu_act") > 1:
                        sc.wait_ge(S["mgu_act"], G.at("mgu_act", G.seen("mgu_act") - 1))
                    G.n["mgu_act"] = G.seen("mgu_act") + 1
                    act_(me[:, j % 2, :], ps[j % 3][:, 0:256], ACT.Exp, scale=-1.0).then_inc(S["mgu_exp"], G.up("mgu_exp"))
                    if j >= 3:
                        copy_T(j - 3)
                for j in (8, 9, 10):
                    copy_T(j)
                for n, bank in enumerate((5, 0)):
                    sc.wait_ge(S["y2_psum"], G.next("y2_psum"))
                    sc.copy(y2[:, 512 * n:512 * n + 512], ps[bank][:, :]).then_inc(S["y2"], G.up("y2"))

            def experts():
                slot_tables()
                G.begin()
                expert(0)
                with sc.Fori(1, EXPERTS) as e:
                    G.repeat(e)
                    expert(e)
                G.end(EXPERTS)

            sc.wait_ge(S["params_in"], 16)
            act_(cond[:, :, :].rearrange("p a b -> p (a b)"), pr("cond"), ACT.Exp, scale=-1.0).then_inc(S["cond_exp"], G.up("cond_exp"))
            sc.wait_ge(S["x_in"], 16)
            for layer in range(LAYERS):
                modulation(layer)
                norm(0, TOK, "h_ffn" if layer else None)
                projections(layer)
                attention(layer)
                gdn_prepare(layer)
                gdn(layer)
                gla(layer)
                closing(layer)
                norm(*h_range(layer), "h_mix")
                if layer == 0:
                    dense_ffn()
            routing()
            experts()
            sc.wait_ge(S["flag"], 1)
            over = sc.value_load(flag[0:1, 0:1], min_val=0, max_val=1)
            with sc.If(over > 0):
                experts()

        @block.vector
        def _(v):
            G = Counts(S)
            tt, ts, stt, cp = v.tensor_tensor, v.tensor_scalar, v.scalar_tensor_tensor, v.tensor_copy

            def modulation(layer):
                v.wait_ge(S["modT_psum"], G.next("modT_psum"))
                bm = rep(pr("bmod", 48, 48 * layer), 2, 2)
                tt(mcol[:, :, :], ps[0][:, 0:96].rearrange("p (a b) -> p a b", a=48), bm, ALU.add).then_inc(S["dve_step"], G.up("dve_step"))
                v.wait_ge(S["dve_step"], G.now("dve_step"))
                for w in range(2):
                    gain = rep(pr("norms", 8, 16 * layer + 8 * w), 2, 2)
                    m = stt(coef[:, w, :, :], mcol[:, 24 * w + 8:24 * w + 16, :], 1.0, gain, ALU.add, ALU.mult)
                m.then_inc(S["mod"], G.up("mod"))
                v.wait_ge(S["mod"], G.now("mod"))

            def norm(layer, which, t0, t1):
                v.wait_ge(S["rstd"], G.next("rstd"))
                for k in range(KD):
                    tt(nhn[:, k, t0:t1], hT[:, k, t0:t1], rstd_buf(t1 - t0), ALU.mult).then_inc(S["dve_step"], G.up("dve_step"))
                    v.wait_ge(S["dve_step"], G.now("dve_step"))
                    for s0 in range(t0, t1, STREAM):
                        st = 1 if s0 == 0 else 0
                        m = ts(aT[:, k, s0:s0 + STREAM], nhn[:, k, s0:s0 + STREAM], coef[:, which, k, st:st + 1],
                               mcol[:, 24 * which + k, st:st + 1], ALU.mult, ALU.add)
                    m.then_inc(S["a"], G.up("a"))

            def projections(layer):
                for n, (name, _, by_token) in enumerate(IN_BLOCKS):
                    v.wait_ge(S["projd_psum"], G.next("projd_psum"))
                    if name == "gdn0":
                        v.wait_ge(S["cin_zero"], G.next("cin_zero"))
                    cp(proj_dst(name, 0), proj_src(name, n % 2)).then_inc(S["projd"], G.up("projd"))
                    if n == 5:
                        v.wait_ge(S["projd_psum"], G.next("projd_psum"))
                        cp(ab[:, :, :].rearrange("p a b -> p (a b)"), ps[4][:, 0:64]).then_inc(S["projd"], G.up("projd"))

            def attention(layer):
                for i in range(TILES):
                    v.wait_ge(S["att_sq"], G.next("att_sq"))
                    m = v.tensor_reduce(ssq[:, i, :], asq[:, i, :, :], AX, ALU.add)
                m.then_inc(S["att_ss"], G.up("att_ss"))
                v.wait_ge(S["att_rstd"], G.next("att_rstd"))
                for i in range(TILES):
                    tt(att[:, i, 0:10, :], att[:, i, 0:10, :], rep(ssq[:, i, :], 2, HD), ALU.mult).then_inc(S["att_normed"], G.up("att_normed"))
                for i in range(TILES):
                    if layer == 0 or i >= 2:
                        v.wait_ge(S["qT_psum"], G.next("qT_psum"))
                        cp(qT[:, :, P * i:P * i + P], ps[2 + i % 2][:, :].rearrange("p (a b) -> p a b", a=4)).then_inc(S["qT"], G.up("qT"))
                units = att_units(layer)
                for i in range(len(units) + 3):
                    if i < len(units):
                        nk = units[i][2]
                        v.wait_ge(S["scores_psum"], G.next("scores_psum"))
                        v.tensor_reduce(nmx[:, i:i + 1], ps[i % 2][:, 0:P * nk], AX, ALU.max, negate=True).then_inc(S["dve_step"], G.up("dve_step"))
                        v.wait_ge(S["dve_step"], G.now("dve_step"))
                        ts(nmx[:, i:i + 1], nmx[:, i:i + 1], HD ** -0.5, None, ALU.mult).then_inc(S["smax"], G.up("smax"))
                    if 1 <= i <= len(units):
                        j = i - 1
                        nk = units[j][2]
                        v.wait_ge(S["att_exp"], G.next("att_exp"))
                        v.reciprocal(rsum[:, j:j + 1], rsum[:, j:j + 1]).then_inc(S["dve_step"], G.up("dve_step"))
                        v.wait_ge(S["dve_step"], G.now("dve_step"))
                        ts(Pb[:, j % 3, 0:P * nk], Pb[:, j % 3, 0:P * nk], rsum[:, j:j + 1], None, ALU.mult).then_inc(S["att_p"], G.up("att_p"))
                    if i >= 3 and (i - 3) % 4 == 3:
                        _, _, _, g, pair, lat, _ = units[i - 3]
                        v.wait_ge(S["pv_psum"], G.next("pv_psum"))
                        cp(aT[:, 4 + pair, STREAM * lat:STREAM * lat + STREAM], ps[4 + g % 2][:, 0:STREAM]).then_inc(S["att_out"], G.up("att_out"))

            def gdn_prepare(layer):
                x_, l_ = gsm[:, 0, :, :], gsm[:, 1, :, :]
                v.wait_ge(S["projd"], G.now("projd"))
                tt(x_, ab[:, :, 0:8], rep(pr("dtb", 8, 8 * layer), 1, TILES), ALU.add).then_inc(S["gx"], G.up("gx"))
                base = 12 * layer
                v.wait_ge(S["proja"], G.at("proja", base + 6))
                for c in range(6):
                    def tap(j):
                        return pr("conv", 1, 30 * layer + 5 * c + j)
                    ts(cv[:, c, :, :], cin[:, c, :, 0:256], tap(0), None, ALU.mult).then_inc(S["dve_step"], G.up("dve_step"))
                    v.wait_ge(S["dve_step"], G.now("dve_step"))
                    for j in range(1, 5):
                        m = stt(cv[:, c, :, :], cin[:, c, :, j:j + 256], tap(j), cv[:, c, :, :], ALU.mult, ALU.add)
                        if j < 4:
                            m.then_inc(S["dve_step"], G.up("dve_step"))
                            v.wait_ge(S["dve_step"], G.now("dve_step"))
                    m.then_inc(S["conv"], G.up("conv"))
                v.wait_ge(S["g_act"], G.next("g_act"))
                m = gsm[:, 5, :, :]
                ts(x_, x_, 0.0, None, ALU.max).then_inc(S["dve_step"], G.up("dve_step"))
                v.wait_ge(S["dve_step"], G.now("dve_step"))
                tt(x_, x_, l_, ALU.add).then_inc(S["dve_step"], G.up("dve_step"))
                v.wait_ge(S["dve_step"], G.now("dve_step"))
                stt(gsm[:, 4, :, :], x_, -1.0, rep(gsm[:, 2, 0, :], 1, TILES), ALU.mult, ALU.mult)
                ts(gsm[:, 3, :, :], gsm[:, 3, :, :], 1.0, None, ALU.add).then_inc(S["dve_step"], G.up("dve_step"))
                v.wait_ge(S["dve_step"], G.now("dve_step"))
                v.reciprocal(m, gsm[:, 3, :, :]).then_inc(S["g"], G.up("g"))
                for c in range(6):
                    v.wait_ge(S["conv_exp1"], G.next("conv_exp1"))
                    v.reciprocal(ce[:, c, :, :], ce[:, c, :, :]).then_inc(S["conv_rec"], G.up("conv_rec"))
                for n, c in enumerate((2, 3, 0, 1)):
                    v.wait_ge(S["qk_rn"], G.next("qk_rn"))
                    src = cv[:, c, :, :].rearrange("p a b -> p (a b)")
                    if c >= 2:
                        m = tt(kq[:, 0, c - 2, :], src, crn[:, c, :], ALU.mult)
                    else:
                        m = stt(kq[:, 1, c, :], src, HD ** -0.5, crn[:, c, :], ALU.mult, ALU.mult)
                    m.then_inc(S["kq"], G.up("kq"))

            def gdn(layer):
                misc = [0]
                v.memset(state[:, :, :, :], 0.0).then_inc(S["dve_step"], G.up("dve_step"))
                v.wait_ge(S["dve_step"], G.now("dve_step"))
                qg_n = {}
                for kind, d, i, k in gdn_order():
                    pt, xv, xk, kd_, qg_ = slot(d, i)
                    if kind == "kk":
                        v.wait_ge(S["dtb"], G.next("dtb"))
                        for pair in range(2):
                            bank = (d, 4 + d)[pair]
                            v.wait_ge(S["kk_psum"], G.next("kk_psum"))
                            src = ps[bank][:, :].rearrange("p (h w t) -> p h w t", h=2, w=2)
                            h = slice(2 * pair, 2 * pair + 2)
                            tt(AT[d][:, h, :], src[:, :, 0, :], E[d][:, h, :], ALU.mult)
                            tt(pt[:, h, :], src[:, :, 1, :], E[d][:, h, :], ALU.mult).then_inc(S["kk_out"], G.up("kk_out"))
                    elif kind == "first":
                        v.wait_ge(S["kk_out"], G.now("kk_out"))
                        stt(U[d], AT[d], -1.0, rep(level_mask(1 - d, 1), 1, 4), ALU.mult, ALU.mult).then_inc(S["dve_step"], G.up("dve_step"))
                        v.wait_ge(S["dve_step"], G.now("dve_step"))
                        tt(U[d], U[d], rep(ident, 1, 4), ALU.add).then_inc(S["dve_step"], G.up("dve_step"))
                        v.wait_ge(S["dve_step"], G.now("dve_step"))
                        v.wait_ge(S["y_psum"], G.next("y_psum"))
                        stt(T[d], ps[d][:, :].rearrange("p (a b) -> p a b", a=4), -1.0,
                                   rep(level_mask(d, 1), 1, 4), ALU.mult, ALU.mult).then_inc(S["dve_step"], G.up("dve_step"))
                        v.wait_ge(S["dve_step"], G.now("dve_step"))
                        tt(T[d], T[d], rep(ident, 1, 4), ALU.add).then_inc(S["tu"], G.up("tu"))
                    elif kind == "Y":
                        if k == 2:
                            v.wait_ge(S["qg"], G.next("qg"))
                        v.wait_ge(S["y_psum"], G.next("y_psum"))
                        tt(Y[d], ps[d][:, :].rearrange("p (a b) -> p a b", a=4),
                                 rep(level_mask(d, k), 1, 4), ALU.mult).then_inc(S["ym"], G.up("ym"))
                    elif kind == "dTU":
                        v.wait_ge(S["dtu_psum"], G.next("dtu_psum"))
                        v.wait_ge(S["tu"], G.now("tu"))
                        if k < LEVELS:
                            tt(T[d], T[d], ps[2 + d][:, :].rearrange("p (a b) -> p a b", a=4), ALU.subtract)
                        tt(U[d], U[d], ps[4 + d][:, :].rearrange("p (a b) -> p a b", a=4), ALU.subtract).then_inc(S["tu"], G.up("tu"))
                    elif kind == "ru":
                        misc[0] += 1
                        bank = 6 + misc[0] % 2
                        c = k if d == 0 else 1 - k
                        r = slice(CHUNK * c, CHUNK * c + CHUNK)
                        if k == 0:
                            v.wait_ge(S["x_out"], G.next("x_out", 2))
                        v.wait_ge(S["ru_psum"], G.next("ru_psum"))
                        tt(ubuf[r, d, :], xv[r, :], ps[bank][r, 0:256], ALU.subtract).then_inc(S["gdn_u"], G.up("gdn_u"))
                    elif kind == "ro":
                        misc[0] += 2
                        bank = 6 + misc[0] % 2
                        c = k if d == 0 else 1 - k
                        if (i, k) != (0, 0):
                            v.wait_ge(S["gdn_s"], G.now("gdn_s"))
                        v.wait_ge(S["rw_psum"], G.next("rw_psum"))
                        for h in range(4):
                            half = slice(HD * (h % 2), HD * (h % 2) + HD)
                            m = stt(state[half, d, h // 2, half], state[half, d, h // 2, half],
                                    eend[half, d, i % 2, h, c:c + 1],
                                    ps[bank][half, P * (h // 2) + HD * (h % 2):P * (h // 2) + HD * (h % 2) + HD],
                                    ALU.mult, ALU.add)
                        m.then_inc(S["gdn_s"], G.up("gdn_s"))

            def gla(layer):
                v.wait_ge(S["gdn_s"], G.now("gdn_s"))
                v.memset(state[:, :, :, :], 0.0).then_inc(S["dve_step"], G.up("dve_step"))
                v.wait_ge(S["dve_step"], G.now("dve_step"))
                for n in range(4):
                    d, ch = n // 2, n % 2
                    w = gw_[:, n % 2]
                    x_, l_, f_, d_ = (w[:, q, :] for q in range(4))
                    v.wait_ge(S["gate_psum"], G.next("gate_psum"))
                    ts(x_, ps[n][:, :], pr("gate_bias", 1, 4 * layer + 2 * d + ch), None, ALU.add).then_inc(S["gate_x"], G.up("gate_x"))
                    v.wait_ge(S["gate_x"], G.now("gate_x"))
                    ts(f_, x_, 0.0, 1.0 / 16.0, ALU.min, ALU.mult).then_inc(S["dve_step"], G.up("dve_step"))
                    v.wait_ge(S["dve_step"], G.now("dve_step"))
                    v.wait_ge(S["gate_ln"], G.next("gate_ln"))
                    stt(x_, l_, -1.0 / 16.0, f_, ALU.mult, ALU.add).then_inc(S["dve_step"], G.up("dve_step"))
                    v.wait_ge(S["dve_step"], G.now("dve_step"))
                    v.tensor_tensor_scan(f_, pr("scanmask"), x_, 0.0, ALU.mult, ALU.add).then_inc(S["dve_step"], G.up("dve_step"))
                    v.wait_ge(S["dve_step"], G.now("dve_step"))
                    fc = f_.rearrange("p (c t) -> p c t", c=CHUNKS)
                    if d == 0:
                        mid = fc[:, :, 31]
                        cp(gfac[:, 0, d, ch, :], mid)
                        tt(gfac[:, 1, d, ch, :], fc[:, :, 63], mid, ALU.subtract).then_inc(S["dve_step"], G.up("dve_step"))
                        v.wait_ge(S["dve_step"], G.now("dve_step"))
                        src = fc
                    else:
                        tt(x_, f_, x_, ALU.subtract).then_inc(S["dve_step"], G.up("dve_step"))
                        v.wait_ge(S["dve_step"], G.now("dve_step"))
                        src = x_.rearrange("p (c t) -> p c t", c=CHUNKS)
                        mid = src[:, :, 32]
                        tt(gfac[:, 0, d, ch, :], fc[:, :, 63], mid, ALU.subtract)
                        cp(gfac[:, 1, d, ch, :], mid).then_inc(S["dve_step"], G.up("dve_step"))
                        v.wait_ge(S["dve_step"], G.now("dve_step"))
                    dc = d_.rearrange("p (c t) -> p c t", c=CHUNKS)
                    tt(dc, src, rep(mid, 2, CHUNK), ALU.subtract).then_inc(S["dve_step"], G.up("dve_step"))
                    v.wait_ge(S["dve_step"], G.now("dve_step"))
                    ts(d_, d_, 80.0, -80.0, ALU.min, ALU.max).then_inc(S["gate_D"], G.up("gate_D"))
                    v.wait_ge(S["gate_E"], G.next("gate_E"))
                    eq, ek = (w[:, 2, :], w[:, 1, :]) if d == 0 else (w[:, 1, :], w[:, 2, :])
                    stt(qp[:, d, ch, :], gq[:, ch, :], HD ** -0.5, eq, ALU.mult, ALU.mult)
                    for p_ in range(2):
                        half = slice(HD * p_, HD * p_ + HD)
                        m = stt(qz[half, d, ch, p_, :], gq[half, ch, :], HD ** -0.5, eq[half, :],
                                ALU.mult, ALU.mult)
                        other = slice(HD - HD * p_, 2 * HD - HD * p_)
                        v.memset(qz[other, d, ch, p_, :], 0.0)
                    tt(kp[:, d, ch, :], gk[:, ch, :], ek, ALU.mult).then_inc(S["gate_k"], G.up("gate_k"))
                    v.memset(nmx[0:1, 33:34], 0.0).then_inc(S["gate_q"], G.up("gate_q"))
                tt(gfac[:, 1, 0, :, 0:7], gfac[:, 1, 0, :, 0:7], gfac[:, 0, 0, :, 1:8], ALU.add).then_inc(S["dve_step"], G.up("dve_step"))
                v.wait_ge(S["dve_step"], G.now("dve_step"))
                for a, b, n in ((1, 0, 3), (5, 4, 3), (0, 7, 1)):
                    tt(gfac[:, 1, 1, :, a:a + n], gfac[:, 1, 1, :, a:a + n], gfac[:, 0, 1, :, b:b + n], ALU.add)
                v.memset(nmx[0:1, 33:34], 0.0).then_inc(S["gate_f"], G.up("gate_f"))
                v.wait_ge(S["gate_fe"], G.next("gate_fe"))
                v.memset(nmx[0:1, 33:34], 0.0).then_inc(S["gate_c"], G.up("gate_c"))
                for d in range(2):
                    for hf in range(2):
                        v.wait_ge(S["gs_psum"], G.next("gs_psum"))
                        tt(pg[:, d, 2 * hf:2 * hf + 2, :, :].rearrange("p a b c -> p (a b) c"),
                                 ps[6 + hf][:, :].rearrange("p (a b) -> p a b", a=8),
                                 rep(maskc[d], 1, 8), ALU.mult).then_inc(S["gla_pt"], G.up("gla_pt"))
                n = 0
                for k in range(CHUNKS):
                    for d in range(2):
                        g = CHUNK_ORDER[d][k]
                        bank = n % 4
                        v.wait_ge(S["gw_psum"], G.next("gw_psum"))
                        v.wait_ge(S["go_psum"], G.next("go_psum"))
                        for p_ in range(2):
                            half = slice(HD * p_, HD * p_ + HD)
                            m = tt(state[half, d, :, half], state[half, d, :, half],
                                   ps[bank][half, 0:256].rearrange("p (a b) -> p a b", a=2)[:, :, half], ALU.add)
                        m.then_inc(S["dve_step"], G.up("dve_step"))
                        v.wait_ge(S["dve_step"], G.now("dve_step"))
                        for pair in range(2):
                            m = ts(state[:, d, pair, :], state[:, d, pair, :], gfac[:, 3, d, pair, g:g + 1], None,
                                   ALU.mult)
                        m.then_inc(S["gla_s"], G.up("gla_s"))
                        v.wait_ge(S["gla_s"], G.now("gla_s"))
                        n += 1

            def closing(layer):
                t0, t1 = h_range(layer)
                for m_ in range(4):
                    v.wait_ge(S["fin_e1"], G.next("fin_e1"))
                    v.reciprocal(fsg[:, m_, t0:t1], fsg[:, m_, t0:t1]).then_inc(S["fin_rec"], G.up("fin_rec"))
                for m_ in range(4):
                    o = (ol if m_ < 2 else og)[:, 0, m_ % 2, t0:t1]
                    v.wait_ge(S["fin_rs"], G.next("fin_rs"))
                    stt(o, o, pr("gains", 1, 2 * layer + m_ // 2), frs[:, m_, t0:t1], ALU.mult, ALU.mult).then_inc(S["dve_step"], G.up("dve_step"))
                    v.wait_ge(S["dve_step"], G.now("dve_step"))
                    v.wait_ge(S["fin_sg"], G.next("fin_sg"))
                    tt(aT[:, m_, t0:t1], o, fsg[:, m_, t0:t1], ALU.mult).then_inc(S["mix"], G.up("mix"))

            def add_to_h(m_, which, t0, t1, psum):
                for s0 in range(t0, t1, STREAM):
                    st = 1 if s0 == 0 else 0
                    m = stt(hT[:, m_, s0:s0 + STREAM], psum[:, s0 - t0:s0 - t0 + STREAM],
                            mcol[:, 24 * which + 16 + m_, st:st + 1], hT[:, m_, s0:s0 + STREAM], ALU.mult, ALU.add)
                return m

            def out_projection(layer):
                t0, t1 = h_range(layer)
                for m_ in range(KD):
                    v.wait_ge(S["wout_psum"], G.next("wout_psum"))
                    add_to_h(m_, 0, t0, t1, ps[m_ % 4]).then_inc(S["h_mix"], G.up("h_mix"))
                v.wait_ge(S["h_mix"], G.now("h_mix"))

            def dense_ffn():
                for j in range(11):
                    v.wait_ge(S["gu_psum"], G.next("gu_psum", 2))
                    v.wait_ge(S["gu_exp"], G.next("gu_exp"))
                    b = 4 * (j % 2)
                    for x in range(2):
                        g = fe[:, 2 * (j % 2) + x, :]
                        ts(g, g, 1.0, None, ALU.add).then_inc(S["dve_step"], G.up("dve_step"))
                        v.wait_ge(S["dve_step"], G.now("dve_step"))
                        v.reciprocal(g, g).then_inc(S["dve_step"], G.up("dve_step"))
                        v.wait_ge(S["dve_step"], G.now("dve_step"))
                        tt(g, g, ps[b + x][:, :], ALU.mult).then_inc(S["dve_step"], G.up("dve_step"))
                        v.wait_ge(S["dve_step"], G.now("dve_step"))
                        tt(act[:, 2 * j + x, :], g, ps[b + 2 + x][:, :], ALU.mult).then_inc(S["gu_act"], G.up("gu_act"))
                for m_ in range(KD):
                    v.wait_ge(S["down_psum"], G.next("down_psum"))
                    add_to_h(m_, 1, 0, TOK, ps[m_]).then_inc(S["h_ffn"], G.up("h_ffn"))
                v.wait_ge(S["h_ffn"], G.now("h_ffn"))

            def routing():
                v.wait_ge(S["logit_psum"], G.next("logit_psum"))
                lg = rtop[:, :, 0, :]
                tt(lg, ps[0][:, 0:16].rearrange("p (a b) -> p a b", a=2), rep(pr("rbias"), 1, 2), ALU.add).then_inc(S["dve_step"], G.up("dve_step"))
                v.wait_ge(S["dve_step"], G.now("dve_step"))
                for tile in range(2):
                    v.max(rtop[:, tile, 1, :], rtop[:, tile, 0, :]).then_inc(S["dve_step"], G.up("dve_step"))
                    v.wait_ge(S["dve_step"], G.now("dve_step"))
                    v.max_index(idx[:, tile, :], rtop[:, tile, 1, :], rtop[:, tile, 0, :]).then_inc(S["dve_step"], G.up("dve_step"))
                    v.wait_ge(S["dve_step"], G.now("dve_step"))
                    cp(rtop[:, tile, 2, :], idx[:, tile, :]).then_inc(S["dve_step"], G.up("dve_step"))
                    v.wait_ge(S["dve_step"], G.now("dve_step"))
                tt(rtop[:, :, 4, 1:2], rtop[:, :, 1, 1:2], rtop[:, :, 1, 0:1], ALU.subtract).then_inc(S["dve_step"], G.up("dve_step"))
                v.wait_ge(S["dve_step"], G.now("dve_step"))
                v.memset(nmx[0:1, 33:34], 0.0).then_inc(S["top"], G.up("top"))
                v.wait_ge(S["top_e"], G.next("top_e"))
                ts(rtop[:, :, 4, 2:3], rtop[:, :, 4, 0:1], 1.0, None, ALU.add).then_inc(S["dve_step"], G.up("dve_step"))
                v.wait_ge(S["dve_step"], G.now("dve_step"))
                v.reciprocal(rtop[:, :, 4, 3:4], rtop[:, :, 4, 2:3]).then_inc(S["dve_step"], G.up("dve_step"))
                v.wait_ge(S["dve_step"], G.now("dve_step"))
                tt(rtop[:, :, 4, 4:5], rtop[:, :, 4, 3:4], rtop[:, :, 4, 0:1], ALU.mult).then_inc(S["dve_step"], G.up("dve_step"))
                v.wait_ge(S["dve_step"], G.now("dve_step"))
                for tile in range(2):
                    i8 = pr("iota8")
                    o1, o2 = rtop[:, tile, 0, :], rtop[:, tile, 1, :]
                    ts(o1, i8, rtop[:, tile, 2, 0:1], None, ALU.is_equal).then_inc(S["dve_step"], G.up("dve_step"))
                    v.wait_ge(S["dve_step"], G.now("dve_step"))
                    ts(o2, i8, rtop[:, tile, 2, 1:2], None, ALU.is_equal).then_inc(S["dve_step"], G.up("dve_step"))
                    v.wait_ge(S["dve_step"], G.now("dve_step"))
                    tt(rtop[:, tile, 3, :], o1, o2, ALU.add).then_inc(S["dve_step"], G.up("dve_step"))
                    v.wait_ge(S["dve_step"], G.now("dve_step"))
                    ts(o1, o1, rtop[:, tile, 4, 3:4], None, ALU.mult).then_inc(S["dve_step"], G.up("dve_step"))
                    v.wait_ge(S["dve_step"], G.now("dve_step"))
                    ts(o2, o2, rtop[:, tile, 4, 4:5], None, ALU.mult).then_inc(S["dve_step"], G.up("dve_step"))
                    v.wait_ge(S["dve_step"], G.now("dve_step"))
                    tt(rtop[:, tile, 5, :], o1, o2, ALU.add).then_inc(S["dve_step"], G.up("dve_step"))
                    v.wait_ge(S["dve_step"], G.now("dve_step"))
                v.memset(nmx[0:1, 33:34], 0.0).then_inc(S["mask"], G.up("mask"))
                v.wait_ge(S["rank_psum"], G.next("rank_psum"))
                for tile in range(2):
                    sl = rtop[:, tile, 0, :]
                    ts(sl, ps[0][:, 8 * tile:8 * tile + 8], 1.0, None, ALU.add).then_inc(S["dve_step"], G.up("dve_step"))
                    v.wait_ge(S["dve_step"], G.now("dve_step"))
                    tt(sl, sl, rtop[:, tile, 3, :], ALU.mult).then_inc(S["dve_step"], G.up("dve_step"))
                    v.wait_ge(S["dve_step"], G.now("dve_step"))
                    ts(sl, sl, -1.0, None, ALU.add).then_inc(S["dve_step"], G.up("dve_step"))
                    v.wait_ge(S["dve_step"], G.now("dve_step"))
                v.tensor_reduce(cnt[:, 0:1], ps[0][:, 16:24], AX, ALU.max).then_inc(S["dve_step"], G.up("dve_step"))
                v.wait_ge(S["dve_step"], G.now("dve_step"))
                ts(cnt[:, 1:2], cnt[:, 0:1], float(SLOTS), None, ALU.is_gt).then_inc(S["dve_step"], G.up("dve_step"))
                v.wait_ge(S["dve_step"], G.now("dve_step"))
                cp(flag[0:1, 0:1], cnt[0:1, 1:2]).then_inc(S["flag"], G.up("flag"))

            def slot_tables(second):
                for tile in range(2):
                    sl = rtop[:, tile, 0, :]
                    if second:
                        ts(sl, sl, -float(SLOTS), None, ALU.add).then_inc(S["dve_step"], G.up("dve_step"))
                        v.wait_ge(S["dve_step"], G.now("dve_step"))
                    for e in range(EXPERTS):
                        ts(gm[:, tile, e, :], pr("iota"), rtop[:, tile, 0, e:e + 1], None, ALU.is_equal)
                        m = ts(gwt[:, tile, e, :], pr("iota"), rtop[:, tile, 0, e:e + 1], rtop[:, tile, 5, e:e + 1],
                               ALU.is_equal, ALU.mult)
                m.then_inc(S["gw"], G.up("gw"))

            def expert(e):
                for j in range(11):
                    v.wait_ge(S["mgu_psum"], G.next("mgu_psum"))
                    v.wait_ge(S["mgu_exp"], G.next("mgu_exp"))
                    b = me[:, j % 2, :]
                    ts(b, b, 1.0, None, ALU.add).then_inc(S["dve_step"], G.up("dve_step"))
                    v.wait_ge(S["dve_step"], G.now("dve_step"))
                    v.reciprocal(b, b).then_inc(S["dve_step"], G.up("dve_step"))
                    v.wait_ge(S["dve_step"], G.now("dve_step"))
                    tt(b, b, ps[j % 3][:, 0:256], ALU.mult).then_inc(S["dve_step"], G.up("dve_step"))
                    v.wait_ge(S["dve_step"], G.now("dve_step"))
                    tt(mact[:, 256 * j:256 * j + 256], b, ps[j % 3][:, 256:512], ALU.mult).then_inc(S["mgu_act"], G.up("mgu_act"))
                for g in range(4):
                    bank = 1 + g % 2 if g < 2 else 6 + g % 2
                    v.wait_ge(S["sc_psum"], G.next("sc_psum"))
                    for q in range(2):
                        m = add_to_h(2 * g + q, 1, STREAM, TOK, ps[bank][:, STREAM * q:STREAM * q + STREAM])
                    m.then_inc(S["h_ffn"], G.up("h_ffn"))
                    v.wait_ge(S["h_ffn"], G.now("h_ffn"))

            def experts(second):
                slot_tables(second)
                G.begin()
                expert(0)
                with v.Fori(1, EXPERTS) as e:
                    G.repeat(e)
                    expert(e)
                G.end(EXPERTS)

            def program():
                v.wait_ge(S["cond_exp"], G.next("cond_exp"))
                c_ = cond[:, :, :].rearrange("p a b -> p (a b)")
                ts(c_, c_, 1.0, None, ALU.add).then_inc(S["dve_step"], G.up("dve_step"))
                v.wait_ge(S["dve_step"], G.now("dve_step"))
                v.reciprocal(c_, c_).then_inc(S["dve_step"], G.up("dve_step"))
                v.wait_ge(S["dve_step"], G.now("dve_step"))
                tt(c_, c_, pr("cond"), ALU.mult).then_inc(S["cond"], G.up("cond"))
                for layer in range(LAYERS):
                    modulation(layer)
                    norm(layer, 0, 0, TOK)
                    projections(layer)
                    attention(layer)
                    gdn_prepare(layer)
                    gdn(layer)
                    gla(layer)
                    closing(layer)
                    out_projection(layer)
                    norm(layer, 1, *h_range(layer))
                    if layer == 0:
                        dense_ffn()
                routing()
                experts(False)
                v.wait_ge(S["flag"], 1)
                over = v.value_load(flag[0:1, 0:1], min_val=0, max_val=1)
                with v.If(over > 0):
                    experts(True)

            program()
            v.tensor_copy(osb, hT[:, :, STREAM:TOK]).then_inc(S["final"], 1)

        @block.gpsimd
        def _(pool):
            G = Counts(S)
            tt, ts, cp = pool.tensor_tensor, pool.tensor_scalar, pool.tensor_copy

            def zeros(layer):
                pool.wait_ge(S["a"], G.at("a", 16 * layer + 8))
                for q, w in ((0, 2), (258, 2)):
                    m = pool.memset(cin[:, :, :, q:q + w].rearrange("p a b c -> p (a b) c"), 0.0)
                m.then_inc(S["cin_zero"], G.up("cin_zero"))

            def attention(layer):
                pool.wait_ge(S["att_rstd"], G.next("att_rstd"))
                pool.memset(akz[HD:P, 0, :], 0.0).then_inc(S["pool_step"], G.up("pool_step"))
                pool.wait_ge(S["pool_step"], G.now("pool_step"))
                pool.memset(akz[0:HD, 1, :], 0.0).then_inc(S["kz_zero"], G.up("kz_zero"))
                pool.wait_ge(S["kz_zero"], G.now("kz_zero"))
                for i in range(TILES):
                    pool.wait_ge(S["att_normed"], G.next("att_normed"))
                    for lo, hi, w in ((0, 8, 0), (8, 10, 64)):
                        gain = pr("qkgain", HD, 128 * layer + w)
                        m = tt(att[:, i, lo:hi, :], att[:, i, lo:hi, :], rep(gain, 1, hi - lo), ALU.mult)
                    if i >= 2:
                        m.then_inc(S["pool_step"], G.up("pool_step"))
                        pool.wait_ge(S["pool_step"], G.now("pool_step"))
                        x = att[:, i, 0:10, :]
                        cos = pr("cos", HD, HD * (i - 2))
                        sin = pr("sin", HD, HD * (i - 2))
                        tt(ra, x, rep(cos, 1, 10), ALU.mult)
                        x5 = x.rearrange("p h (w s c) -> p (h w) s c", w=2, s=2)
                        r5 = rb.rearrange("p h (w s c) -> p (h w) s c", w=2, s=2)
                        s5 = sin.rearrange("p (w s c) -> p w s c", w=2, s=2)
                        for s in range(2):
                            for w in range(2):
                                o = r5[:, w:20:2, s, :]
                                m = tt(o, x5[:, w:20:2, 1 - s, :], rep(s5[:, w, s, :], 1, 10), ALU.mult)
                        m.then_inc(S["pool_step"], G.up("pool_step"))
                        pool.wait_ge(S["pool_step"], G.now("pool_step"))
                        m = tt(x, ra, rb, ALU.add)
                    m.then_inc(S["qk"], G.up("qk"))
                    pool.wait_ge(S["qk"], G.now("qk"))

            def gdn_prepare(layer):
                pool.wait_ge(S["conv"], G.next("conv", 6))
                pool.memset(kz[HD:P, :, 0, :], 0.0).then_inc(S["pool_step"], G.up("pool_step"))
                pool.wait_ge(S["pool_step"], G.now("pool_step"))
                pool.memset(kz[0:HD, :, 1, :], 0.0).then_inc(S["pool_step"], G.up("pool_step"))
                pool.wait_ge(S["pool_step"], G.now("pool_step"))
                for c in range(6):
                    pool.wait_ge(S["conv_exp"], G.next("conv_exp"))
                    ts(ce[:, c, :, :], ce[:, c, :, :], 1.0, None, ALU.add).then_inc(S["conv_exp1"], G.up("conv_exp1"))
                for c in (2, 3, 0, 1, 4, 5):
                    pool.wait_ge(S["conv_rec"], G.at("conv_rec", 6 * layer + c + 1))
                    tt(cv[:, c, :, :], cv[:, c, :, :], ce[:, c, :, :], ALU.mult).then_inc(S["convd"], G.up("convd"))
                    if c < 4:
                        pool.wait_ge(S["convd"], G.now("convd"))
                        x = cv[:, c, :, :].rearrange("p a b -> p (a b)")
                        tt(csq[:, c, :], x, x, ALU.mult).then_inc(S["qk_sq"], G.up("qk_sq"))
                pool.wait_ge(S["convd"], G.now("convd"))
                G.n["conv_rec"] = 6 * layer + 6
                pool.wait_ge(S["kq"], G.next("kq", 4))
                cp(kz[0:HD, :, 0, :], kq[0:HD, 0, :, :]).then_inc(S["pool_step"], G.up("pool_step"))
                pool.wait_ge(S["pool_step"], G.now("pool_step"))
                cp(kz[HD:P, :, 1, :], kq[HD:P, 0, :, :]).then_inc(S["kz2"], G.up("kz2"))
                pool.wait_ge(S["kz2"], G.now("kz2"))
                pool.wait_ge(S["eg"], G.next("eg"))
                for d in range(2):
                    m = tt(erb[:, d, :, :], eg[:, 2 + d, :, :], gsm[:, 5, :, 4 * d:4 * d + 4], ALU.mult)
                m.then_inc(S["pool_step"], G.up("pool_step"))
                pool.wait_ge(S["pool_step"], G.now("pool_step"))

            def gdn(layer):
                pool.wait_ge(S["kvtok"], G.next("kvtok", 4))
                pool.wait_ge(S["kz2"], G.now("kz2"))
                s0 = 16 * layer
                for kind, d, i, k in gdn_order():
                    tile = TILE_ORDER[d][i]
                    pt, xv, xk, kd_, qg_ = slot(d, i)
                    if kind == "decay":
                        g = gsm[:, 4, tile, 4 * d:4 * d + 4]
                        tt(Gr[d], rep(minc[d], 1, 4), rep(g, 2, P), ALU.mult).then_inc(S["gr"], G.up("gr"))
                    elif kind == "kk":
                        if i >= 2:
                            pool.wait_ge(S["gdn_s"], G.at("gdn_s", s0 + 4 * (i - 2) + 2 + d + 1))
                        beta = gsm[:, 5, tile, 4 * d:4 * d + 4]
                        tt(pt, rep(minc[d], 1, 4), rep(beta, 2, P), ALU.mult).then_inc(S["pool_step"], G.up("pool_step"))
                        pool.wait_ge(S["pool_step"], G.now("pool_step"))
                        pool.wait_ge(S["decE"], G.next("decE"))
                        tt(E[d], E[d], pt, ALU.mult).then_inc(S["dtb"], G.up("dtb"))
                        pool.wait_ge(S["dtb"], G.now("dtb"))
                        pool.wait_ge(S["decB"], G.next("decB"))
                        for p_ in range(2):
                            half = slice(HD * p_, HD * p_ + HD)
                            tt(qg_[half, :, :], kq[half, 1, :, P * tile:P * tile + P], Y[d][half, p_:4:2, :], ALU.mult).then_inc(S["pool_step"], G.up("pool_step"))
                            pool.wait_ge(S["pool_step"], G.now("pool_step"))
                        end = 63 if d == 0 else 0
                        cp(eend[:, d, i % 2, :, :], Y[d][:, :, end:P:CHUNK]).then_inc(S["qg"], G.up("qg"))
                        k_ = kvtok[:, tile, 0:256].rearrange("p (h e) -> p h e", h=4)
                        tt(kd_, k_, rep(erb[:, d, tile, :], 2, HD), ALU.mult).then_inc(S["kd"], G.up("kd"))
                    elif kind == "first":
                        pool.wait_ge(S["kk_out"], G.next("kk_out", 2))
                        k_ = kvtok[:, tile, 0:256].rearrange("p (h e) -> p h e", h=4)
                        ke = E[d].rearrange("p a b -> p (a b)")[:, 0:256].rearrange("p (h e) -> p h e", h=4)
                        tt(ke, k_, rep(eg[:, d, tile, :], 2, HD), ALU.mult).then_inc(S["ke"], G.up("ke"))

            def closing(layer):
                t0, t1 = h_range(layer)
                pool.wait_ge(S["gla_o"], G.next("gla_o", 16))
                pool.wait_ge(S["gdn_o"], G.next("gdn_o", 16))
                for m_ in range(4):
                    src = ol if m_ < 2 else og
                    o = src[:, 0, m_ % 2, t0:t1]
                    tt(o, o, src[:, 1, m_ % 2, t0:t1], ALU.add).then_inc(S["pool_step"], G.up("pool_step"))
                    pool.wait_ge(S["pool_step"], G.now("pool_step"))
                    tt(fsq[:, m_, t0:t1], o, o, ALU.mult).then_inc(S["fin_sq"], G.up("fin_sq"))
                for m_ in range(4):
                    pool.wait_ge(S["fin_e"], G.next("fin_e"))
                    ts(fsg[:, m_, t0:t1], fsg[:, m_, t0:t1], 1.0, None, ALU.add).then_inc(S["fin_e1"], G.up("fin_e1"))
                for m_ in range(4):
                    src = gr_ if m_ < 2 else gz
                    pool.wait_ge(S["fin_rec"], G.next("fin_rec"))
                    tt(fsg[:, m_, t0:t1], fsg[:, m_, t0:t1], src[:, m_ % 2, t0:t1], ALU.mult).then_inc(S["fin_sg"], G.up("fin_sg"))

            pool.wait_ge(S["params_in"], 16)
            for layer in range(LAYERS):
                zeros(layer)
                attention(layer)
                gdn_prepare(layer)
                gdn(layer)
                closing(layer)


def constants():
    r = np.arange(P)
    same = (r[:, None] // CHUNK) == (r[None, :] // CHUNK)
    c = {"ident": np.eye(P), "ones": np.ones((P, P)), "headones": same,
         "lt": np.concatenate([(r[:, None] > r[None, :]) & same, (r[:, None] < r[None, :]) & same], 1),
         "minc": np.concatenate([(r[:, None] <= r[None, :]) & same, (r[:, None] >= r[None, :]) & same], 1)}
    levels = []
    for d in range(2):
        for l in range(LEVELS):
            s = 1 << l
            m = (r[:, None] // (2 * s) == r[None, :] // (2 * s)) & (r[:, None] // s % 2 == 1) & (r[None, :] // s % 2 == 0)
            levels.append(m if d == 0 else m.T)
    c["level"] = np.concatenate(levels, 1)
    c["ranktri"] = r[:, None] < r[None, :]
    t = np.arange(CHUNK)
    s = (r % CHUNK)[:, None]
    c["maskc"] = np.concatenate([s <= t[None, :], s >= t[None, :]], 1)
    c["iota"] = np.tile(r, (P, 1))
    c["iota8"] = np.tile(np.arange(8), (P, 1))
    c["scanmask"] = np.tile((np.arange(TOK) % CHUNK != 0), (P, 1))
    inv = (np.float32(10000.0) ** (-np.arange(0, 32, 2, dtype=np.float32) / np.float32(32))).astype(np.float32)
    pos = np.arange(STREAM)
    ang = np.stack([(pos // 64).astype(np.float32)[:, None] * inv, (pos % 64).astype(np.float32)[:, None] * inv], 1)
    cos, sin = np.cos(ang), np.sin(ang)
    c["cos"] = np.stack([cos, cos], 2).reshape(2, P, 64).transpose(1, 0, 2).reshape(P, 128)
    c["sin"] = np.stack([-sin, sin], 2).reshape(2, P, 64).transpose(1, 0, 2).reshape(P, 128)
    c["eps"] = np.full((P, 1), EPS)
    c["one"] = np.ones((P, 1))
    return {k: np.ascontiguousarray(x, dtype=np.float32) for k, x in c.items()}


def cols(a):
    a = np.asarray(a)
    return np.moveaxis(a.reshape(a.shape[:-1] + (-1, P)), -1, 0).reshape(P, -1)


def rows(a):
    return np.broadcast_to(np.asarray(a).reshape(1, -1), (P, np.asarray(a).size))


def kernel(**inputs):
    import concourse.bacc as bacc
    from concourse.bass_utils import run_bass_kernel_spmd

    x = {k: np.asarray(a) for k, a in inputs.items()}
    p = constants()
    p["cond"] = np.stack([x["c"].reshape(KD, P), x["c_ctx"].reshape(KD, P)], 2).transpose(1, 0, 2).reshape(P, 16)
    p["bmod"] = cols(x["b_mod"])
    p["norms"] = np.stack([x["norm_mix"].reshape(LAYERS, KD, P), x["norm_ffn"].reshape(LAYERS, KD, P)], 1) \
        .transpose(3, 0, 1, 2).reshape(P, -1)
    up = np.zeros((P, LAYERS, 2, 256), np.float32)
    for d in range(2):
        up[16 * d:16 * d + 16, :, d] = x["gla_gate_up"][:, d].transpose(1, 0, 2)
    p["gate_up"] = up.reshape(P, -1)
    p["gate_bias"] = cols(x["gla_gate_bias"])
    gains = np.stack([x["gla_out_gain"], x["gdn_out_gain"]], 1).transpose(2, 0, 1)
    p["gains"] = np.concatenate([gains, gains], 0).reshape(P, -1)
    p["conv"] = x["gdn_conv"].reshape(LAYERS, 5, 6, P).transpose(3, 0, 2, 1).reshape(P, -1)
    p["dtb"], p["alog"] = rows(x["gdn_dt_bias"]), rows(x["gdn_a_log"])
    p["qkgain"] = rows(np.stack([x["att_q_gain"], x["att_k_gain"]], 1))
    p["router"] = x["moe_router"][0].reshape(KD, P, 8).transpose(1, 0, 2).reshape(P, -1)
    p["rbias"] = rows(x["moe_router_bias"][0])
    small = np.concatenate([x["w_in"][:, :, C_GLOW:C_GLOW + 32], x["w_in"][:, :, C_AB:C_AB + 16]], 2)
    p["wsmall"] = small.reshape(LAYERS, KD, P, 48).transpose(2, 0, 1, 3).reshape(P, -1)
    packed = np.concatenate([np.asarray(p[name]).reshape(P, width) for name, width in PARAMS], 1)
    arrays = {
        "in_xT": np.ascontiguousarray(np.concatenate([x["ctx"][0], x["x"][0]], 0).T),
        "in_params": np.ascontiguousarray(packed),
        "in_w_mod": x["w_mod"], "in_w_in": x["w_in"], "in_w_out": x["w_out"],
        "in_ffn_gu": x["ffn_gate_up"], "in_ffn_down": x["ffn_down"],
        "in_moe_gu": x["moe_gate_up"], "in_moe_down": x["moe_down"],
    }
    nc = bacc.Bacc("TRN2", target_bir_lowering=False, num_devices=1)
    args = [nc.dram_tensor(n, a.shape, mybir.dt.from_np(a.dtype), kind="ExternalInput").ap()
            for n, a in arrays.items()]
    out = nc.dram_tensor("out_T", (D, STREAM), F32, kind="ExternalOutput").ap()
    build(nc, *args, out)
    r = run_bass_kernel_spmd(nc, [arrays], core_ids=[0])
    return np.ascontiguousarray(r.results[0]["out_T"].T).reshape(1, STREAM, D)
```

```python
from contextlib import ExitStack

import numpy as np
import concourse.bass as bass
from concourse import mybir

ALU = mybir.AluOpType
ACT = mybir.ActivationFunctionType
F32 = mybir.dt.float32
I32 = mybir.dt.int32
U32 = mybir.dt.uint32
AX = mybir.AxisListType.X

P = 128
LAYERS = 2
D = 1024
KD = D // P
TOK = 512
STREAM = 256
TILES = TOK // P
CHUNK = 64
CHUNKS = TOK // CHUNK
HD = 64
EPS = 1e-6
D_FF = 2816
FC = D_FF // P
EXPERTS = 8
SLOTS = 128
RING = 11
BLK = 1024
LEVELS = 6
Q_HEADS, KV_HEADS = 8, 2
C_GLA_Q, C_GLA_K, C_GLA_V, C_GLA_R, C_GLOW = 0, 256, 512, 768, 1024
C_GDN_Q, C_GDN_K, C_GDN_V, C_GDN_Z, C_AB, C_ATT = 1056, 1312, 1568, 1824, 2080, 2096
IN_BLOCKS = [("att0", C_ATT, True), ("att1", C_ATT + 256, True), ("att2", C_ATT + 512, True),
             ("gdn0", C_GDN_Q, False), ("gdn1", C_GDN_K, False), ("gdn2", C_GDN_V, False),
             ("gq", C_GLA_Q, False), ("gk", C_GLA_K, False), ("gv", C_GLA_V, True),
             ("gr", C_GLA_R, False), ("gz", C_GDN_Z, False)]
MOD_BLOCKS = 6 * D // 512

PARAMS = [("ident", 128), ("cond", 16), ("eps", 1), ("one", 1),
          ("ones", 128), ("headones", 128), ("lt", 256), ("minc", 256),
          ("level", 2 * LEVELS * 128), ("ranktri", 128), ("maskc", 128), ("iota", 128), ("iota8", 8),
          ("scanmask", TOK), ("cos", 128), ("sin", 128),
          ("bmod", LAYERS * 48), ("norms", LAYERS * 16), ("gate_up", LAYERS * 512),
          ("gate_bias", LAYERS * 4), ("gains", LAYERS * 2), ("conv", LAYERS * 30), ("dtb", LAYERS * 8),
          ("alog", LAYERS * 8), ("qkgain", LAYERS * 128), ("router", 64), ("rbias", 8),
          ("wsmall", LAYERS * KD * 48)]
HEAD = 146
OFFSET, NPARAM = {}, 0
for _name, _width in PARAMS:
    OFFSET[_name] = NPARAM
    NPARAM += _width


class Counts:

    def __init__(self, sems):
        self.sems, self.n, self.per, self.turn, self.start = sems, {}, {}, None, None
        self.held = {bank: ("head_in", 16) for bank in range(8)}

    def seen(self, name):
        return self.n.get(name, 0)

    def at(self, name, count):
        if self.turn is not None and self.per.get(name):
            assert self.per[name] + count > 0, (name, count)
            return self.per[name] * self.turn + count
        assert count > 0, (name, count)
        return count

    def next(self, name, k=1):
        self.n[name] = self.seen(name) + k
        return self.at(name, self.n[name])

    def up(self, name, k=1):
        self.n[name] = self.seen(name) + k
        return k

    def now(self, name):
        return self.at(name, self.seen(name))

    def filled(self, bank, emptied_by, k=1):
        self.n[emptied_by] = self.seen(emptied_by) + k
        for b in (bank if isinstance(bank, (list, tuple)) else [bank]):
            self.held[b] = (emptied_by, self.n[emptied_by])
        return self.n[emptied_by]

    def emptied(self, bank):
        name, count = self.held[bank]
        return self.sems[name], self.at(name, count)

    def begin(self):
        self.start = dict(self.n)
        self.held_start = dict(self.held)

    def repeat(self, turn):
        self.per = {k: v - self.start.get(k, 0) for k, v in self.n.items() if v != self.start.get(k, 0)}
        for b, (name, count) in self.held.items():
            if self.held_start.get(b) != (name, count):
                self.held[b] = (name, count - self.per.get(name, 0))
        self.n, self.turn = dict(self.start), turn

    def end(self, turns):
        self.n = dict(self.start)
        for k, v in self.per.items():
            self.n[k] = self.start.get(k, 0) + v * turns
        for b, (name, count) in list(self.held.items()):
            self.held[b] = (name, count + self.per.get(name, 0) * (turns - 1)) if self.per.get(name) else (name, count)
        self.per, self.turn = {}, None


SEMS = ["head_in", "params_in", "x_in", "ring_free", "out_stored"] + [f"ring_full{i}" for i in range(RING)] + [
    "act_step", "dve_step", "pool_step",
    "cond_exp", "cond", "mod_psum", "mod_row", "modT_psum", "mod",
    "sq", "sumsq_psum", "rstd", "a", "h_mix", "h_ffn",
    "projd_psum", "proja_psum", "projd", "proja",
    "att_sq", "att_ss", "att_rstd", "att_normed", "qk", "qk_last", "kz_zero", "cin_zero",
    "qT_psum", "kT_psum", "qT", "kz", "scores_psum", "smax", "att_exp", "att_p", "pT_psum", "pT",
    "pv_psum", "att_out",
    "conv", "conv_tap", "conv_exp", "conv_exp1", "conv_rec", "convd", "qk_sq", "qk_ss_psum", "qk_rn", "kq", "kz2",
    "kvT_psum", "kvtok",
    "gx", "g_act", "g", "gscan_psum", "eg", 
    "gr", "dec_psum", "decE", "decB", "dtb", "qg", "kd", "ke", "kk_psum", "kk_out",
    "y_psum", "ym", "dtu_psum", "tu", "x_psum", "x_out", "ru_psum", "gdn_u", "ro_psum", "gdn_o",
    "rw_psum", "gdn_s",
    "gate_psum", "gate_x", "gate_ln", "gate_D", "gate_E", "gate_k", "gate_f", "gate_fe", 
    "ktr_psum", "ktok", "gs_psum", "gla_pt", "go_psum", "gla_o", "gw_psum", "gla_s",
    "fin_sq", "fin_psum", "fin_rs", "fin_e", "fin_e1", "fin_rec", "fin_sg", "mix",
    "wout_psum", "gu_psum", "gu_exp", "gu_act", "down_psum",
    "logit_psum", "bT_psum", "btok", "top", "top_e", "mask", "rank_psum", "gw", "gT_psum", "smat",
    "xe_psum", "xe", "mgu_psum", "mgu_exp", "mgu_act", "aT_psum", "aT_sb", "y2_psum", "y2", "sc_psum",
    "flag", "final"]


def gdn_order():
    order = []
    for i in range(TILES + 1):
        if i < TILES:
            for kind in ("decay", "kk", "first"):
                order += [(kind, d, i, 1) for d in range(2)]
        for level in range(2, LEVELS + 1):
            if i < TILES:
                order += [("Y", d, i, level) for d in range(2)]
            if i > 0 and level < 6:
                kind, k = ("ru", "ro")[level % 2], (level - 2) // 2
                order += [(kind, d, i - 1, k) for d in range(2)]
            if i < TILES:
                order += [("dTU", d, i, level) for d in range(2)]
        if i < TILES:
            order += [("X", d, i, 0) for d in range(2)]
    return order


SCORE_BANK = (0, 1, 6)
MOD_PLACES = {"attention": (0, 2), "gdn": (2, 6), "gla": (6, 10), "closing": (10, 12)}
MOD_TURNED = {"attention": (0, 1), "gdn": (1, 6), "gla": (6, 9), "closing": (9, 11)}
TILE_ORDER = [[0, 1, 2, 3], [1, 0, 3, 2]]
CHUNK_ORDER = [[0, 1, 2, 3, 4, 5, 6, 7], [3, 2, 1, 0, 7, 6, 5, 4]]


def rep(ap, axis, n):
    ap = ap.unsqueeze(axis)
    shape = list(ap.shape)
    shape[axis] = n
    return ap.broadcast_to(shape)


def build(nc, xT, params, w_mod, w_in, w_out, ffn_gu, ffn_down, moe_gu, moe_down, outT):
    with ExitStack() as ctx:
        def sb(name, shape, dt=F32):
            return ctx.enter_context(nc.sbuf_tensor(name, shape, dt))

        par = sb("par", [P, NPARAM])
        hT = sb("hT", [P, KD, TOK])
        aT = sb("aT", [P, KD, TOK])
        ring = sb("ring", [P, RING, BLK])
        arena = sb("arena", [P, 26112])
        mcol = sb("mcol", [P, LAYERS, 48, 2])
        coef = sb("coef", [P, 2, 8, 2])
        cond = sb("cond_sb", [P, 8, 2])
        ab = sb("ab", [P, TILES, 16])
        gsm = sb("gsm", [P, 6, TILES, 8])
        eend = sb("eend", [P, 2, 2, 4, 2])
        state = sb("state", [P, 2, 2, P])
        ubuf = sb("ubuf", [P, 2, 256])
        small = sb("small", [P, 104])
        rsum = small[:, 0:32]
        ssq = small[:, 32:72].rearrange("p (a b) -> p a b", a=TILES)
        nmx = small[:, 72:104]
        eg = small[:, 0:64].rearrange("p (a b c) -> p a b c", a=4, b=TILES)
        erb = small[:, 64:96].rearrange("p (a b c) -> p a b c", a=2, b=TILES)
        flag = sb("flag", [1, 1], I32)
        gfac = gsm[:, 0:4, :, :].rearrange("p a b c -> p (a b c)").rearrange("p (a b c d) -> p a b c d", a=4, b=2, c=2)
        mrow = ubuf[0:2, :, :].rearrange("p a b -> p (a b)")
        rtop = state[:, 0, 0, 0:96].rearrange("p (a b c) -> p a b c", a=2, b=6)
        cnt = state[:, 0, 0, 96:104]
        idx = state[:, 0, 1, 0:16].bitcast(U32).rearrange("p (a b) -> p a b", a=2)
        ps = [ctx.enter_context(nc.psum_tensor(f"ps{i}", [P, 512], F32)) for i in range(8)]
        S = {name: ctx.enter_context(nc.semaphore(name)) for name in SEMS}

        def pr(name, width=None, at=0, rows=P):
            o = OFFSET[name] + at
            return par[0:rows, o:o + (width if width is not None else dict(PARAMS)[name])]

        ident, ones, headones = pr("ident"), pr("ones"), pr("headones")
        eps, one = pr("eps"), pr("one")
        lt = [pr("lt", 128, 128 * d) for d in range(2)]
        minc = [pr("minc", 128, 128 * d) for d in range(2)]
        maskc = [pr("maskc", 64, 64 * d) for d in range(2)]

        def level_mask(d, l):
            return pr("level", 128, 128 * (LEVELS * d + l - 1))

        def ar(offset, *shape):
            size = int(np.prod(shape))
            v = arena[:, offset:offset + size]
            if len(shape) == 1:
                return v
            names = "abcde"[:len(shape)]
            return v.rearrange(f"p ({' '.join(names)}) -> p {' '.join(names)}",
                               **{n: s for n, s in zip(names[1:], shape[1:])})

        gq, gk, gr_, gz = (ar(1024 * i, 2, TOK) for i in range(4))
        glow = arena[0:32, 4096:4608]
        gv = ar(4608, TILES, 256)
        KQ = 5632
        UN = KQ + 4096 + 2048
        OT = UN + 12288
        kq = ar(KQ, 2, 2, TOK)
        kz = ar(KQ + 2048, 2, 2, TOK)
        cin = ar(KQ, 6, 2, 260)
        kvtok = ar(KQ + 4096, TILES, 512)
        cv = ar(UN + 11264, 6, 2, 256)
        ce = ar(UN, 6, 2, 256)
        csq = ar(UN + 3072, 4, TOK)
        crn = ar(UN + 5120, 4, TOK)
        og = ar(OT, 2, 2, TOK)
        att = ar(UN, TILES, 12, HD)
        qT = ar(UN + 3072, 4, TOK)
        akz = ar(UN + 5120, 2, TOK)
        Pb = ar(UN + 6144, 3, TOK)
        PTb = ar(UN + 7680, 2, 4, P)
        asq = ar(UN + 6144, TILES, 10, HD)
        ra = ar(UN + 8704, 10, HD)
        rb = ar(UN + 9344, 10, HD)
        ra3, rb3 = ar(UN + 9984, 10, HD), ar(UN + 10624, 10, HD)

        def scratch(d, k):
            return ar(UN + 3072 * d + 512 * k, 4, P)

        Gr, E, AT, T, U, Y = ([scratch(d, k) for d in range(2)] for k in range(6))

        def slot(d, i):
            o = UN + 6144 + 1536 * (2 * d + i % 2)
            return ar(o, 4, P), ar(o + 512, 256), ar(o + 768, 2, P), ar(o + 1024, 4, HD), ar(o + 1280, 2, P)

        GA = KQ
        qp = ar(GA, 2, 2, TOK)
        kp = ar(GA + 2048, 2, 2, TOK)
        qz = ar(GA + 4096, 2, 2, 2, TOK)
        kt = ar(GA + 8192, 2, TILES, 256)
        pg = ar(GA + 10240, 2, TILES, 4, CHUNK)
        gw_ = ar(GA + 12288, 2, 4, TOK)
        ol = ar(GA + 16384, 2, 2, TOK)
        fsq, fsg, frs = ar(GA, 4, TOK), ar(GA + 2048, 4, TOK), ar(GA + 4096, 4, TOK)
        nsq, nhn = ar(0, KD, TOK), ar(4096, KD, TOK)
        act = ar(0, FC, TOK)
        fe, ft = ar(11264, 4, TOK), ar(13312, 4, TOK)
        btok = ar(8192, 2, D)
        gm = ar(10240, 2, EXPERTS, SLOTS)
        gwt = ar(12288, 2, EXPERTS, SLOTS)
        sm = ar(14336, EXPERTS, STREAM)
        xe = ar(16384, KD, SLOTS)
        mact = ar(17408, D_FF)
        mactT = ar(20224, FC, SLOTS)
        y2 = ar(23040, D)
        me, mt = ar(24064, 2, 256), ar(24576, 2, 256)
        osb = ar(0, KD, STREAM)

        def h_range(layer):
            return (0, TOK) if layer < LAYERS - 1 else (STREAM, TOK)

        def tile_needed(layer, tile):
            return layer < LAYERS - 1 or tile >= TILES // 2

        def att_units(layer):
            out, g = [], 0
            for lat in ((0, 1) if layer < LAYERS - 1 else (1,)):
                for pair in range(4):
                    for par_ in range(2):
                        for qt in range(2):
                            out.append((2 * pair + par_, 2 * lat + qt, 4 if lat else 2, g, pair, lat, qt))
                    g += 1
            return out

        def rstd_buf(n):
            return fe_rstd[:, 0:n]

        fe_rstd = ar(8192, TOK)

        def proj_dst(name, half):
            if name.startswith("att"):
                c = 4 * int(name[3])
                place = slice(8, 12) if c == 8 else slice(c // 4, 8, 2)
                return att[:, 2 * half:2 * half + 2, place, :]
            if name == "gv":
                return gv[:, 2 * half:2 * half + 2, :]
            if name.startswith("gdn"):
                return cin[:, 2 * int(name[3]) + half, :, 2:258]
            return {"gq": gq, "gk": gk, "gr": gr_, "gz": gz}[name][:, half, :]

        def proj_src(name, bank):
            if name.startswith("att"):
                return ps[bank][:, :].rearrange("p (a b c) -> p a b c", a=2, b=4)
            if name == "gv" or name.startswith("gdn"):
                return ps[bank][:, :].rearrange("p (a b) -> p a b", a=2)
            return ps[bank][:, :]

        block = ctx.enter_context(nc.Block())

        @block.sync
        def _(sp):
            G = Counts(S)
            sp.dma_start(par[:, 0:HEAD], params[:, 0:HEAD]).then_inc(S["head_in"], 16)
            count = [0]

            def load(src, k):
                n = count[0]
                count[0] += 1
                if G.turn is None and n == RING:
                    sp.dma_start(par[:, HEAD:], params[:, HEAD:]).then_inc(S["params_in"], 16)
                    sp.dma_start(hT[:, :, :], xT.rearrange("(k p) t -> p k t", p=P)).then_inc(S["x_in"], 16)
                if G.turn is not None or n >= RING:
                    G.n["ring_free"] = n - RING + 1
                    sp.wait_ge(S["ring_free"], G.at("ring_free", n - RING + 1))
                dst = ring[:, n % RING, :]
                if k > 1:
                    dst = dst.rearrange("p (k c) -> p k c", k=k)
                sp.dma_start(dst, src).then_inc(S[f"ring_full{n % RING}"], 16)

            def load_cols(w, c0):
                for kb in range(2):
                    load(w[512 * kb:512 * kb + 512, c0:c0 + 256].rearrange("(k p) c -> p k c", p=P), 4)

            def load_ffn(gu, down):
                for j in range(11):
                    for kb in range(2):
                        for s in range(2):
                            c0 = D_FF * s + 256 * j
                            load(gu[512 * kb:512 * kb + 512, c0:c0 + 256].rearrange("(k p) c -> p k c", p=P), 4)
                for f in range(FC):
                    load(down[P * f:P * f + P, :], 1)

            def load_mod(layer):
                for i in range(2 * MOD_BLOCKS):
                    load_cols(w_mod[layer], 256 * i)

            load_mod(0)
            for layer in range(LAYERS):
                for _, c0, _ in IN_BLOCKS:
                    load_cols(w_in[layer], c0)
                if layer + 1 < LAYERS:
                    load_mod(layer + 1)
                for i in range(4):
                    load_cols(w_out[layer], 256 * i)
                if layer == 0:
                    load_ffn(ffn_gu[0], ffn_down[0])

            def experts():
                first = count[0]
                G.n["ring_free"] = first - RING
                G.begin()
                load_ffn(moe_gu[0, 0], moe_down[0, 0])
                G.n["ring_free"] = count[0] - RING
                with sp.Fori(1, EXPERTS) as e:
                    G.repeat(e)
                    count[0] = first
                    load_ffn(moe_gu[0, e], moe_down[0, e])
                G.end(EXPERTS)
                count[0] = first + 66 * EXPERTS

            experts()
            sp.wait_ge(S["flag"], 1)
            over = sp.value_load(flag[0:1, 0:1], min_val=0, max_val=1)
            with sp.If(over > 0):
                experts()
            sp.wait_ge(S["final"], 1)
            sp.dma_start(outT.rearrange("(k p) t -> p k t", p=P), osb).then_inc(S["out_stored"], 16)
            sp.wait_ge(S["out_stored"], 16)

        @block.tensor
        def _(pe):
            G = Counts(S)
            count = [0]

            def block_in():
                s = count[0] % RING
                count[0] += 1
                pe.wait_ge(S[f"ring_full{s}"], G.next(f"ring_full{s}", 16))
                return s

            owed = [0]

            def release(mm):
                mm.then_inc(S["ring_free"], 1)

            def release_next():
                owed[0] += 1

            def pay(mm):
                if owed[0]:
                    owed[0] -= 1
                    release(mm)

            def modulation(first, last, turn_from, turn_to):
                for i in range(first, last):
                    bank = 6 + i % 2
                    pe.wait_ge(*G.emptied(bank))
                    if i == first:
                        pe.wait_ge(*G.emptied(5))
                    for half in range(2):
                        for kb in range(2):
                            s = block_in()
                            w = ring[:, s, :].rearrange("p (k c) -> p k c", k=4)
                            for kk in range(4):
                                mm = pe.matmul(ps[bank][0:2, 256 * half:256 * half + 256],
                                               cond[:, 4 * kb + kk, :], w[:, kk, :],
                                               start=(kb + kk == 0), stop=(kb == 1 and kk == 3))
                                if kk == 0:
                                    pay(mm)
                            if half == 0 or kb == 0:
                                release(mm)
                            else:
                                release_next()
                        if half == 0 and i - 1 >= turn_from:
                            pe.wait_ge(S["mod_row"], G.now("mod_row"))
                            turned = turn_row(i - 1)
                            if i == turn_to:
                                turned.then_inc(S["modT_psum"], 1)
                    mm.then_inc(S["mod_psum"], 1)
                    G.filled(bank, "mod_row")
                if turn_to == last:
                    pe.wait_ge(S["mod_row"], G.now("mod_row"))
                    turn_row(last - 1).then_inc(S["modT_psum"], 1)
                G.filled(5, "mod")

            def turn_row(i):
                for q in range(4):
                    c = 4 * i + q
                    mm = pe.transpose(ps[5][:, 2 * c:2 * c + 2], mrow[0:2, P * q:P * q + P], ident[0:2, 0:2])
                return mm

            def modulation_end():
                pe.wait_ge(S["mod_row"], G.now("mod_row"))
                pe.wait_ge(*G.emptied(5))
                turn_row(MOD_BLOCKS - 1).then_inc(S["modT_psum"], 1)
                G.filled(5, "mod")

            def early_modulation(layer, place):
                if layer + 1 < LAYERS:
                    modulation(*MOD_PLACES[place], *MOD_TURNED[place])

            def sum_over_features(t0, t1):
                pe.wait_ge(*G.emptied(5))
                for k in range(KD):
                    pe.wait_ge(S["sq"], G.next("sq"))
                    mm = pe.matmul(ps[5][:, 0:t1 - t0], ones, nsq[:, k, t0:t1], start=(k == 0), stop=(k == KD - 1))
                mm.then_inc(S["sumsq_psum"], 1)
                G.filled(5, "rstd")

            def projections(layer):
                base = G.seen("a")
                for n, (_, _, by_token) in enumerate(IN_BLOCKS):
                    s = [block_in(), block_in()]
                    w = [ring[:, x, :].rearrange("p (k c) -> p k c", k=4) for x in s]
                    for half in range(2):
                        bank = (0, 5)[half] + n % 2
                        pe.wait_ge(*G.emptied(bank))
                        for t in range(2 if by_token else 1):
                            for k in range(KD):
                                if n == 0 and half == 0 and t == 0:
                                    pe.wait_ge(S["a"], G.at("a", base + k + 1))
                                if by_token:
                                    tile = 2 * half + t
                                    mm = pe.matmul(ps[bank][:, 256 * t:256 * t + 256],
                                                   aT[:, k, P * tile:P * tile + P], w[k // 4][:, k % 4, :],
                                                   start=(k == 0), stop=(k == KD - 1))
                                else:
                                    mm = pe.matmul(ps[bank][:, :], w[k // 4][:, k % 4, P * half:P * half + P],
                                                   aT[:, k, :], start=(k == 0), stop=(k == KD - 1))
                                if k == 0:
                                    pay(mm)
                                if half == 1 and t == (1 if by_token else 0) and k == 3:
                                    release(mm)
                        if half == 0:
                            mm.then_inc(S["projd_psum"], 1)
                            G.filled(bank, "projd")
                        else:
                            mm.then_inc(S["proja_psum"], 1)
                            G.filled(bank, "proja")
                            release_next()
                    if n == 5:
                        w_small = pr("wsmall", KD * 48, layer * KD * 48).rearrange("p (k c) -> p k c", k=KD)
                        pe.wait_ge(*G.emptied(4))
                        for tile in range(TILES):
                            for k in range(KD):
                                mm = pe.matmul(ps[4][:, 16 * tile:16 * tile + 16],
                                               aT[:, k, P * tile:P * tile + P], w_small[:, k, 32:48],
                                               start=(k == 0), stop=(k == KD - 1))
                        mm.then_inc(S["projd_psum"], 1)
                        G.filled(4, "projd")
                        pe.wait_ge(*G.emptied(7))
                        for k in range(KD):
                            mm = pe.matmul(ps[7][0:32, :], w_small[:, k, 0:32], aT[:, k, :],
                                           start=(k == 0), stop=(k == KD - 1))
                        mm.then_inc(S["proja_psum"], 1)
                        G.filled(7, "proja")
                G.n["a"] = base + KD

            def attention(layer):
                for i in range(TILES):
                    if i == 2:
                        early_modulation(layer, "attention")
                    if i < TILES - 1:
                        pe.wait_ge(S["qk"], G.next("qk"))
                    else:
                        pe.wait_ge(S["qk_last"], G.next("qk_last"))
                    if layer == 0 or i >= 2:
                        pe.wait_ge(*G.emptied(2 + i % 2))
                        for hh in range(4):
                            q = att[:, i, 2 * hh:2 * hh + 2, :]
                            mm = pe.transpose(ps[2 + i % 2][:, P * hh:P * hh + P], q, ident)
                        mm.then_inc(S["qT_psum"], 1)
                        G.filled(2 + i % 2, "qT")
                    pe.wait_ge(*G.emptied(4))
                    mm = pe.transpose(ps[4][:, 0:P], att[:, i, 8:10, :], ident)
                    mm.then_inc(S["kT_psum"], 1)
                    G.filled(4, "kz")
                pe.wait_ge(S["qT"], G.now("qT"))
                pe.wait_ge(S["kz"], G.now("kz"))
                units = att_units(layer)
                pt0 = G.seen("pT")
                for i in range(len(units) + 3):
                    if i < len(units):
                        h, qt, nk, *_ = units[i]
                        pe.wait_ge(*G.emptied(SCORE_BANK[i % 3]))
                        mm = pe.matmul(ps[SCORE_BANK[i % 3]][:, 0:P * nk], qT[:, h % 4, P * qt:P * qt + P],
                                       akz[:, h // 4, 0:P * nk], start=True, stop=True)
                        mm.then_inc(S["scores_psum"], 1)
                        G.filled(SCORE_BANK[i % 3], "att_exp")
                    if 2 <= i <= len(units) + 1:
                        h, qt, nk, *_ = units[i - 2]
                        pe.wait_ge(S["att_p"], G.next("att_p"))
                        pe.wait_ge(*G.emptied(2 + (i - 2) % 2))
                        for kt_ in range(nk):
                            mm = pe.transpose(ps[2 + (i - 2) % 2][:, P * kt_:P * kt_ + P],
                                              Pb[:, (i - 2) % 3, P * kt_:P * kt_ + P], ident)
                        mm.then_inc(S["pT_psum"], 1)
                        G.filled(2 + (i - 2) % 2, "pT")
                    if i >= 3:
                        h, qt, nk, g, pair, lat, qq = units[i - 3]
                        pe.wait_ge(S["pT"], G.at("pT", pt0 + i - 2))
                        bank = 4 + g % 2
                        if (i - 3) % 4 == 0:
                            pe.wait_ge(*G.emptied(bank))
                        half = HD * (h % 2)
                        for kt_ in range(nk):
                            mm = pe.matmul(ps[bank][half:half + HD, P * qq:P * qq + P],
                                           att[:, kt_, 10 + h // 4, :], PTb[:, (i - 3) % 2, kt_, :],
                                           start=(kt_ == 0), stop=(kt_ == nk - 1))
                        if (i - 3) % 4 == 3:
                            mm.then_inc(S["pv_psum"], 1)
                            G.filled(bank, "att_out")

            def gdn_prepare(layer):
                early_modulation(layer, "gdn")
                for n, c in enumerate((2, 3, 0, 1)):
                    pe.wait_ge(S["qk_sq"], G.next("qk_sq"))
                    pe.wait_ge(*G.emptied(n % 2))
                    mm = pe.matmul(ps[n % 2][:, :], headones, csq[:, c, :], start=True, stop=True)
                    mm.then_inc(S["qk_ss_psum"], 1)
                    G.filled(n % 2, "qk_rn")
                pe.wait_ge(S["g"], G.next("g"))
                pe.wait_ge(*G.emptied(4))
                for d in range(2):
                    for kind, m in ((0, minc[d]), (2, lt[d])):
                        mm = pe.matmul(ps[4][:, 16 * (kind + d):16 * (kind + d) + 16], m,
                                       gsm[:, 4, :, 4 * d:4 * d + 4], start=True, stop=True)
                mm.then_inc(S["gscan_psum"], 1)
                G.filled(4, "eg")
                pe.wait_ge(S["kq"], G.next("kq", 4))
                pe.wait_ge(S["convd"], G.next("convd", 6))
                for tile in range(TILES):
                    pe.wait_ge(*G.emptied(2 + tile % 2))
                    t = slice(P * tile, P * tile + P)
                    for n in range(4):
                        src = kq[:, 0, n, t] if n < 2 else cv[:, 2 + n, tile // 2, P * (tile % 2):P * (tile % 2) + P]
                        mm = pe.transpose(ps[2 + tile % 2][:, P * n:P * n + P], src, ident)
                    mm.then_inc(S["kvT_psum"], 1)
                    G.filled(2 + tile % 2, "kvtok")
                pe.wait_ge(S["kvtok"], G.now("kvtok"))
                pe.wait_ge(S["kz2"], G.next("kz2"))

            def gdn(layer):
                misc = [0]

                def bank67():
                    misc[0] += 1
                    return 6 + misc[0] % 2

                tu, kko, xo = {}, {}, {}
                for kind, d, i, k in gdn_order():
                    if kind in ("ru", "ro"):
                        c = k if d == 0 else 1 - k
                        r = slice(CHUNK * c, CHUNK * c + CHUNK)
                    tile = TILE_ORDER[d][i]
                    pt, xv, xk, kd_, qg_ = slot(d, i)
                    if kind == "decay":
                        pe.wait_ge(S["gr"], G.next("gr"))
                        pe.wait_ge(*G.emptied(4 + d))
                        mm = pe.matmul(ps[4 + d][:, :], lt[d], Gr[d].rearrange("p a b -> p (a b)"), start=True, stop=True)
                        mm.then_inc(S["dec_psum"], 1)
                        G.filled(4 + d, "decE")
                        pe.wait_ge(*G.emptied(2 + d))
                        mm = pe.matmul(ps[2 + d][:, :], ones, Gr[d].rearrange("p a b -> p (a b)"), start=True, stop=True)
                        mm.then_inc(S["dec_psum"], 1)
                        G.filled(2 + d, "decB")
                    elif kind == "kk":
                        t = slice(P * tile, P * tile + P)
                        for pair in range(2):
                            bank = (d, 4 + d)[pair]
                            pe.wait_ge(*G.emptied(bank))
                            for p_ in range(2):
                                mm = pe.matmul(ps[bank][:, 256 * p_:256 * p_ + 256], kz[:, pair, p_, t],
                                               kq[:, :, pair, t], start=True, stop=True)
                            mm.then_inc(S["kk_psum"], 1)
                            kko[d] = G.filled(bank, "kk_out")
                    elif kind == "first":
                        pe.wait_ge(S["kk_out"], G.at("kk_out", kko[d]))
                        pe.wait_ge(*G.emptied(d))
                        for h in range(4):
                            mm = pe.matmul(ps[d][:, P * h:P * h + P], AT[d][:, h, :], ident, start=True, stop=True)
                        mm.then_inc(S["y_psum"], 1)
                        tu[d] = G.filled(d, "tu")
                    elif kind == "Y":
                        pe.wait_ge(S["tu"], G.at("tu", tu[d]))
                        pe.wait_ge(*G.emptied(d))
                        for h in range(4):
                            mm = pe.matmul(ps[d][:, P * h:P * h + P], AT[d][:, h, :], T[d][:, h, :],
                                           start=True, stop=True)
                        mm.then_inc(S["y_psum"], 1)
                        xo[d, "ym"] = G.filled(d, "ym")
                    elif kind == "dTU":
                        pe.wait_ge(S["ym"], G.at("ym", xo[d, "ym"]))
                        if k < LEVELS:
                            pe.wait_ge(*G.emptied(2 + d))
                            for h in range(4):
                                pe.matmul(ps[2 + d][:, P * h:P * h + P], U[d][:, h, :], Y[d][:, h, :],
                                          start=True, stop=True)
                        pe.wait_ge(*G.emptied(4 + d))
                        for h in range(4):
                            mm = pe.matmul(ps[4 + d][:, P * h:P * h + P], Y[d][:, h, :], U[d][:, h, :],
                                           start=True, stop=True)
                        mm.then_inc(S["dtu_psum"], 1)
                        tu[d] = G.filled([2 + d, 4 + d] if k < LEVELS else 4 + d, "tu")
                    elif kind == "X":
                        pe.wait_ge(S["tu"], G.at("tu", tu[d]))
                        pe.wait_ge(S["ke"], G.next("ke"))
                        pe.wait_ge(*G.emptied(d))
                        for h in range(4):
                            mm = pe.matmul(ps[d][:, HD * h:HD * h + HD], U[d][:, h, :],
                                           kvtok[:, tile, 256 + HD * h:256 + HD * h + HD], start=True, stop=True)
                        mm.then_inc(S["x_psum"], 1)
                        G.filled(d, "x_out")
                        pe.wait_ge(*G.emptied(2 + d))
                        for h in range(4):
                            half = HD * (h % 2)
                            mm = pe.matmul(ps[2 + d][half:half + HD, P * (h // 2):P * (h // 2) + P],
                                           E[d].rearrange("p a b -> p (a b)")[:, HD * h:HD * h + HD],
                                           U[d][:, h, :], start=True, stop=True)
                        mm.then_inc(S["x_psum"], 1)
                        xo[d, i] = G.filled(2 + d, "x_out")
                    elif kind == "ru":
                        pe.wait_ge(S["x_out"], G.at("x_out", xo[d, i]))
                        if (i, k) != (0, 0):
                            pe.wait_ge(S["gdn_s"], G.at("gdn_s", G.seen("gdn_s") - 1 + d))
                        bank = bank67()
                        pe.wait_ge(*G.emptied(bank))
                        for pair in range(2):
                            mm = pe.matmul(ps[bank][r, P * pair:P * pair + P], xk[:, pair, r], state[:, d, pair, :],
                                           start=True, stop=True)
                        mm.then_inc(S["ru_psum"], 1)
                        xo[d, "u"] = G.filled(bank, "gdn_u")
                    elif kind == "ro":
                        pe.wait_ge(S["gdn_u"], G.at("gdn_u", xo[d, "u"]))
                        if k == 0:
                            pe.wait_ge(S["qg"], G.next("qg"))
                            pe.wait_ge(S["kd"], G.next("kd"))
                        bank = bank67()
                        if tile_needed(layer, tile):
                            pe.wait_ge(*G.emptied(bank))
                        for pair in range(2 if tile_needed(layer, tile) else 0):
                            pe.matmul(ps[bank][:, HD * pair:HD * pair + HD], state[:, d, pair, :], qg_[:, pair, r],
                                      start=True, stop=False, skip_group_check=True)
                            for p_ in range(2):
                                h = 2 * pair + p_
                                half = HD * p_
                                mm = pe.matmul(ps[bank][half:half + HD, HD * pair:HD * pair + HD],
                                               ubuf[r, d, HD * h:HD * h + HD], pt[r, h, r],
                                               start=False, stop=True, skip_group_check=True)
                        if tile_needed(layer, tile):
                            mm.then_inc(S["ro_psum"], 1)
                            G.filled(bank, "gdn_o")
                        bank = bank67()
                        pe.wait_ge(*G.emptied(bank))
                        for pair in range(2):
                            mm = pe.matmul(ps[bank][:, P * pair:P * pair + P],
                                           kd_[r, 2 * pair:2 * pair + 2, :].rearrange("p a b -> p (a b)"),
                                           ubuf[r, d, P * pair:P * pair + P], start=True, stop=True)
                        mm.then_inc(S["rw_psum"], 1)
                        G.filled(bank, "gdn_s")

            def gla(layer):
                gu_ = pr("gate_up", 512, 512 * layer, 32)
                for d in range(2):
                    for ch in range(2):
                        pe.wait_ge(*G.emptied(2 * d + ch))
                        mm = pe.matmul(ps[2 * d + ch][:, :], gu_[:, 256 * d + P * ch:256 * d + P * ch + P], glow,
                                       start=True, stop=True)
                        mm.then_inc(S["gate_psum"], 1)
                        G.filled(2 * d + ch, "gate_x")
                early_modulation(layer, "gla")
                for d in range(2):
                    pe.wait_ge(S["gate_k"], G.next("gate_k", 2))
                    for hf in range(2):
                        pe.wait_ge(*G.emptied(4 + hf))
                        for tt in range(2):
                            tile = 2 * hf + tt
                            for pair in range(2):
                                mm = pe.transpose(ps[4 + hf][:, 256 * tt + P * pair:256 * tt + P * pair + P],
                                                  kp[:, d, pair, P * tile:P * tile + P], ident)
                        mm.then_inc(S["ktr_psum"], 1)
                        G.filled(4 + hf, "ktok")
                        pe.wait_ge(*G.emptied(6 + hf))
                        for tt in range(2):
                            for c in range(2):
                                t = slice(P * (2 * hf + tt) + CHUNK * c, P * (2 * hf + tt) + CHUNK * c + CHUNK)
                                for pair in range(2):
                                    o = 256 * tt + P * pair
                                    mm = pe.matmul(ps[6 + hf][CHUNK * c:CHUNK * c + CHUNK, o:o + P],
                                                   kp[:, d, pair, t], qz[:, d, pair, :, t], start=True, stop=True)
                        mm.then_inc(S["gs_psum"], 1)
                        G.filled(6 + hf, "gla_pt")
                pe.wait_ge(S["ktok"], G.now("ktok"))
                pe.wait_ge(S["gla_pt"], G.now("gla_pt"))
                n = 0
                for k in range(CHUNKS):
                    for d in range(2):
                        g = CHUNK_ORDER[d][k]
                        tile, c = g // 2, g % 2
                        r = slice(CHUNK * c, CHUNK * c + CHUNK)
                        t = slice(CHUNK * g, CHUNK * g + CHUNK)
                        bank = n % 4
                        pe.wait_ge(*G.emptied(bank))
                        for pair in range(2):
                            mm = pe.matmul(ps[bank][:, P * pair:P * pair + P], kt[r, d, tile, P * pair:P * pair + P],
                                           gv[r, tile, P * pair:P * pair + P], start=True, stop=True)
                        mm.then_inc(S["gw_psum"], 1)
                        G.filled(bank, "gla_s")
                        if k:
                            pe.wait_ge(S["gla_s"], G.at("gla_s", G.seen("gla_s") - 2))
                        n += 1
                        if not tile_needed(layer, tile):
                            continue
                        bank = 4 + (n - 1) % 4
                        pe.wait_ge(*G.emptied(bank))
                        for pair in range(2):
                            pe.matmul(ps[bank][:, HD * pair:HD * pair + HD], state[:, d, pair, :], qp[:, d, pair, t],
                                      start=True, stop=False, skip_group_check=True)
                            for p_ in range(2):
                                h, half = 2 * pair + p_, HD * p_
                                mm = pe.matmul(ps[bank][half:half + HD, HD * pair:HD * pair + HD],
                                               gv[r, tile, HD * h:HD * h + HD], pg[r, d, tile, h, :],
                                               start=False, stop=True, skip_group_check=True)
                        mm.then_inc(S["go_psum"], 1)
                        G.filled(bank, "gla_o")

            def closing(layer):
                t0, t1 = h_range(layer)
                early_modulation(layer, "closing")
                for m in range(4):
                    pe.wait_ge(S["fin_sq"], G.next("fin_sq"))
                    pe.wait_ge(*G.emptied(m))
                    mm = pe.matmul(ps[m][:, 0:t1 - t0], headones, fsq[:, m, t0:t1], start=True, stop=True)
                    mm.then_inc(S["fin_psum"], 1)
                    G.filled(m, "fin_rs")

            def out_projection(layer):
                t0, t1 = h_range(layer)
                pe.wait_ge(S["mix"], G.next("mix", 4))
                pe.wait_ge(S["att_out"], G.now("att_out"))
                for i in range(4):
                    s = [block_in(), block_in()]
                    w = [ring[:, x, :].rearrange("p (k c) -> p k c", k=4) for x in s]
                    for half in range(2):
                        bank = (2 * i + half) % 4
                        pe.wait_ge(*G.emptied(bank))
                        for k in range(KD):
                            mm = pe.matmul(ps[bank][:, 0:t1 - t0], w[k // 4][:, k % 4, P * half:P * half + P],
                                           aT[:, k, t0:t1], start=(k == 0), stop=(k == KD - 1))
                            if k == 0:
                                pay(mm)
                            if half == 1 and k == 3:
                                release(mm)
                        mm.then_inc(S["wout_psum"], 1)
                        G.filled(bank, "h_mix")
                        if half == 1:
                            release_next()

            def dense_ffn():
                base, act0 = G.seen("a"), G.seen("gu_act")
                for j in range(11):
                    banks = [4 * (j % 2) + x for x in range(4)]
                    for b in banks:
                        pe.wait_ge(*G.emptied(b))
                    for kb in range(2):
                        for u in range(2):
                            s = block_in()
                            w = ring[:, s, :].rearrange("p (k c) -> p k c", k=4)
                            for x in range(2):
                                for k4 in range(4):
                                    k = 4 * kb + k4
                                    if j == 0 and x == 0:
                                        pe.wait_ge(S["a"], G.at("a", base + k + 1))
                                    mm = pe.matmul(ps[banks[2 * u + x]][:, :], w[:, k4, P * x:P * x + P],
                                                   aT[:, k, :], start=(k == 0), stop=(k == KD - 1))
                                    if x == 0 and k4 == 0:
                                        pay(mm)
                            if kb == 0:
                                release(mm)
                            elif u == 0:
                                mm.then_inc(S["gu_psum"], 1)
                                release_next()
                    mm.then_inc(S["gu_psum"], 1)
                    G.filled(banks, "gu_act", 2)
                    release_next()
                G.n["a"] = base + KD
                for b in range(8):
                    pe.wait_ge(*G.emptied(b))
                for f in range(FC):
                    s = block_in()
                    pe.wait_ge(S["gu_act"], G.at("gu_act", act0 + f + 1))
                    for m in range(KD):
                        mm = pe.matmul(ps[m][:, :], ring[:, s, P * m:P * m + P], act[:, f, :],
                                       start=(f == 0), stop=(f == FC - 1))
                        if f == FC - 1:
                            mm.then_inc(S["down_psum"], 1)
                            G.filled(m, "h_ffn")
                        elif m == 0:
                            pay(mm)
                    if f < FC - 1:
                        release(mm)
                release_next()

            def routing():
                base = G.seen("a")
                pe.wait_ge(*G.emptied(0))
                for tile in range(2):
                    t = slice(STREAM + P * tile, STREAM + P * tile + P)
                    for k in range(KD):
                        pe.wait_ge(S["a"], G.at("a", base + k + 1))
                        mm = pe.matmul(ps[0][:, 8 * tile:8 * tile + 8], aT[:, k, t], pr("router", 8, 8 * k),
                                       start=(k == 0), stop=(k == KD - 1))
                mm.then_inc(S["logit_psum"], 1)
                G.filled(0, "top")
                G.n["a"] = base + KD
                for n in range(4):
                    tile, hf = n // 2, n % 2
                    t = slice(STREAM + P * tile, STREAM + P * tile + P)
                    pe.wait_ge(*G.emptied(1 + n))
                    for q in range(4):
                        mm = pe.transpose(ps[1 + n][:, P * q:P * q + P], aT[:, 4 * hf + q, t], ident)
                    mm.then_inc(S["bT_psum"], 1)
                    G.filled(1 + n, "btok")
                pe.wait_ge(S["mask"], G.next("mask", 2))
                pe.wait_ge(*G.emptied(0))
                pe.matmul(ps[0][:, 0:8], pr("ranktri"), rtop[:, 0, 3, :], start=True, stop=True)
                pe.matmul(ps[0][:, 8:16], ones, rtop[:, 0, 3, :], start=True, stop=False)
                pe.matmul(ps[0][:, 8:16], pr("ranktri"), rtop[:, 1, 3, :], start=False, stop=True)
                pe.matmul(ps[0][:, 16:24], ones, rtop[:, 0, 3, :], start=True, stop=False)
                mm = pe.matmul(ps[0][:, 16:24], ones, rtop[:, 1, 3, :], start=False, stop=True)
                mm.then_inc(S["rank_psum"], 1)
                G.filled(0, "flag")
                pe.wait_ge(S["btok"], G.now("btok"))

            def slot_tables():
                pe.wait_ge(S["gw"], G.next("gw"))
                for n in range(4):
                    pe.wait_ge(*G.emptied(1 + n))
                    for q in range(4):
                        e, tile = 2 * n + q // 2, q % 2
                        mm = pe.transpose(ps[1 + n][:, P * q:P * q + P], gwt[:, tile, e, :], ident)
                    mm.then_inc(S["gT_psum"], 1)
                    G.filled(1 + n, "smat")
                pe.wait_ge(S["smat"], G.now("smat"))

            def expert(e):
                for hf in range(2):
                    pe.wait_ge(*G.emptied(6 + hf))
                    for q in range(4):
                        k = 4 * hf + q
                        for tile in range(2):
                            mm = pe.matmul(ps[6 + hf][:, P * q:P * q + P], btok[:, tile, P * k:P * k + P],
                                           gm[:, tile, e, :], start=(tile == 0), stop=(tile == 1))
                            if q == 0 and tile == 0:
                                pay(mm)
                    mm.then_inc(S["xe_psum"], 1)
                    got = G.filled(6 + hf, "xe")
                evac = {}
                tr = {}

                def transposes(j):
                    pe.wait_ge(S["mgu_act"], G.at("mgu_act", evac[j]))
                    bank = 3 + j % 2
                    pe.wait_ge(*G.emptied(bank))
                    for q in range(2):
                        mm = pe.transpose(ps[bank][:, P * q:P * q + P], mact[:, 256 * j + P * q:256 * j + P * q + P],
                                          ident)
                    mm.then_inc(S["aT_psum"], 1)
                    tr[j] = G.filled(bank, "aT_sb")

                for j in range(11):
                    bank = j % 3
                    pe.wait_ge(*G.emptied(bank))
                    for kb in range(2):
                        s = [block_in(), block_in()]
                        if j == 0:
                            pe.wait_ge(S["xe"], G.at("xe", got - (1 - kb)))
                        for k4 in range(4):
                            k = 4 * kb + k4
                            if s[1] == s[0] + 1:
                                w = ring[:, s[0]:s[0] + 2, 256 * k4:256 * k4 + 256]
                                mm = pe.matmul(ps[bank][:, :], xe[:, k, :], w, start=(k == 0), stop=(k == KD - 1),
                                               skip_group_check=True)
                                if k4 == 0:
                                    pay(mm)
                                if k4 == 1:
                                    pay(mm)
                            else:
                                for u in range(2):
                                    w = ring[:, s[u], 256 * k4:256 * k4 + 256]
                                    mm = pe.matmul(ps[bank][:, 256 * u:256 * u + 256], xe[:, k, :], w,
                                                   start=(k == 0 and u == 0), stop=(k == KD - 1),
                                                   skip_group_check=True)
                                    if k4 == 0:
                                        pay(mm)
                        if kb == 0:
                            release(mm)
                            release_next()
                    mm.then_inc(S["mgu_psum"], 1)
                    evac[j] = G.filled(bank, "mgu_act")
                    release_next()
                    release_next()
                    if j >= 2:
                        transposes(j - 2)
                transposes(9)
                transposes(10)
                pe.wait_ge(*G.emptied(5))
                pe.wait_ge(*G.emptied(0))
                for f in range(FC):
                    s = block_in()
                    if f % 2 == 0:
                        pe.wait_ge(S["aT_sb"], G.at("aT_sb", tr[f // 2]))
                    for n, bank in enumerate((5, 0)):
                        mm = pe.matmul(ps[bank][:, :], mactT[:, f, :], ring[:, s, 512 * n:512 * n + 512],
                                       start=(f == 0), stop=(f == FC - 1))
                        if f == FC - 1:
                            mm.then_inc(S["y2_psum"], 1)
                            got = G.filled(bank, "y2")
                        elif n == 0:
                            pay(mm)
                    if f < FC - 1:
                        release(mm)
                release_next()
                for g in range(4):
                    bank = 1 + g % 2 if g < 2 else 6 + g % 2
                    pe.wait_ge(S["y2"], G.at("y2", got - (1 if g < 2 else 0)))
                    pe.wait_ge(*G.emptied(bank))
                    for q in range(2):
                        m = 2 * g + q
                        mm = pe.matmul(ps[bank][:, STREAM * q:STREAM * q + STREAM], y2[:, P * m:P * m + P],
                                       sm[:, e, :], start=True, stop=True)
                        if q == 0:
                            pay(mm)
                    mm.then_inc(S["sc_psum"], 1)
                    G.filled(bank, "h_ffn")

            def experts():
                slot_tables()
                G.begin()
                expert(0)
                after = count[0]
                with pe.Fori(1, EXPERTS) as e:
                    G.repeat(e)
                    count[0] = after - 66
                    expert(e)
                G.end(EXPERTS)
                count[0] = after + 66 * (EXPERTS - 1)

            pe.wait_ge(S["head_in"], 16)
            pe.wait_ge(S["cond"], G.next("cond"))
            for layer in range(LAYERS):
                if layer == 0:
                    modulation(0, MOD_BLOCKS, 0, MOD_BLOCKS - 1)
                    pe.wait_ge(S["params_in"], 16)
                modulation_end()
                sum_over_features(0, TOK)
                projections(layer)
                attention(layer)
                gdn_prepare(layer)
                gdn(layer)
                gla(layer)
                closing(layer)
                out_projection(layer)
                sum_over_features(*h_range(layer))
                if layer == 0:
                    dense_ffn()
            routing()
            experts()
            pe.wait_ge(S["flag"], 1)
            over = pe.value_load(flag[0:1, 0:1], min_val=0, max_val=1)
            with pe.If(over > 0):
                experts()

        @block.scalar
        def _(sc):
            G = Counts(S)
            act_ = sc.activation

            def mod_row(i):
                sc.wait_ge(S["mod_psum"], G.next("mod_psum"))
                sc.copy(mrow[:, :], ps[6 + i % 2][0:2, :]).then_inc(S["mod_row"], G.up("mod_row"))

            def early_row(layer, place, n):
                first, last = MOD_PLACES[place]
                if layer + 1 < LAYERS and first + n < last:
                    mod_row(first + n)

            def norm(t0, t1, source):
                for k in range(KD):
                    if source:
                        sc.wait_ge(S[source], G.next(source))
                    act_(nsq[:, k, t0:t1], hT[:, k, t0:t1], ACT.Square).then_inc(S["sq"], G.up("sq"))
                sc.wait_ge(S["sumsq_psum"], G.next("sumsq_psum"))
                act_(ps[5][:, 0:t1 - t0], ps[5][:, 0:t1 - t0], ACT.Ln, bias=eps, scale=1.0 / D).then_inc(
                    S["act_step"], G.up("act_step"))
                sc.wait_ge(S["act_step"], G.now("act_step"))
                act_(rstd_buf(t1 - t0), ps[5][:, 0:t1 - t0], ACT.Exp, scale=-0.5).then_inc(S["rstd"], G.up("rstd"))

            def att_squares(layer):
                sc.wait_ge(S["projd"], G.at("projd", 12 * layer + 3))
                sc.wait_ge(S["proja"], G.now("proja"))
                for i in range(TILES):
                    act_(asq[:, i, :, :], att[:, i, 0:10, :], ACT.Square).then_inc(S["att_sq"], G.up("att_sq"))

            def att_rstd():
                sc.wait_ge(S["att_ss"], G.next("att_ss"))
                act_(ssq[:, :, :], ssq[:, :, :], ACT.Ln, bias=eps, scale=1.0 / HD).then_inc(
                    S["act_step"], G.up("act_step"))
                sc.wait_ge(S["act_step"], G.now("act_step"))
                act_(ssq[:, :, :], ssq[:, :, :], ACT.Exp, scale=-0.5).then_inc(S["att_rstd"], G.up("att_rstd"))

            def projections(layer):
                for n, (name, _, by_token) in enumerate(IN_BLOCKS):
                    sc.wait_ge(S["proja_psum"], G.next("proja_psum"))
                    if name in ("gdn0",):
                        sc.wait_ge(S["cin_zero"], G.next("cin_zero"))
                    sc.copy(proj_dst(name, 1), proj_src(name, 5 + n % 2)).then_inc(S["proja"], G.up("proja"))
                    if n == 5:
                        sc.wait_ge(S["proja_psum"], G.next("proja_psum"))
                        sc.copy(glow, ps[7][0:32, :]).then_inc(S["proja"], G.up("proja"))
                    if n == 4:
                        att_squares(layer)
                    if n == 6:
                        att_rstd()

            def attention(layer):
                sc.wait_ge(S["kz_zero"], G.next("kz_zero"))
                for i in range(TILES):
                    if i == 2:
                        for n in range(2):
                            early_row(layer, "attention", n)
                    sc.wait_ge(S["kT_psum"], G.next("kT_psum"))
                    t = slice(P * i, P * i + P)
                    sc.copy(akz[0:HD, 0, t], ps[4][0:HD, 0:P])
                    sc.copy(akz[HD:P, 1, t], ps[4][HD:P, 0:P]).then_inc(S["kz"], G.up("kz"))
                units = att_units(layer)
                for i in range(len(units) + 2):
                    if i < len(units):
                        nk = units[i][2]
                        sc.wait_ge(S["smax"], G.next("smax"))
                        act_(Pb[:, i % 3, 0:P * nk], ps[SCORE_BANK[i % 3]][:, 0:P * nk], ACT.Exp,
                             bias=nmx[:, i:i + 1], accum_out=rsum[:, i:i + 1]).then_inc(S["att_exp"], G.up("att_exp"))
                    if i >= 2:
                        nk = units[i - 2][2]
                        sc.wait_ge(S["pT_psum"], G.next("pT_psum"))
                        sc.copy(PTb[:, i % 2, 0:nk, :],
                                      ps[2 + i % 2][:, 0:P * nk].rearrange("p (a b) -> p a b", a=nk)).then_inc(
                                          S["pT"], G.up("pT"))

            def gdn_prepare(layer):
                sc.wait_ge(S["gx"], G.next("gx"))
                x_, l_ = gsm[:, 0, :, :], gsm[:, 1, :, :]
                act_(l_, x_, ACT.Abs).then_inc(S["act_step"], G.up("act_step"))
                sc.wait_ge(S["act_step"], G.now("act_step"))
                act_(l_, l_, ACT.Exp, scale=-1.0).then_inc(S["act_step"], G.up("act_step"))
                sc.wait_ge(S["act_step"], G.now("act_step"))
                act_(l_, l_, ACT.Ln, bias=one)
                act_(gsm[:, 2, 0, :], pr("alog", 8, 8 * layer), ACT.Exp)
                act_(gsm[:, 3, :, :], ab[:, :, 8:16], ACT.Exp, scale=-1.0).then_inc(S["g_act"], G.up("g_act"))
                for c in range(6):
                    sc.wait_ge(S["conv"], G.next("conv"))
                    act_(ce[:, c, :, :], cv[:, c, :, :], ACT.Exp, scale=-1.0).then_inc(S["conv_exp"], G.up("conv_exp"))
                    early_row(layer, "gdn", c)
                for n, c in enumerate((2, 3, 0, 1)):
                    sc.wait_ge(S["qk_ss_psum"], G.next("qk_ss_psum"))
                    act_(crn[:, c, :], ps[n % 2][:, :], ACT.Ln, bias=eps).then_inc(S["act_step"], G.up("act_step"))
                    sc.wait_ge(S["act_step"], G.now("act_step"))
                    act_(crn[:, c, :], crn[:, c, :], ACT.Exp, scale=-0.5).then_inc(S["qk_rn"], G.up("qk_rn"))
                sc.wait_ge(S["gscan_psum"], G.next("gscan_psum"))
                act_(eg[:, :, :, :].rearrange("p a b c -> p (a b c)"), ps[4][:, 0:64], ACT.Exp).then_inc(
                    S["eg"], G.up("eg"))
                for tile in range(TILES):
                    sc.wait_ge(S["kvT_psum"], G.next("kvT_psum"))
                    sc.copy(kvtok[:, tile, :], ps[2 + tile % 2][:, :]).then_inc(S["kvtok"], G.up("kvtok"))

            def gdn(layer):
                misc = [0]
                for kind, d, i, k in gdn_order():
                    pt, xv, xk, kd_, qg_ = slot(d, i)
                    if kind == "decay":
                        sc.wait_ge(S["dec_psum"], G.next("dec_psum"))
                        act_(E[d].rearrange("p a b -> p (a b)"), ps[4 + d][:, :], ACT.Exp).then_inc(
                            S["decE"], G.up("decE"))
                        sc.wait_ge(S["dec_psum"], G.next("dec_psum"))
                        act_(Y[d].rearrange("p a b -> p (a b)"), ps[2 + d][:, :], ACT.Exp).then_inc(
                            S["decB"], G.up("decB"))
                    elif kind == "X":
                        sc.wait_ge(S["x_psum"], G.next("x_psum"))
                        sc.copy(xv, ps[d][:, 0:256]).then_inc(S["x_out"], G.up("x_out"))
                        sc.wait_ge(S["x_psum"], G.next("x_psum"))
                        sc.copy(xk.rearrange("p a b -> p (a b)"), ps[2 + d][:, 0:256]).then_inc(
                            S["x_out"], G.up("x_out"))
                    elif kind == "ru":
                        misc[0] += 1
                    elif kind == "ro":
                        misc[0] += 1
                        bank = 6 + misc[0] % 2
                        misc[0] += 1
                        c = k if d == 0 else 1 - k
                        t0 = P * TILE_ORDER[d][i] + CHUNK * c
                        if not tile_needed(layer, TILE_ORDER[d][i]):
                            continue
                        sc.wait_ge(S["ro_psum"], G.next("ro_psum"))
                        sc.copy(og[:, d, :, t0:t0 + CHUNK],
                                      ps[bank][:, 0:P].rearrange("p (a b) -> p a b", a=2)).then_inc(
                                          S["gdn_o"], G.up("gdn_o"))

            def gla(layer):
                def log_part(n):
                    w = gw_[:, n % 2]
                    l_ = w[:, 1, :]
                    sc.wait_ge(S["gate_x"], G.next("gate_x"))
                    act_(l_, w[:, 0, :], ACT.Abs).then_inc(S["act_step"], G.up("act_step"))
                    sc.wait_ge(S["act_step"], G.now("act_step"))
                    act_(l_, l_, ACT.Exp, scale=-1.0).then_inc(S["act_step"], G.up("act_step"))
                    sc.wait_ge(S["act_step"], G.now("act_step"))
                    act_(l_, l_, ACT.Ln, bias=one).then_inc(S["gate_ln"], G.up("gate_ln"))

                def exponentials(n):
                    w = gw_[:, n % 2]
                    sc.wait_ge(S["gate_D"], G.next("gate_D"))
                    act_(w[:, 2, :], w[:, 3, :], ACT.Exp, scale=1.0)
                    act_(w[:, 1, :], w[:, 3, :], ACT.Exp, scale=-1.0).then_inc(S["gate_E"], G.up("gate_E"))
                    early_row(layer, "gla", n)

                for d in range(2):
                    log_part(2 * d)
                    log_part(2 * d + 1)
                    exponentials(2 * d)
                    exponentials(2 * d + 1)
                sc.wait_ge(S["gate_f"], G.next("gate_f"))
                act_(gfac[:, 2:4, :, :, :].rearrange("p a b c d -> p (a b c d)"),
                           gfac[:, 0:2, :, :, :].rearrange("p a b c d -> p (a b c d)"), ACT.Exp).then_inc(
                               S["gate_fe"], G.up("gate_fe"))
                for d in range(2):
                    for hf in range(2):
                        sc.wait_ge(S["ktr_psum"], G.next("ktr_psum"))
                        sc.copy(kt[:, d, 2 * hf:2 * hf + 2, :],
                                      ps[4 + hf][:, :].rearrange("p (a b) -> p a b", a=2)).then_inc(
                                          S["ktok"], G.up("ktok"))
                n = 0
                for k in range(CHUNKS):
                    for d in range(2):
                        t0 = CHUNK * CHUNK_ORDER[d][k]
                        n += 1
                        if not tile_needed(layer, t0 // P):
                            continue
                        sc.wait_ge(S["go_psum"], G.next("go_psum"))
                        sc.copy(ol[:, d, :, t0:t0 + CHUNK],
                                      ps[4 + (n - 1) % 4][:, 0:P].rearrange("p (a b) -> p a b", a=2)).then_inc(
                                          S["gla_o"], G.up("gla_o"))

            def closing(layer):
                t0, t1 = h_range(layer)
                for m in range(4):
                    src = gr_ if m < 2 else gz
                    act_(fsg[:, m, t0:t1], src[:, m % 2, t0:t1], ACT.Exp, scale=-1.0).then_inc(
                        S["fin_e"], G.up("fin_e"))
                for n in range(2):
                    early_row(layer, "closing", n)
                for m in range(4):
                    sc.wait_ge(S["fin_psum"], G.next("fin_psum"))
                    act_(frs[:, m, t0:t1], ps[m][:, 0:t1 - t0], ACT.Ln, bias=eps, scale=1.0 / HD).then_inc(
                        S["act_step"], G.up("act_step"))
                    sc.wait_ge(S["act_step"], G.now("act_step"))
                    act_(frs[:, m, t0:t1], frs[:, m, t0:t1], ACT.Exp, scale=-0.5).then_inc(S["fin_rs"], G.up("fin_rs"))

            def dense_ffn():
                act0 = G.seen("gu_act")
                for j in range(11):
                    sc.wait_ge(S["gu_psum"], G.next("gu_psum"))
                    if j > 1:
                        sc.wait_ge(S["gu_act"], G.at("gu_act", act0 + 2 * (j - 1)))
                    for x in range(2):
                        m = act_(fe[:, 2 * (j % 2) + x, :], ps[4 * (j % 2) + x][:, :], ACT.Exp, scale=-1.0)
                    m.then_inc(S["gu_exp"], G.up("gu_exp"))
                    sc.wait_ge(S["gu_psum"], G.next("gu_psum"))
                G.n["gu_act"] = act0 + 22

            def routing():
                for n in range(4):
                    tile, hf = n // 2, n % 2
                    sc.wait_ge(S["bT_psum"], G.next("bT_psum"))
                    sc.copy(btok[:, tile, 512 * hf:512 * hf + 512], ps[1 + n][:, :]).then_inc(S["btok"], G.up("btok"))
                sc.wait_ge(S["top"], G.next("top"))
                act_(rtop[:, :, 4, 0:1], rtop[:, :, 4, 1:2], ACT.Exp).then_inc(S["top_e"], G.up("top_e"))

            def slot_tables():
                for n in range(4):
                    sc.wait_ge(S["gT_psum"], G.next("gT_psum"))
                    sc.copy(sm[:, 2 * n:2 * n + 2, :], ps[1 + n][:, :].rearrange("p (a b) -> p a b", a=2)).then_inc(
                        S["smat"], G.up("smat"))

            def expert(e):
                for hf in range(2):
                    sc.wait_ge(S["xe_psum"], G.next("xe_psum"))
                    sc.copy(xe[:, 4 * hf:4 * hf + 4, :], ps[6 + hf][:, :].rearrange("p (a b) -> p a b", a=4)).then_inc(
                        S["xe"], G.up("xe"))

                def copy_T(j):
                    sc.wait_ge(S["aT_psum"], G.next("aT_psum"))
                    sc.copy(mactT[:, 2 * j:2 * j + 2, :],
                                  ps[3 + j % 2][:, 0:256].rearrange("p (a b) -> p a b", a=2)).then_inc(
                                      S["aT_sb"], G.up("aT_sb"))

                for j in range(11):
                    sc.wait_ge(S["mgu_psum"], G.next("mgu_psum"))
                    if G.turn is not None or G.seen("mgu_act") > 1:
                        sc.wait_ge(S["mgu_act"], G.at("mgu_act", G.seen("mgu_act") - 1))
                    G.n["mgu_act"] = G.seen("mgu_act") + 1
                    act_(me[:, j % 2, :], ps[j % 3][:, 0:256], ACT.Exp, scale=-1.0).then_inc(
                        S["mgu_exp"], G.up("mgu_exp"))
                    if j >= 3:
                        copy_T(j - 3)
                for j in (8, 9, 10):
                    copy_T(j)
                for n, bank in enumerate((5, 0)):
                    sc.wait_ge(S["y2_psum"], G.next("y2_psum"))
                    sc.copy(y2[:, 512 * n:512 * n + 512], ps[bank][:, :]).then_inc(S["y2"], G.up("y2"))

            def experts():
                slot_tables()
                G.begin()
                expert(0)
                with sc.Fori(1, EXPERTS) as e:
                    G.repeat(e)
                    expert(e)
                G.end(EXPERTS)

            sc.wait_ge(S["head_in"], 16)
            act_(cond[:, :, :].rearrange("p a b -> p (a b)"), pr("cond"), ACT.Exp, scale=-1.0).then_inc(
                S["cond_exp"], G.up("cond_exp"))
            for i in range(MOD_BLOCKS):
                mod_row(i)
            sc.wait_ge(S["params_in"], 16)
            sc.wait_ge(S["x_in"], 16)
            for layer in range(LAYERS):
                norm(0, TOK, "h_ffn" if layer else None)
                projections(layer)
                attention(layer)
                gdn_prepare(layer)
                gdn(layer)
                gla(layer)
                closing(layer)
                norm(*h_range(layer), "h_mix")
                if layer == 0:
                    dense_ffn()
            routing()
            experts()
            sc.wait_ge(S["flag"], 1)
            over = sc.value_load(flag[0:1, 0:1], min_val=0, max_val=1)
            with sc.If(over > 0):
                experts()

        @block.vector
        def _(v):
            G = Counts(S)
            tt, ts, stt, cp = v.tensor_tensor, v.tensor_scalar, v.scalar_tensor_tensor, v.tensor_copy

            def mod_columns(layer, first, last):
                v.wait_ge(S["modT_psum"], G.next("modT_psum"))
                bm = rep(pr("bmod", 4 * (last - first), 48 * layer + 4 * first), 2, 2)
                tt(mcol[:, layer, 4 * first:4 * last, :],
                   ps[5][:, 8 * first:8 * last].rearrange("p (a b) -> p a b", b=2), bm,
                   ALU.add).then_inc(S["mod"], G.up("mod"))

            def early_columns(layer, place):
                if layer + 1 < LAYERS:
                    mod_columns(layer + 1, *MOD_TURNED[place])

            def modulation_end(layer):
                mod_columns(layer, MOD_BLOCKS - 1, MOD_BLOCKS)
                v.wait_ge(S["mod"], G.now("mod"))
                for w in range(2):
                    gain = rep(pr("norms", 8, 16 * layer + 8 * w), 2, 2)
                    m = stt(coef[:, w, :, :], mcol[:, layer, 24 * w + 8:24 * w + 16, :], 1.0, gain, ALU.add, ALU.mult)
                m.then_inc(S["dve_step"], G.up("dve_step"))
                v.wait_ge(S["dve_step"], G.now("dve_step"))

            def norm(layer, which, t0, t1):
                v.wait_ge(S["rstd"], G.next("rstd"))
                for k in range(KD):
                    tt(nhn[:, k, t0:t1], hT[:, k, t0:t1], rstd_buf(t1 - t0), ALU.mult).then_inc(
                        S["dve_step"], G.up("dve_step"))
                    v.wait_ge(S["dve_step"], G.now("dve_step"))
                    for s0 in range(t0, t1, STREAM):
                        st = 1 if s0 == 0 else 0
                        m = ts(aT[:, k, s0:s0 + STREAM], nhn[:, k, s0:s0 + STREAM], coef[:, which, k, st:st + 1],
                               mcol[:, layer, 24 * which + k, st:st + 1], ALU.mult, ALU.add)
                    m.then_inc(S["a"], G.up("a"))

            def att_sums():
                for i in range(TILES):
                    v.wait_ge(S["att_sq"], G.next("att_sq"))
                    m = v.tensor_reduce(ssq[:, i, :], asq[:, i, :, :], AX, ALU.add)
                m.then_inc(S["att_ss"], G.up("att_ss"))

            def att_norm(layer):
                v.wait_ge(S["att_rstd"], G.next("att_rstd"))
                for i in range(TILES):
                    tt(att[:, i, 0:10, :], att[:, i, 0:10, :], rep(ssq[:, i, :], 2, HD), ALU.mult).then_inc(
                        S["att_normed"], G.up("att_normed"))
                i = TILES - 1
                x = att[:, i, 0:10, :]
                v.wait_ge(S["att_normed"], G.now("att_normed"))
                for lo, hi, w in ((0, 8, 0), (8, 10, 64)):
                    gain = pr("qkgain", HD, 128 * layer + w)
                    m = tt(att[:, i, lo:hi, :], att[:, i, lo:hi, :], rep(gain, 1, hi - lo), ALU.mult)
                m.then_inc(S["dve_step"], G.up("dve_step"))
                v.wait_ge(S["dve_step"], G.now("dve_step"))
                tt(ra3, x, rep(pr("cos", HD, HD * (i - 2)), 1, 10), ALU.mult)
                x5 = x.rearrange("p h (w s c) -> p (h w) s c", w=2, s=2)
                r5 = rb3.rearrange("p h (w s c) -> p (h w) s c", w=2, s=2)
                s5 = pr("sin", HD, HD * (i - 2)).rearrange("p (w s c) -> p w s c", w=2, s=2)
                for s in range(2):
                    for w in range(2):
                        m = tt(r5[:, w:20:2, s, :], x5[:, w:20:2, 1 - s, :], rep(s5[:, w, s, :], 1, 10), ALU.mult)
                m.then_inc(S["dve_step"], G.up("dve_step"))
                v.wait_ge(S["dve_step"], G.now("dve_step"))
                tt(x, ra3, rb3, ALU.add).then_inc(S["qk_last"], G.up("qk_last"))

            def projections(layer):
                for n, (name, _, by_token) in enumerate(IN_BLOCKS):
                    v.wait_ge(S["projd_psum"], G.next("projd_psum"))
                    if name == "gdn0":
                        v.wait_ge(S["cin_zero"], G.next("cin_zero"))
                    cp(proj_dst(name, 0), proj_src(name, n % 2)).then_inc(S["projd"], G.up("projd"))
                    if n == 5:
                        v.wait_ge(S["projd_psum"], G.next("projd_psum"))
                        cp(ab[:, :, :].rearrange("p a b -> p (a b)"), ps[4][:, 0:64]).then_inc(S["projd"], G.up("projd"))
                    if n == 4:
                        att_sums()
                    if n == 7:
                        att_norm(layer)

            def conv_tap(layer, step):
                c, j = step // 5, step % 5
                if step == 0:
                    v.wait_ge(S["proja"], G.at("proja", 12 * layer + 6))
                tap = pr("conv", 1, 30 * layer + 5 * c + j)
                if j == 0:
                    m = ts(cv[:, c, :, :], cin[:, c, :, 0:256], tap, None, ALU.mult)
                else:
                    v.wait_ge(S["conv_tap"], G.now("conv_tap"))
                    m = stt(cv[:, c, :, :], cin[:, c, :, j:j + 256], tap, cv[:, c, :, :], ALU.mult, ALU.add)
                if j < 4:
                    m.then_inc(S["conv_tap"], G.up("conv_tap"))
                else:
                    m.then_inc(S["conv"], G.up("conv"))

            def attention(layer):
                for i in range(TILES):
                    if layer == 0 or i >= 2:
                        v.wait_ge(S["qT_psum"], G.next("qT_psum"))
                        ts(qT[:, :, P * i:P * i + P], ps[2 + i % 2][:, :].rearrange("p (a b) -> p a b", a=4),
                           HD ** -0.5, None, ALU.mult).then_inc(S["qT"], G.up("qT"))
                early_columns(layer, "attention")
                units = att_units(layer)
                taps = -(-30 // (len(units) + 4))
                for i in range(len(units) + 4):
                    for step in range(taps * i, min(taps * i + taps, 30)):
                        conv_tap(layer, step)
                    if i < len(units):
                        nk = units[i][2]
                        v.wait_ge(S["scores_psum"], G.next("scores_psum"))
                        v.tensor_reduce(nmx[:, i:i + 1], ps[SCORE_BANK[i % 3]][:, 0:P * nk], AX, ALU.max,
                                        negate=True).then_inc(S["smax"], G.up("smax"))
                    if 1 <= i <= len(units):
                        j = i - 1
                        nk = units[j][2]
                        v.wait_ge(S["att_exp"], G.next("att_exp"))
                        v.reciprocal(rsum[:, j:j + 1], rsum[:, j:j + 1]).then_inc(S["dve_step"], G.up("dve_step"))
                        v.wait_ge(S["dve_step"], G.now("dve_step"))
                        ts(Pb[:, j % 3, 0:P * nk], Pb[:, j % 3, 0:P * nk], rsum[:, j:j + 1], None, ALU.mult).then_inc(
                            S["att_p"], G.up("att_p"))
                    if i >= 4 and i % 4 == 3:
                        _, _, _, g, pair, lat, _ = units[i - 4]
                        v.wait_ge(S["pv_psum"], G.next("pv_psum"))
                        cp(aT[:, 4 + pair, STREAM * lat:STREAM * lat + STREAM], ps[4 + g % 2][:, 0:STREAM]).then_inc(
                            S["att_out"], G.up("att_out"))

            def gdn_prepare(layer):
                x_, l_ = gsm[:, 0, :, :], gsm[:, 1, :, :]
                v.wait_ge(S["projd"], G.now("projd"))
                tt(x_, ab[:, :, 0:8], rep(pr("dtb", 8, 8 * layer), 1, TILES), ALU.add).then_inc(S["gx"], G.up("gx"))
                early_columns(layer, "gdn")
                v.wait_ge(S["g_act"], G.next("g_act"))
                m = gsm[:, 5, :, :]
                ts(x_, x_, 0.0, None, ALU.max).then_inc(S["dve_step"], G.up("dve_step"))
                v.wait_ge(S["dve_step"], G.now("dve_step"))
                tt(x_, x_, l_, ALU.add).then_inc(S["dve_step"], G.up("dve_step"))
                v.wait_ge(S["dve_step"], G.now("dve_step"))
                stt(gsm[:, 4, :, :], x_, -1.0, rep(gsm[:, 2, 0, :], 1, TILES), ALU.mult, ALU.mult)
                ts(gsm[:, 3, :, :], gsm[:, 3, :, :], 1.0, None, ALU.add).then_inc(S["dve_step"], G.up("dve_step"))
                v.wait_ge(S["dve_step"], G.now("dve_step"))
                v.reciprocal(m, gsm[:, 3, :, :]).then_inc(S["g"], G.up("g"))
                for c in range(6):
                    v.wait_ge(S["conv_exp1"], G.next("conv_exp1"))
                    v.reciprocal(ce[:, c, :, :], ce[:, c, :, :]).then_inc(S["conv_rec"], G.up("conv_rec"))
                for n, c in enumerate((2, 3, 0, 1)):
                    v.wait_ge(S["qk_rn"], G.next("qk_rn"))
                    src = cv[:, c, :, :].rearrange("p a b -> p (a b)")
                    if c >= 2:
                        m = tt(kq[:, 0, c - 2, :], src, crn[:, c, :], ALU.mult)
                    else:
                        m = stt(kq[:, 1, c, :], src, HD ** -0.5, crn[:, c, :], ALU.mult, ALU.mult)
                    m.then_inc(S["kq"], G.up("kq"))

            def gdn(layer):
                misc = [0]
                v.memset(state[:, :, :, :], 0.0).then_inc(S["dve_step"], G.up("dve_step"))
                v.wait_ge(S["dve_step"], G.now("dve_step"))
                for kind, d, i, k in gdn_order():
                    pt, xv, xk, kd_, qg_ = slot(d, i)
                    if kind == "kk":
                        v.wait_ge(S["dtb"], G.next("dtb"))
                        for pair in range(2):
                            bank = (d, 4 + d)[pair]
                            v.wait_ge(S["kk_psum"], G.next("kk_psum"))
                            src = ps[bank][:, :].rearrange("p (h w t) -> p h w t", h=2, w=2)
                            h = slice(2 * pair, 2 * pair + 2)
                            tt(AT[d][:, h, :], src[:, :, 0, :], E[d][:, h, :], ALU.mult)
                            tt(pt[:, h, :], src[:, :, 1, :], E[d][:, h, :], ALU.mult).then_inc(
                                S["kk_out"], G.up("kk_out"))
                    elif kind == "first":
                        v.wait_ge(S["kk_out"], G.now("kk_out"))
                        stt(U[d], AT[d], -1.0, rep(level_mask(1 - d, 1), 1, 4), ALU.mult, ALU.mult).then_inc(
                            S["dve_step"], G.up("dve_step"))
                        v.wait_ge(S["dve_step"], G.now("dve_step"))
                        tt(U[d], U[d], rep(ident, 1, 4), ALU.add).then_inc(S["dve_step"], G.up("dve_step"))
                        v.wait_ge(S["dve_step"], G.now("dve_step"))
                        v.wait_ge(S["y_psum"], G.next("y_psum"))
                        stt(T[d], ps[d][:, :].rearrange("p (a b) -> p a b", a=4), -1.0,
                                   rep(level_mask(d, 1), 1, 4), ALU.mult, ALU.mult).then_inc(
                                       S["dve_step"], G.up("dve_step"))
                        v.wait_ge(S["dve_step"], G.now("dve_step"))
                        tt(T[d], T[d], rep(ident, 1, 4), ALU.add).then_inc(S["tu"], G.up("tu"))
                    elif kind == "Y":
                        if k == 2:
                            v.wait_ge(S["qg"], G.next("qg"))
                        v.wait_ge(S["y_psum"], G.next("y_psum"))
                        tt(Y[d], ps[d][:, :].rearrange("p (a b) -> p a b", a=4),
                                 rep(level_mask(d, k), 1, 4), ALU.mult).then_inc(S["ym"], G.up("ym"))
                    elif kind == "dTU":
                        v.wait_ge(S["dtu_psum"], G.next("dtu_psum"))
                        v.wait_ge(S["tu"], G.now("tu"))
                        if k < LEVELS:
                            tt(T[d], T[d], ps[2 + d][:, :].rearrange("p (a b) -> p a b", a=4), ALU.subtract)
                        tt(U[d], U[d], ps[4 + d][:, :].rearrange("p (a b) -> p a b", a=4), ALU.subtract).then_inc(
                            S["tu"], G.up("tu"))
                    elif kind == "ru":
                        misc[0] += 1
                        bank = 6 + misc[0] % 2
                        c = k if d == 0 else 1 - k
                        r = slice(CHUNK * c, CHUNK * c + CHUNK)
                        if k == 0:
                            v.wait_ge(S["x_out"], G.next("x_out", 2))
                        v.wait_ge(S["ru_psum"], G.next("ru_psum"))
                        tt(ubuf[r, d, :], xv[r, :], ps[bank][r, 0:256], ALU.subtract).then_inc(
                            S["gdn_u"], G.up("gdn_u"))
                    elif kind == "ro":
                        misc[0] += 2
                        bank = 6 + misc[0] % 2
                        c = k if d == 0 else 1 - k
                        if (i, k) != (0, 0):
                            v.wait_ge(S["gdn_s"], G.now("gdn_s"))
                        v.wait_ge(S["rw_psum"], G.next("rw_psum"))
                        for h in range(4):
                            half = slice(HD * (h % 2), HD * (h % 2) + HD)
                            m = stt(state[half, d, h // 2, half], state[half, d, h // 2, half],
                                    eend[half, d, i % 2, h, c:c + 1],
                                    ps[bank][half, P * (h // 2) + HD * (h % 2):P * (h // 2) + HD * (h % 2) + HD],
                                    ALU.mult, ALU.add)
                        m.then_inc(S["gdn_s"], G.up("gdn_s"))

            def gla(layer):
                v.wait_ge(S["gdn_s"], G.now("gdn_s"))
                v.memset(state[:, :, :, :], 0.0).then_inc(S["dve_step"], G.up("dve_step"))
                v.wait_ge(S["dve_step"], G.now("dve_step"))
                def gate_input(n):
                    v.wait_ge(S["gate_psum"], G.next("gate_psum"))
                    ts(gw_[:, n % 2, 0, :], ps[n][:, :], pr("gate_bias", 1, 4 * layer + n), None,
                       ALU.add).then_inc(S["gate_x"], G.up("gate_x"))

                def decay_sums(n):
                    d, ch = n // 2, n % 2
                    x_, l_, f_, d_ = (gw_[:, n % 2, q, :] for q in range(4))
                    v.wait_ge(S["gate_x"], G.now("gate_x"))
                    ts(f_, x_, 0.0, 1.0 / 16.0, ALU.min, ALU.mult).then_inc(S["dve_step"], G.up("dve_step"))
                    v.wait_ge(S["dve_step"], G.now("dve_step"))
                    v.wait_ge(S["gate_ln"], G.next("gate_ln"))
                    stt(x_, l_, -1.0 / 16.0, f_, ALU.mult, ALU.add).then_inc(S["dve_step"], G.up("dve_step"))
                    v.wait_ge(S["dve_step"], G.now("dve_step"))
                    v.tensor_tensor_scan(f_, pr("scanmask"), x_, 0.0, ALU.mult,
                                         ALU.add).then_inc(S["dve_step"], G.up("dve_step"))
                    v.wait_ge(S["dve_step"], G.now("dve_step"))
                    fc = f_.rearrange("p (c t) -> p c t", c=CHUNKS)
                    if d == 0:
                        mid = fc[:, :, 31]
                        cp(gfac[:, 0, d, ch, :], mid)
                        tt(gfac[:, 1, d, ch, :], fc[:, :, 63], mid, ALU.subtract).then_inc(
                            S["dve_step"], G.up("dve_step"))
                        v.wait_ge(S["dve_step"], G.now("dve_step"))
                        src = fc
                    else:
                        tt(x_, f_, x_, ALU.subtract).then_inc(S["dve_step"], G.up("dve_step"))
                        v.wait_ge(S["dve_step"], G.now("dve_step"))
                        src = x_.rearrange("p (c t) -> p c t", c=CHUNKS)
                        mid = src[:, :, 32]
                        tt(gfac[:, 0, d, ch, :], fc[:, :, 63], mid, ALU.subtract)
                        cp(gfac[:, 1, d, ch, :], mid).then_inc(S["dve_step"], G.up("dve_step"))
                        v.wait_ge(S["dve_step"], G.now("dve_step"))
                    dc = d_.rearrange("p (c t) -> p c t", c=CHUNKS)
                    tt(dc, src, rep(mid, 2, CHUNK), ALU.subtract).then_inc(S["dve_step"], G.up("dve_step"))
                    v.wait_ge(S["dve_step"], G.now("dve_step"))
                    ts(d_, d_, 80.0, -80.0, ALU.min, ALU.max).then_inc(S["gate_D"], G.up("gate_D"))

                def decayed_qk(n):
                    d, ch = n // 2, n % 2
                    w = gw_[:, n % 2]
                    v.wait_ge(S["gate_E"], G.next("gate_E"))
                    eq, ek = (w[:, 2, :], w[:, 1, :]) if d == 0 else (w[:, 1, :], w[:, 2, :])
                    stt(qp[:, d, ch, :], gq[:, ch, :], HD ** -0.5, eq, ALU.mult, ALU.mult)
                    for p_ in range(2):
                        half = slice(HD * p_, HD * p_ + HD)
                        stt(qz[half, d, ch, p_, :], gq[half, ch, :], HD ** -0.5, eq[half, :], ALU.mult, ALU.mult)
                        other = slice(HD - HD * p_, 2 * HD - HD * p_)
                        v.memset(qz[other, d, ch, p_, :], 0.0)
                    tt(kp[:, d, ch, :], gk[:, ch, :], ek, ALU.mult).then_inc(S["gate_k"], G.up("gate_k"))

                gate_input(0)
                gate_input(1)
                for d in range(2):
                    for ch in range(2):
                        decay_sums(2 * d + ch)
                    for ch in range(2):
                        decayed_qk(2 * d + ch)
                        if d == 0:
                            gate_input(2 + ch)
                early_columns(layer, "gla")
                tt(gfac[:, 1, 0, :, 0:7], gfac[:, 1, 0, :, 0:7], gfac[:, 0, 0, :, 1:8], ALU.add).then_inc(
                    S["dve_step"], G.up("dve_step"))
                v.wait_ge(S["dve_step"], G.now("dve_step"))
                for a, b, n in ((1, 0, 3), (5, 4, 3), (0, 7, 1)):
                    m = tt(gfac[:, 1, 1, :, a:a + n], gfac[:, 1, 1, :, a:a + n], gfac[:, 0, 1, :, b:b + n], ALU.add)
                m.then_inc(S["gate_f"], G.up("gate_f"))
                v.wait_ge(S["gate_fe"], G.next("gate_fe"))
                for d in range(2):
                    for hf in range(2):
                        v.wait_ge(S["gs_psum"], G.next("gs_psum"))
                        tt(pg[:, d, 2 * hf:2 * hf + 2, :, :].rearrange("p a b c -> p (a b) c"),
                                 ps[6 + hf][:, :].rearrange("p (a b) -> p a b", a=8),
                                 rep(maskc[d], 1, 8), ALU.mult).then_inc(S["gla_pt"], G.up("gla_pt"))
                n = 0
                for k in range(CHUNKS):
                    for d in range(2):
                        g = CHUNK_ORDER[d][k]
                        bank = n % 4
                        v.wait_ge(S["gw_psum"], G.next("gw_psum"))
                        if tile_needed(layer, g // 2):
                            v.wait_ge(S["go_psum"], G.next("go_psum"))
                        for p_ in range(2):
                            half = slice(HD * p_, HD * p_ + HD)
                            m = tt(state[half, d, :, half], state[half, d, :, half],
                                   ps[bank][half, 0:256].rearrange("p (a b) -> p a b", a=2)[:, :, half], ALU.add)
                        m.then_inc(S["dve_step"], G.up("dve_step"))
                        v.wait_ge(S["dve_step"], G.now("dve_step"))
                        for pair in range(2):
                            m = ts(state[:, d, pair, :], state[:, d, pair, :], gfac[:, 3, d, pair, g:g + 1], None,
                                   ALU.mult)
                        m.then_inc(S["gla_s"], G.up("gla_s"))
                        v.wait_ge(S["gla_s"], G.now("gla_s"))
                        n += 1

            def closing(layer):
                t0, t1 = h_range(layer)
                for m_ in range(4):
                    v.wait_ge(S["fin_e1"], G.next("fin_e1"))
                    v.reciprocal(fsg[:, m_, t0:t1], fsg[:, m_, t0:t1]).then_inc(S["fin_rec"], G.up("fin_rec"))
                early_columns(layer, "closing")
                for m_ in range(4):
                    o = (ol if m_ < 2 else og)[:, 0, m_ % 2, t0:t1]
                    v.wait_ge(S["fin_rs"], G.next("fin_rs"))
                    stt(o, o, pr("gains", 1, 2 * layer + m_ // 2), frs[:, m_, t0:t1], ALU.mult, ALU.mult).then_inc(
                        S["dve_step"], G.up("dve_step"))
                    v.wait_ge(S["dve_step"], G.now("dve_step"))
                    v.wait_ge(S["fin_sg"], G.next("fin_sg"))
                    tt(aT[:, m_, t0:t1], o, fsg[:, m_, t0:t1], ALU.mult).then_inc(S["mix"], G.up("mix"))

            def add_to_h(layer, m_, which, t0, t1, psum):
                for s0 in range(t0, t1, STREAM):
                    st = 1 if s0 == 0 else 0
                    m = stt(hT[:, m_, s0:s0 + STREAM], psum[:, s0 - t0:s0 - t0 + STREAM],
                            mcol[:, layer, 24 * which + 16 + m_, st:st + 1], hT[:, m_, s0:s0 + STREAM], ALU.mult, ALU.add)
                return m

            def out_projection(layer):
                t0, t1 = h_range(layer)
                for m_ in range(KD):
                    v.wait_ge(S["wout_psum"], G.next("wout_psum"))
                    add_to_h(layer, m_, 0, t0, t1, ps[m_ % 4]).then_inc(S["h_mix"], G.up("h_mix"))
                v.wait_ge(S["h_mix"], G.now("h_mix"))

            def dense_ffn():
                for j in range(11):
                    v.wait_ge(S["gu_psum"], G.next("gu_psum", 2))
                    v.wait_ge(S["gu_exp"], G.next("gu_exp"))
                    b = 4 * (j % 2)
                    for x in range(2):
                        g = fe[:, 2 * (j % 2) + x, :]
                        ts(g, g, 1.0, None, ALU.add).then_inc(S["dve_step"], G.up("dve_step"))
                        v.wait_ge(S["dve_step"], G.now("dve_step"))
                        v.reciprocal(g, g).then_inc(S["dve_step"], G.up("dve_step"))
                        v.wait_ge(S["dve_step"], G.now("dve_step"))
                        tt(g, g, ps[b + x][:, :], ALU.mult).then_inc(S["dve_step"], G.up("dve_step"))
                        v.wait_ge(S["dve_step"], G.now("dve_step"))
                        tt(act[:, 2 * j + x, :], g, ps[b + 2 + x][:, :], ALU.mult).then_inc(S["gu_act"], G.up("gu_act"))
                for m_ in range(KD):
                    v.wait_ge(S["down_psum"], G.next("down_psum"))
                    add_to_h(0, m_, 1, 0, TOK, ps[m_]).then_inc(S["h_ffn"], G.up("h_ffn"))
                v.wait_ge(S["h_ffn"], G.now("h_ffn"))

            def routing():
                v.wait_ge(S["logit_psum"], G.next("logit_psum"))
                lg = rtop[:, :, 0, :]
                tt(lg, ps[0][:, 0:16].rearrange("p (a b) -> p a b", a=2), rep(pr("rbias"), 1, 2), ALU.add).then_inc(
                    S["dve_step"], G.up("dve_step"))
                v.wait_ge(S["dve_step"], G.now("dve_step"))
                for tile in range(2):
                    v.max(rtop[:, tile, 1, :], rtop[:, tile, 0, :]).then_inc(S["dve_step"], G.up("dve_step"))
                    v.wait_ge(S["dve_step"], G.now("dve_step"))
                    v.max_index(idx[:, tile, :], rtop[:, tile, 1, :], rtop[:, tile, 0, :]).then_inc(
                        S["dve_step"], G.up("dve_step"))
                    v.wait_ge(S["dve_step"], G.now("dve_step"))
                    cp(rtop[:, tile, 2, :], idx[:, tile, :]).then_inc(S["dve_step"], G.up("dve_step"))
                    v.wait_ge(S["dve_step"], G.now("dve_step"))
                tt(rtop[:, :, 4, 1:2], rtop[:, :, 1, 1:2], rtop[:, :, 1, 0:1],
                   ALU.subtract).then_inc(S["top"], G.up("top"))
                v.wait_ge(S["top"], G.now("top"))
                for tile in range(2):
                    i8 = pr("iota8")
                    o1, o2 = rtop[:, tile, 0, :], rtop[:, tile, 1, :]
                    ts(o1, i8, rtop[:, tile, 2, 0:1], None, ALU.is_equal)
                    ts(o2, i8, rtop[:, tile, 2, 1:2], None, ALU.is_equal).then_inc(S["dve_step"], G.up("dve_step"))
                    v.wait_ge(S["dve_step"], G.now("dve_step"))
                    tt(rtop[:, tile, 3, :], o1, o2, ALU.add).then_inc(S["mask"], G.up("mask"))
                v.wait_ge(S["top_e"], G.next("top_e"))
                ts(rtop[:, :, 4, 2:3], rtop[:, :, 4, 0:1], 1.0, None, ALU.add).then_inc(S["dve_step"], G.up("dve_step"))
                v.wait_ge(S["dve_step"], G.now("dve_step"))
                v.reciprocal(rtop[:, :, 4, 3:4], rtop[:, :, 4, 2:3]).then_inc(S["dve_step"], G.up("dve_step"))
                v.wait_ge(S["dve_step"], G.now("dve_step"))
                tt(rtop[:, :, 4, 4:5], rtop[:, :, 4, 3:4], rtop[:, :, 4, 0:1],
                   ALU.mult).then_inc(S["dve_step"], G.up("dve_step"))
                v.wait_ge(S["dve_step"], G.now("dve_step"))
                v.wait_ge(S["mask"], G.now("mask"))
                for tile in range(2):
                    o1, o2 = rtop[:, tile, 0, :], rtop[:, tile, 1, :]
                    ts(o1, o1, rtop[:, tile, 4, 3:4], None, ALU.mult)
                    ts(o2, o2, rtop[:, tile, 4, 4:5], None, ALU.mult).then_inc(S["dve_step"], G.up("dve_step"))
                    v.wait_ge(S["dve_step"], G.now("dve_step"))
                    tt(rtop[:, tile, 5, :], o1, o2, ALU.add).then_inc(S["dve_step"], G.up("dve_step"))
                    v.wait_ge(S["dve_step"], G.now("dve_step"))
                v.wait_ge(S["rank_psum"], G.next("rank_psum"))
                for tile in range(2):
                    sl = rtop[:, tile, 0, :]
                    ts(sl, ps[0][:, 8 * tile:8 * tile + 8], 1.0, None, ALU.add).then_inc(
                        S["dve_step"], G.up("dve_step"))
                    v.wait_ge(S["dve_step"], G.now("dve_step"))
                    tt(sl, sl, rtop[:, tile, 3, :], ALU.mult).then_inc(S["dve_step"], G.up("dve_step"))
                    v.wait_ge(S["dve_step"], G.now("dve_step"))
                    ts(sl, sl, -1.0, None, ALU.add).then_inc(S["dve_step"], G.up("dve_step"))
                    v.wait_ge(S["dve_step"], G.now("dve_step"))
                v.tensor_reduce(cnt[:, 0:1], ps[0][:, 16:24], AX, ALU.max).then_inc(S["dve_step"], G.up("dve_step"))
                v.wait_ge(S["dve_step"], G.now("dve_step"))
                ts(cnt[:, 1:2], cnt[:, 0:1], float(SLOTS), None, ALU.is_gt).then_inc(S["dve_step"], G.up("dve_step"))
                v.wait_ge(S["dve_step"], G.now("dve_step"))
                cp(flag[0:1, 0:1], cnt[0:1, 1:2]).then_inc(S["flag"], G.up("flag"))

            def slot_tables(second):
                for tile in range(2):
                    sl = rtop[:, tile, 0, :]
                    if second:
                        ts(sl, sl, -float(SLOTS), None, ALU.add).then_inc(S["dve_step"], G.up("dve_step"))
                        v.wait_ge(S["dve_step"], G.now("dve_step"))
                    for e in range(EXPERTS):
                        ts(gm[:, tile, e, :], pr("iota"), rtop[:, tile, 0, e:e + 1], None, ALU.is_equal)
                        m = ts(gwt[:, tile, e, :], pr("iota"), rtop[:, tile, 0, e:e + 1], rtop[:, tile, 5, e:e + 1],
                               ALU.is_equal, ALU.mult)
                m.then_inc(S["gw"], G.up("gw"))

            def expert(e):
                for j in range(11):
                    v.wait_ge(S["mgu_psum"], G.next("mgu_psum"))
                    v.wait_ge(S["mgu_exp"], G.next("mgu_exp"))
                    b = me[:, j % 2, :]
                    ts(b, b, 1.0, None, ALU.add).then_inc(S["dve_step"], G.up("dve_step"))
                    v.wait_ge(S["dve_step"], G.now("dve_step"))
                    v.reciprocal(b, b).then_inc(S["dve_step"], G.up("dve_step"))
                    v.wait_ge(S["dve_step"], G.now("dve_step"))
                    tt(b, b, ps[j % 3][:, 0:256], ALU.mult).then_inc(S["dve_step"], G.up("dve_step"))
                    v.wait_ge(S["dve_step"], G.now("dve_step"))
                    tt(mact[:, 256 * j:256 * j + 256], b, ps[j % 3][:, 256:512], ALU.mult).then_inc(
                        S["mgu_act"], G.up("mgu_act"))
                for g in range(4):
                    bank = 1 + g % 2 if g < 2 else 6 + g % 2
                    v.wait_ge(S["sc_psum"], G.next("sc_psum"))
                    for q in range(2):
                        m = add_to_h(LAYERS - 1, 2 * g + q, 1, STREAM, TOK, ps[bank][:, STREAM * q:STREAM * q + STREAM])
                    m.then_inc(S["h_ffn"], G.up("h_ffn"))
                    v.wait_ge(S["h_ffn"], G.now("h_ffn"))

            def experts(second):
                slot_tables(second)
                G.begin()
                expert(0)
                with v.Fori(1, EXPERTS) as e:
                    G.repeat(e)
                    expert(e)
                G.end(EXPERTS)

            def program():
                v.wait_ge(S["head_in"], 16)
                v.wait_ge(S["cond_exp"], G.next("cond_exp"))
                c_ = cond[:, :, :].rearrange("p a b -> p (a b)")
                ts(c_, c_, 1.0, None, ALU.add).then_inc(S["dve_step"], G.up("dve_step"))
                v.wait_ge(S["dve_step"], G.now("dve_step"))
                v.reciprocal(c_, c_).then_inc(S["dve_step"], G.up("dve_step"))
                v.wait_ge(S["dve_step"], G.now("dve_step"))
                tt(c_, c_, pr("cond"), ALU.mult).then_inc(S["cond"], G.up("cond"))
                v.wait_ge(S["params_in"], 16)
                for layer in range(LAYERS):
                    if layer == 0:
                        mod_columns(0, 0, MOD_BLOCKS - 1)
                    modulation_end(layer)
                    norm(layer, 0, 0, TOK)
                    projections(layer)
                    attention(layer)
                    gdn_prepare(layer)
                    gdn(layer)
                    gla(layer)
                    closing(layer)
                    out_projection(layer)
                    norm(layer, 1, *h_range(layer))
                    if layer == 0:
                        dense_ffn()
                routing()
                experts(False)
                v.wait_ge(S["flag"], 1)
                over = v.value_load(flag[0:1, 0:1], min_val=0, max_val=1)
                with v.If(over > 0):
                    experts(True)

            program()
            v.tensor_copy(osb, hT[:, :, STREAM:TOK]).then_inc(S["final"], 1)

        @block.gpsimd
        def _(pool):
            G = Counts(S)
            tt, ts, cp = pool.tensor_tensor, pool.tensor_scalar, pool.tensor_copy

            def zeros(layer):
                pool.wait_ge(S["a"], G.at("a", 16 * layer + 8))
                for q, w in ((0, 2), (258, 2)):
                    m = pool.memset(cin[:, :, :, q:q + w].rearrange("p a b c -> p (a b) c"), 0.0)
                m.then_inc(S["cin_zero"], G.up("cin_zero"))

            def attention(layer):
                pool.wait_ge(S["att_rstd"], G.next("att_rstd"))
                pool.memset(akz[HD:P, 0, :], 0.0).then_inc(S["pool_step"], G.up("pool_step"))
                pool.wait_ge(S["pool_step"], G.now("pool_step"))
                pool.memset(akz[0:HD, 1, :], 0.0).then_inc(S["kz_zero"], G.up("kz_zero"))
                pool.wait_ge(S["kz_zero"], G.now("kz_zero"))
                for i in range(TILES - 1):
                    pool.wait_ge(S["att_normed"], G.next("att_normed"))
                    for lo, hi, w in ((0, 8, 0), (8, 10, 64)):
                        gain = pr("qkgain", HD, 128 * layer + w)
                        m = tt(att[:, i, lo:hi, :], att[:, i, lo:hi, :], rep(gain, 1, hi - lo), ALU.mult)
                    if i >= 2:
                        m.then_inc(S["pool_step"], G.up("pool_step"))
                        pool.wait_ge(S["pool_step"], G.now("pool_step"))
                        x = att[:, i, 0:10, :]
                        cos = pr("cos", HD, HD * (i - 2))
                        sin = pr("sin", HD, HD * (i - 2))
                        tt(ra, x, rep(cos, 1, 10), ALU.mult)
                        x5 = x.rearrange("p h (w s c) -> p (h w) s c", w=2, s=2)
                        r5 = rb.rearrange("p h (w s c) -> p (h w) s c", w=2, s=2)
                        s5 = sin.rearrange("p (w s c) -> p w s c", w=2, s=2)
                        for s in range(2):
                            for w in range(2):
                                o = r5[:, w:20:2, s, :]
                                m = tt(o, x5[:, w:20:2, 1 - s, :], rep(s5[:, w, s, :], 1, 10), ALU.mult)
                        m.then_inc(S["pool_step"], G.up("pool_step"))
                        pool.wait_ge(S["pool_step"], G.now("pool_step"))
                        m = tt(x, ra, rb, ALU.add)
                    m.then_inc(S["qk"], G.up("qk"))
                    pool.wait_ge(S["qk"], G.now("qk"))
                G.n["att_normed"] += 1

            def gdn_prepare(layer):
                pool.wait_ge(S["conv"], G.next("conv", 6))
                pool.memset(kz[HD:P, :, 0, :], 0.0).then_inc(S["pool_step"], G.up("pool_step"))
                pool.wait_ge(S["pool_step"], G.now("pool_step"))
                pool.memset(kz[0:HD, :, 1, :], 0.0).then_inc(S["pool_step"], G.up("pool_step"))
                pool.wait_ge(S["pool_step"], G.now("pool_step"))
                for c in range(6):
                    pool.wait_ge(S["conv_exp"], G.next("conv_exp"))
                    ts(ce[:, c, :, :], ce[:, c, :, :], 1.0, None, ALU.add).then_inc(S["conv_exp1"], G.up("conv_exp1"))
                for c in (2, 3, 0, 1, 4, 5):
                    pool.wait_ge(S["conv_rec"], G.at("conv_rec", 6 * layer + c + 1))
                    tt(cv[:, c, :, :], cv[:, c, :, :], ce[:, c, :, :], ALU.mult).then_inc(S["convd"], G.up("convd"))
                    if c < 4:
                        pool.wait_ge(S["convd"], G.now("convd"))
                        x = cv[:, c, :, :].rearrange("p a b -> p (a b)")
                        tt(csq[:, c, :], x, x, ALU.mult).then_inc(S["qk_sq"], G.up("qk_sq"))
                pool.wait_ge(S["convd"], G.now("convd"))
                G.n["conv_rec"] = 6 * layer + 6
                pool.wait_ge(S["kq"], G.next("kq", 4))
                cp(kz[0:HD, :, 0, :], kq[0:HD, 0, :, :]).then_inc(S["pool_step"], G.up("pool_step"))
                pool.wait_ge(S["pool_step"], G.now("pool_step"))
                cp(kz[HD:P, :, 1, :], kq[HD:P, 0, :, :]).then_inc(S["kz2"], G.up("kz2"))
                pool.wait_ge(S["kz2"], G.now("kz2"))
                pool.wait_ge(S["eg"], G.next("eg"))
                for d in range(2):
                    m = tt(erb[:, d, :, :], eg[:, 2 + d, :, :], gsm[:, 5, :, 4 * d:4 * d + 4], ALU.mult)
                m.then_inc(S["pool_step"], G.up("pool_step"))
                pool.wait_ge(S["pool_step"], G.now("pool_step"))

            def gdn(layer):
                pool.wait_ge(S["kvtok"], G.next("kvtok", 4))
                pool.wait_ge(S["kz2"], G.now("kz2"))
                s0 = 16 * layer
                for kind, d, i, k in gdn_order():
                    tile = TILE_ORDER[d][i]
                    pt, xv, xk, kd_, qg_ = slot(d, i)
                    if kind == "decay":
                        g = gsm[:, 4, tile, 4 * d:4 * d + 4]
                        tt(Gr[d], rep(minc[d], 1, 4), rep(g, 2, P), ALU.mult).then_inc(S["gr"], G.up("gr"))
                    elif kind == "kk":
                        if i >= 2:
                            pool.wait_ge(S["gdn_s"], G.at("gdn_s", s0 + 4 * (i - 2) + 2 + d + 1))
                        beta = gsm[:, 5, tile, 4 * d:4 * d + 4]
                        tt(pt, rep(minc[d], 1, 4), rep(beta, 2, P), ALU.mult).then_inc(
                            S["pool_step"], G.up("pool_step"))
                        pool.wait_ge(S["pool_step"], G.now("pool_step"))
                        pool.wait_ge(S["decE"], G.next("decE"))
                        tt(E[d], E[d], pt, ALU.mult).then_inc(S["dtb"], G.up("dtb"))
                        pool.wait_ge(S["dtb"], G.now("dtb"))
                        pool.wait_ge(S["decB"], G.next("decB"))
                        for p_ in range(2):
                            half = slice(HD * p_, HD * p_ + HD)
                            tt(qg_[half, :, :], kq[half, 1, :, P * tile:P * tile + P], Y[d][half, p_:4:2, :], ALU.mult).then_inc(
                                S["pool_step"], G.up("pool_step"))
                            pool.wait_ge(S["pool_step"], G.now("pool_step"))
                        end = 63 if d == 0 else 0
                        cp(eend[:, d, i % 2, :, :], Y[d][:, :, end:P:CHUNK]).then_inc(S["qg"], G.up("qg"))
                        k_ = kvtok[:, tile, 0:256].rearrange("p (h e) -> p h e", h=4)
                        tt(kd_, k_, rep(erb[:, d, tile, :], 2, HD), ALU.mult).then_inc(S["kd"], G.up("kd"))
                    elif kind == "first":
                        pool.wait_ge(S["kk_out"], G.next("kk_out", 2))
                        k_ = kvtok[:, tile, 0:256].rearrange("p (h e) -> p h e", h=4)
                        ke = E[d].rearrange("p a b -> p (a b)")[:, 0:256].rearrange("p (h e) -> p h e", h=4)
                        tt(ke, k_, rep(eg[:, d, tile, :], 2, HD), ALU.mult).then_inc(S["ke"], G.up("ke"))

            def closing(layer):
                t0, t1 = h_range(layer)
                chunks = sum(tile_needed(layer, c // 2) for c in range(CHUNKS))
                pool.wait_ge(S["gla_o"], G.next("gla_o", 2 * chunks))
                pool.wait_ge(S["gdn_o"], G.next("gdn_o", 2 * chunks))
                for m_ in range(4):
                    src = ol if m_ < 2 else og
                    o = src[:, 0, m_ % 2, t0:t1]
                    tt(o, o, src[:, 1, m_ % 2, t0:t1], ALU.add).then_inc(S["pool_step"], G.up("pool_step"))
                    pool.wait_ge(S["pool_step"], G.now("pool_step"))
                    tt(fsq[:, m_, t0:t1], o, o, ALU.mult).then_inc(S["fin_sq"], G.up("fin_sq"))
                for m_ in range(4):
                    pool.wait_ge(S["fin_e"], G.next("fin_e"))
                    ts(fsg[:, m_, t0:t1], fsg[:, m_, t0:t1], 1.0, None, ALU.add).then_inc(S["fin_e1"], G.up("fin_e1"))
                for m_ in range(4):
                    src = gr_ if m_ < 2 else gz
                    pool.wait_ge(S["fin_rec"], G.next("fin_rec"))
                    tt(fsg[:, m_, t0:t1], fsg[:, m_, t0:t1], src[:, m_ % 2, t0:t1], ALU.mult).then_inc(
                        S["fin_sg"], G.up("fin_sg"))

            pool.wait_ge(S["params_in"], 16)
            for layer in range(LAYERS):
                zeros(layer)
                attention(layer)
                gdn_prepare(layer)
                gdn(layer)
                closing(layer)


def constants():
    r = np.arange(P)
    same = (r[:, None] // CHUNK) == (r[None, :] // CHUNK)
    c = {"ident": np.eye(P), "ones": np.ones((P, P)), "headones": same,
         "lt": np.concatenate([(r[:, None] > r[None, :]) & same, (r[:, None] < r[None, :]) & same], 1),
         "minc": np.concatenate([(r[:, None] <= r[None, :]) & same, (r[:, None] >= r[None, :]) & same], 1)}
    levels = []
    for d in range(2):
        for l in range(LEVELS):
            s = 1 << l
            m = (r[:, None] // (2 * s) == r[None, :] // (2 * s)) & (r[:, None] // s % 2 == 1) & (r[None, :] // s % 2 == 0)
            levels.append(m if d == 0 else m.T)
    c["level"] = np.concatenate(levels, 1)
    c["ranktri"] = r[:, None] < r[None, :]
    t = np.arange(CHUNK)
    s = (r % CHUNK)[:, None]
    c["maskc"] = np.concatenate([s <= t[None, :], s >= t[None, :]], 1)
    c["iota"] = np.tile(r, (P, 1))
    c["iota8"] = np.tile(np.arange(8), (P, 1))
    c["scanmask"] = np.tile((np.arange(TOK) % CHUNK != 0), (P, 1))
    inv = (np.float32(10000.0) ** (-np.arange(0, 32, 2, dtype=np.float32) / np.float32(32))).astype(np.float32)
    pos = np.arange(STREAM)
    ang = np.stack([(pos // 64).astype(np.float32)[:, None] * inv, (pos % 64).astype(np.float32)[:, None] * inv], 1)
    cos, sin = np.cos(ang), np.sin(ang)
    c["cos"] = np.stack([cos, cos], 2).reshape(2, P, 64).transpose(1, 0, 2).reshape(P, 128)
    c["sin"] = np.stack([-sin, sin], 2).reshape(2, P, 64).transpose(1, 0, 2).reshape(P, 128)
    c["eps"] = np.full((P, 1), EPS)
    c["one"] = np.ones((P, 1))
    return {k: np.ascontiguousarray(x, dtype=np.float32) for k, x in c.items()}


def cols(a):
    a = np.asarray(a)
    return np.moveaxis(a.reshape(a.shape[:-1] + (-1, P)), -1, 0).reshape(P, -1)


def rows(a):
    return np.broadcast_to(np.asarray(a).reshape(1, -1), (P, np.asarray(a).size))


def kernel(**inputs):
    import concourse.bacc as bacc
    from concourse.bass_utils import run_bass_kernel_spmd

    x = {k: np.asarray(a) for k, a in inputs.items()}
    p = constants()
    p["cond"] = np.stack([x["c"].reshape(KD, P), x["c_ctx"].reshape(KD, P)], 2).transpose(1, 0, 2).reshape(P, 16)
    p["bmod"] = cols(x["b_mod"])
    p["norms"] = np.stack([x["norm_mix"].reshape(LAYERS, KD, P), x["norm_ffn"].reshape(LAYERS, KD, P)], 1) \
        .transpose(3, 0, 1, 2).reshape(P, -1)
    up = np.zeros((P, LAYERS, 2, 256), np.float32)
    for d in range(2):
        up[16 * d:16 * d + 16, :, d] = x["gla_gate_up"][:, d].transpose(1, 0, 2)
    p["gate_up"] = up.reshape(P, -1)
    p["gate_bias"] = cols(x["gla_gate_bias"])
    gains = np.stack([x["gla_out_gain"], x["gdn_out_gain"]], 1).transpose(2, 0, 1)
    p["gains"] = np.concatenate([gains, gains], 0).reshape(P, -1)
    p["conv"] = x["gdn_conv"].reshape(LAYERS, 5, 6, P).transpose(3, 0, 2, 1).reshape(P, -1)
    p["dtb"], p["alog"] = rows(x["gdn_dt_bias"]), rows(x["gdn_a_log"])
    p["qkgain"] = rows(np.stack([x["att_q_gain"], x["att_k_gain"]], 1))
    p["router"] = x["moe_router"][0].reshape(KD, P, 8).transpose(1, 0, 2).reshape(P, -1)
    p["rbias"] = rows(x["moe_router_bias"][0])
    small = np.concatenate([x["w_in"][:, :, C_GLOW:C_GLOW + 32], x["w_in"][:, :, C_AB:C_AB + 16]], 2)
    p["wsmall"] = small.reshape(LAYERS, KD, P, 48).transpose(2, 0, 1, 3).reshape(P, -1)
    packed = np.concatenate([np.asarray(p[name]).reshape(P, width) for name, width in PARAMS], 1)
    arrays = {
        "in_xT": np.ascontiguousarray(np.concatenate([x["ctx"][0], x["x"][0]], 0).T),
        "in_params": np.ascontiguousarray(packed),
        "in_w_mod": x["w_mod"], "in_w_in": x["w_in"], "in_w_out": x["w_out"],
        "in_ffn_gu": x["ffn_gate_up"], "in_ffn_down": x["ffn_down"],
        "in_moe_gu": x["moe_gate_up"], "in_moe_down": x["moe_down"],
    }
    nc = bacc.Bacc("TRN2", target_bir_lowering=False, num_devices=1)
    args = [nc.dram_tensor(n, a.shape, mybir.dt.from_np(a.dtype), kind="ExternalInput").ap()
            for n, a in arrays.items()]
    out = nc.dram_tensor("out_T", (D, STREAM), F32, kind="ExternalOutput").ap()
    build(nc, *args, out)
    r = run_bass_kernel_spmd(nc, [arrays], core_ids=[0])
    return np.ascontiguousarray(r.results[0]["out_T"].T).reshape(1, STREAM, D)
```
